# Optimizing a Trainium2 kernel written in Bass

```python
import math
import jax, jax.numpy as jnp
from jax import lax
import numpy as np

D_MODEL = 1024
BATCH = 1
SEQ = 512
DEPTH = 1

GRID_W = 64
N_MEM = 256
D_HYENA = 512
HYENA_GROUPS = 8
HYENA_ORDER = 2
SHORT_CONV = 3
FILTER_BANDS = 16
FILTER_EMB = 1 + 2 * FILTER_BANDS
FILTER_FF = 64
DECAY_TARGET = 1e-2
FAST_DECAY_PCT = 0.3
SLOW_DECAY_PCT = 1.5
N_Q_HEADS = 8
N_KV_HEADS = 2
HEAD_DIM = 64
D_ATTN = N_Q_HEADS * HEAD_DIM
D_KV = N_KV_HEADS * HEAD_DIM
Q_BLOCK = 128
ROPE_THETA = 10000.0
D_MIX = D_HYENA + D_ATTN
D_IN = (HYENA_ORDER + 1) * D_HYENA + D_ATTN + 2 * D_KV
MEM_HEADS = 4
MEM_HEAD_DIM = 128
D_MEM_ATTN = MEM_HEADS * MEM_HEAD_DIM
N_GROUPS = 4
EXPERTS_PER_GROUP = 4
N_EXPERTS = N_GROUPS * EXPERTS_PER_GROUP
TOP_K = 2
D_EXPERT = 512
EPS = 1e-6

kernel_name = 'hybrid_hyena_gqa_hmoe_encoder'

def rms_norm(x, g):
    xf = x.astype(jnp.float32)
    y = xf * lax.rsqrt(jnp.mean(xf * xf, axis=-1, keepdims=True) + EPS)
    return (y * g.astype(jnp.float32)).astype(x.dtype)

def group_rms_norm(x, g, n_groups):
    shp = x.shape
    xg = x.reshape(shp[:-1] + (n_groups, shp[-1] // n_groups))
    return rms_norm(xg, g.reshape(n_groups, -1)).reshape(shp)

def rope_section(x, pos):
    m = x.shape[-1] // 2
    inv = ROPE_THETA ** (-jnp.arange(m, dtype=jnp.float32) / m)
    ang = pos.astype(jnp.float32)[:, None] * inv[None, :]
    cos = jnp.cos(ang)[None, :, None, :]
    sin = jnp.sin(ang)[None, :, None, :]
    xf = x.astype(jnp.float32)
    x1, x2 = xf[..., :m], xf[..., m:]
    return jnp.concatenate([x1 * cos - x2 * sin, x2 * cos + x1 * sin], axis=-1).astype(x.dtype)

def rope_2d(x, row, col):
    half = x.shape[-1] // 2
    return jnp.concatenate([rope_section(x[..., :half], row), rope_section(x[..., half:], col)], axis=-1)

def hyena_filter_spectra(L, w1, b1, w2, b2, w3, sin_freq):
    f32 = jnp.float32
    t = jnp.linspace(0.0, 1.0, L, dtype=f32)[:, None]
    bands = jnp.linspace(1e-4, FILTER_BANDS - 1, FILTER_BANDS, dtype=f32)[None, :]
    w = (2.0 * math.pi / L) * jnp.arange(L, dtype=f32)[:, None]
    z = jnp.concatenate([t, jnp.cos(bands * w), jnp.sin(bands * w)], axis=-1)
    a = jnp.sin(sin_freq[0].astype(f32) * (z @ w1.astype(f32) + b1.astype(f32)))
    a = jnp.sin(sin_freq[1].astype(f32) * (a @ w2.astype(f32) + b2.astype(f32)))
    filt = (a @ w3.astype(f32)).reshape(L, HYENA_ORDER, 2, D_HYENA)
    deltas = jnp.abs(jnp.linspace(math.log(DECAY_TARGET) / SLOW_DECAY_PCT,
                                  math.log(DECAY_TARGET) / FAST_DECAY_PCT, D_HYENA, dtype=f32))
    filt = filt * jnp.exp(-t * deltas)[:, None, None, :]
    fwd, bwd = filt[:, :, 0], filt[:, :, 1]
    k2 = jnp.concatenate([fwd, jnp.zeros_like(fwd[:1]), bwd[:0:-1]], axis=0)
    k2 = k2 / (jnp.sum(jnp.abs(k2), axis=0, keepdims=True) + EPS)
    return jnp.fft.rfft(k2, axis=0)

def fft_long_conv(z, k_f):
    L = z.shape[1]
    zf = jnp.fft.rfft(z.astype(jnp.float32), n=2 * L, axis=1)
    return jnp.fft.irfft(zf * k_f[None], n=2 * L, axis=1)[:, :L]

def hyena_mixer(u, short_w, short_b, skip, k_f):
    C = u.shape[-1]
    u = lax.conv_general_dilated(u, short_w[:, None, :].astype(u.dtype), window_strides=(1,),
                                 padding=((SHORT_CONV // 2, SHORT_CONV // 2),),
                                 dimension_numbers=('NWC', 'WIO', 'NWC'),
                                 feature_group_count=C) + short_b.astype(u.dtype)
    v, g1, g2 = jnp.split(u, 3, axis=-1)
    z = v
    for o, gate in enumerate((g1, g2)):
        zc = fft_long_conv(z, k_f[:, o]) + skip[o].astype(jnp.float32) * z.astype(jnp.float32)
        z = gate * zc.astype(gate.dtype)
    return z

def gqa_mixer(q, k, v, q_norm, k_norm, row, col):
    B, L, _ = q.shape
    G = N_Q_HEADS // N_KV_HEADS
    q = rope_2d(rms_norm(q.reshape(B, L, N_Q_HEADS, HEAD_DIM), q_norm), row, col)
    k = rope_2d(rms_norm(k.reshape(B, L, N_KV_HEADS, HEAD_DIM), k_norm), row, col)
    v = v.reshape(B, L, N_KV_HEADS, HEAD_DIM)
    nb = L // Q_BLOCK
    qb = q.reshape(B, nb, Q_BLOCK, N_KV_HEADS, G, HEAD_DIM).transpose(1, 0, 3, 4, 2, 5)
    kt = k.transpose(0, 2, 1, 3)
    vt = v.transpose(0, 2, 1, 3)
    scale = HEAD_DIM ** -0.5

    def attend_block(qblk):
        s = jnp.einsum('bkgqd,bksd->bkgqs', qblk, kt).astype(jnp.float32) * scale
        p = jax.nn.softmax(s, axis=-1).astype(vt.dtype)
        return jnp.einsum('bkgqs,bksd->bkgqd', p, vt)

    o = lax.map(attend_block, qb)
    return o.transpose(1, 0, 4, 2, 3, 5).reshape(B, L, D_ATTN)

def memory_cross_attn(h, m, w_q, w_k, w_v, q_norm, k_norm, w_o):
    B, L, _ = h.shape
    M = m.shape[1]
    q = rms_norm((h @ w_q).reshape(B, L, MEM_HEADS, MEM_HEAD_DIM), q_norm)
    k = rms_norm((m @ w_k).reshape(B, M, MEM_HEADS, MEM_HEAD_DIM), k_norm)
    v = (m @ w_v).reshape(B, M, MEM_HEADS, MEM_HEAD_DIM)
    s = jnp.einsum('blhd,bmhd->bhlm', q, k).astype(jnp.float32) * (MEM_HEAD_DIM ** -0.5)
    p = jax.nn.softmax(s, axis=-1).astype(v.dtype)
    o = jnp.einsum('bhlm,bmhd->blhd', p, v).reshape(B, L, D_MEM_ATTN)
    return o @ w_o

def hier_moe(h, w_rg, b_rg, w_re, b_re, w_gate, w_up, w_down):
    B, L, D = h.shape
    hf = h.reshape(B * L, D)
    grp_prob = jax.nn.softmax((hf @ w_rg).astype(jnp.float32) + b_rg.astype(jnp.float32), axis=-1)
    p_grp, g_idx = lax.top_k(grp_prob, 1)
    exp_logits = ((hf @ w_re).astype(jnp.float32) + b_re.astype(jnp.float32)).reshape(
        -1, N_GROUPS, EXPERTS_PER_GROUP)
    sel_logits = jnp.take_along_axis(exp_logits, g_idx[:, :, None], axis=1)[:, 0]
    w_top, e_loc = lax.top_k(jax.nn.softmax(sel_logits, axis=-1), TOP_K)
    w_top = p_grp * w_top / jnp.sum(w_top, axis=-1, keepdims=True)
    e_glob = g_idx * EXPERTS_PER_GROUP + e_loc
    gates = jnp.einsum('tk,tke->te', w_top,
                       jax.nn.one_hot(e_glob, N_EXPERTS, dtype=jnp.float32)).astype(h.dtype)
    y = jnp.zeros_like(hf)
    for e in range(N_EXPERTS):
        a = jax.nn.silu(hf @ w_gate[e]) * (hf @ w_up[e])
        y = y + gates[:, e:e + 1] * (a @ w_down[e])
    return y.reshape(B, L, D)

def setup_inputs(seed: int = 0) -> dict:
    key = jax.random.key(seed)
    ks = iter(jax.random.split(key, 40))
    f32 = jnp.float32

    def nrm(shape, scale):
        return jax.random.normal(next(ks), shape, f32) * scale

    def gain(shape):
        return 1.0 + 0.05 * jax.random.normal(next(ks), shape, f32)

    return {
        'x': nrm((BATCH, SEQ, D_MODEL), 1.0),
        'mem': nrm((BATCH, N_MEM, D_MODEL), 1.0),
        'norm_mix': gain((DEPTH, D_MODEL)),
        'w_in': nrm((DEPTH, D_MODEL, D_IN), D_MODEL ** -0.5),
        'hyena_short_w': nrm((DEPTH, SHORT_CONV, (HYENA_ORDER + 1) * D_HYENA), SHORT_CONV ** -0.5),
        'hyena_short_b': nrm((DEPTH, (HYENA_ORDER + 1) * D_HYENA), 0.02),
        'filt_w1': nrm((DEPTH, FILTER_EMB, FILTER_FF), FILTER_EMB ** -0.5),
        'filt_b1': nrm((DEPTH, FILTER_FF), 0.02),
        'filt_w2': nrm((DEPTH, FILTER_FF, FILTER_FF), FILTER_FF ** -0.5),
        'filt_b2': nrm((DEPTH, FILTER_FF), 0.02),
        'filt_w3': nrm((DEPTH, FILTER_FF, HYENA_ORDER * 2 * D_HYENA), FILTER_FF ** -0.5),
        'filt_sin_freq': gain((DEPTH, 2, FILTER_FF)),
        'hyena_skip': nrm((DEPTH, HYENA_ORDER, D_HYENA), 0.1),
        'attn_q_norm': gain((DEPTH, HEAD_DIM)),
        'attn_k_norm': gain((DEPTH, HEAD_DIM)),
        'out_norm_hyena': gain((DEPTH, D_HYENA)),
        'out_norm_attn': gain((DEPTH, D_ATTN)),
        'w_out': nrm((DEPTH, D_MIX, D_MODEL), D_MIX ** -0.5),
        'norm_xattn': gain((DEPTH, D_MODEL)),
        'norm_mem': gain((DEPTH, D_MODEL)),
        'w_q_mem': nrm((DEPTH, D_MODEL, D_MEM_ATTN), D_MODEL ** -0.5),
        'w_k_mem': nrm((DEPTH, D_MODEL, D_MEM_ATTN), D_MODEL ** -0.5),
        'w_v_mem': nrm((DEPTH, D_MODEL, D_MEM_ATTN), D_MODEL ** -0.5),
        'mem_q_norm': gain((DEPTH, MEM_HEAD_DIM)),
        'mem_k_norm': gain((DEPTH, MEM_HEAD_DIM)),
        'w_o_mem': nrm((DEPTH, D_MEM_ATTN, D_MODEL), D_MEM_ATTN ** -0.5),
        'norm_moe': gain((DEPTH, D_MODEL)),
        'w_router_grp': nrm((DEPTH, D_MODEL, N_GROUPS), D_MODEL ** -0.5),
        'b_router_grp': nrm((DEPTH, N_GROUPS), 0.01),
        'w_router_exp': nrm((DEPTH, D_MODEL, N_EXPERTS), D_MODEL ** -0.5),
        'b_router_exp': nrm((DEPTH, N_EXPERTS), 0.01),
        'w_gate': nrm((DEPTH, N_EXPERTS, D_MODEL, D_EXPERT), D_MODEL ** -0.5),
        'w_up': nrm((DEPTH, N_EXPERTS, D_MODEL, D_EXPERT), D_MODEL ** -0.5),
        'w_down': nrm((DEPTH, N_EXPERTS, D_EXPERT, D_MODEL), D_EXPERT ** -0.5),
    }

def reference(x, mem, norm_mix, w_in, hyena_short_w, hyena_short_b, filt_w1, filt_b1, filt_w2,
              filt_b2, filt_w3, filt_sin_freq, hyena_skip, attn_q_norm, attn_k_norm,
              out_norm_hyena, out_norm_attn, w_out, norm_xattn, norm_mem, w_q_mem, w_k_mem,
              w_v_mem, mem_q_norm, mem_k_norm, w_o_mem, norm_moe, w_router_grp, b_router_grp,
              w_router_exp, b_router_exp, w_gate, w_up, w_down):
    L = x.shape[1]
    rows = L // GRID_W
    row = jnp.broadcast_to(jnp.arange(rows, dtype=jnp.int32)[:, None], (rows, GRID_W)).reshape(-1)
    col = jnp.broadcast_to(jnp.arange(GRID_W, dtype=jnp.int32)[None, :], (rows, GRID_W)).reshape(-1)
    split_at = [(HYENA_ORDER + 1) * D_HYENA,
                (HYENA_ORDER + 1) * D_HYENA + D_ATTN,
                (HYENA_ORDER + 1) * D_HYENA + D_ATTN + D_KV]
    for i in range(DEPTH):
        h = rms_norm(x, norm_mix[i])
        u_hy, q, k, v = jnp.split(h @ w_in[i], split_at, axis=-1)
        k_f = hyena_filter_spectra(L, filt_w1[i], filt_b1[i], filt_w2[i], filt_b2[i], filt_w3[i],
                                   filt_sin_freq[i])
        y_hy = hyena_mixer(u_hy, hyena_short_w[i], hyena_short_b[i], hyena_skip[i], k_f)
        y_at = gqa_mixer(q, k, v, attn_q_norm[i], attn_k_norm[i], row, col)
        y = jnp.concatenate([group_rms_norm(y_hy, out_norm_hyena[i], HYENA_GROUPS),
                             group_rms_norm(y_at, out_norm_attn[i], N_Q_HEADS)], axis=-1)
        x = x + y @ w_out[i]
        x = x + memory_cross_attn(rms_norm(x, norm_xattn[i]), rms_norm(mem, norm_mem[i]),
                                  w_q_mem[i], w_k_mem[i], w_v_mem[i], mem_q_norm[i], mem_k_norm[i],
                                  w_o_mem[i])
        x = x + hier_moe(rms_norm(x, norm_moe[i]), w_router_grp[i], b_router_grp[i], w_router_exp[i],
                         b_router_exp[i], w_gate[i], w_up[i], w_down[i])
    return x


_drawn_inputs = setup_inputs


def setup_inputs(seed=0):
    import zlib

    import numpy as np

    out = dict(_drawn_inputs(seed))
    spreads = {}
    factors = {'norm_xattn': 7.403,
     'norm_mem': 5.147,
     'mem_q_norm': 6.303,
     'mem_k_norm': 4.553,
     'b_router_grp': 57.448,
     'b_router_exp': 50.544,
     'norm_moe': 7.053}
    for name, (base, spread) in spreads.items():
        noise = np.random.default_rng([zlib.crc32(name.encode()), seed]).standard_normal(out[name].shape)
        drawn = base * np.exp(spread * noise) if base else spread * noise
        out[name] = __import__('jax').numpy.asarray(drawn.astype(out[name].dtype))
    for name, factor in factors.items():
        out[name] = (out[name] * factor).astype(out[name].dtype)
    return out
```

```python
from contextlib import ExitStack

import numpy as np
import concourse.bass as bass
from concourse import mybir

F32 = mybir.dt.float32
I32 = mybir.dt.int32
ALU = mybir.AluOpType
ACT = mybir.ActivationFunctionType
AX = mybir.AxisListType

P = 128
T, D = 512, 1024
TT, KT = T // P, D // P
NM = 256
MT = NM // P
CH = 512
CT = CH // P
HALF = T // 2
NQ, NKV, HD = 8, 2, 64
MH, MHD = 4, 128
NG, EPG = 4, 4
NE = NG * EPG
FE = 512
FB, FF = 33, 64
EPS = 1e-6
NB = 28
MAXB = 24
SPARE = 2 * T
AHEAD = 2
NPR = 4
KB = 1024

COLS = {}
_at = 0
for _name, _n in (("norm_mix", KT), ("norm_xattn", KT), ("norm_mem", KT), ("norm_moe", KT),
                  ("short_w", 3 * 12), ("short_b", 12), ("skip", 2 * CT), ("hyena_norm", CT),
                  ("attn_norm", CT), ("b1", 1), ("b2", 1), ("freq", 2), ("not_first", 1), ("token", TT)):
    COLS[_name] = _at
    _at += _n
NCOLS = _at
ROWS = {}
_at = 0
for _name, _n in (("gq", HD), ("gk", HD), ("gmq", MHD), ("gmk", MHD), ("b_router", NG + NE),
                  ("first4", 4), ("expert", NE), ("extra", 8)):
    ROWS[_name] = (_at, _at + _n)
    _at += _n
NROWS = _at


def psum_jobs():
    jobs = [("mlp", 0)] + [("hT", 0, k) for k in range(KT)] + [("mlp", 1)]
    jobs += [("memT", j) for j in range(KT // 2)]
    for o in range(2):
        for t in range(4):
            jobs += [("filt", o, t, 0), ("filt", o, t, 1)]
        jobs += [("l1", o)] + [("spec", o, f, c) for f in range(2) for c in range(4)]
    jobs += [("u", c) for c in range(12)]
    for o in range(2):
        jobs += [("zT", o, k) for k in range(4)] + [("fwd", o, f, c) for f in range(2) for c in range(4)]
        if o == 0:
            jobs += [("q", i) for i in range(TT)] + [("kv", i) for i in range(TT)]
        else:
            jobs += [("mk", j) for j in range(MT)] + [("mv", j) for j in range(MT)]
        jobs += [("inv", o, c) for c in range(CT)]
    jobs += [("mkT", j) for j in range(2)]
    jobs += [("qT", p) for p in range(NQ // 2)] + [("kT", g) for g in range(NKV)] + [("hn", c) for c in range(CT)]
    n = TT * NQ
    jobs += [("S", s) for s in range(AHEAD)]
    for s in range(-1, n):
        if s >= 0 and s % NQ == 0:
            jobs += [("O", s // NQ)]
        if s + 1 + AHEAD < n:
            jobs += [("S", s + 1 + AHEAD)]
        if s + 1 < n:
            jobs += [("PT", s + 1)]
    jobs += [("yT", k) for k in range(CT)]
    jobs += [("wout", h, i) for h in range(2) for i in range(TT)]
    jobs += [("hT", 1, k) for k in range(KT)]
    jobs += [("mq", i) for i in range(TT)] + [("mqT", h) for h in range(MH)]
    n = TT * 2
    jobs += [("MS", s) for s in range(AHEAD)]
    for s in range(n):
        if s + AHEAD < n:
            jobs += [("MS", s + AHEAD)]
        jobs += [("MPT", s)]
    jobs += [("mo", h) for h in range(MH)]
    jobs += [("wom", h, i) for h in range(2) for i in range(TT)]
    jobs += [("hT", 2, k) for k in range(KT)]
    jobs += [("router",), ("count",)]
    return jobs


def build(nc, a, out, rec_dram, xn_dram, y_dram):
    with ExitStack() as ctx:
        base = nc.sbuf_base + (-nc.sbuf_base) % 64
        used = []

        def at(name, kb, shape, dt=F32):
            return nc.alloc_sbuf_tensor_at(name, shape, dt, offset=base + int(kb * KB))

        fence = ctx.enter_context(nc.sbuf_tensor("fence", [P, 205 * 256], F32))

        ring = [at(f"ring{s}", 16 * s, [P, 4096]) for s in range(2)]
        memT = at("memT", 32, [P, KT, NM])
        mk = at("mk", 40, [P, MT, 512])
        mv = at("mv", 44, [P, MT, 512])
        hT = at("hT", 48, [P, KT, T])
        x_in = at("x_in", 64, [P, TT, D])
        qkv = at("qkv", 64, [P, TT, 768])
        rope_tmp = at("rope_tmp", 76, [P, 640])
        mem_raw = at("mem_raw", 80, [P, MT, D])
        w3 = at("w3", 88, [FF, 2048])
        w1 = at("w1", 96, [FB, FF])
        w2 = at("w2", 96.5, [FF, FF])
        zemb = at("zemb", 98, [FB, T])
        a1 = at("a1", 100, [FF, T])
        a2 = at("a2", 102, [FF, T])
        u = at("u", 80, [P, 12, T])
        dft = at("dft", 104, [P, 2, 4, HALF])
        idft = at("idft", 112, [P, 2, 4, HALF])
        spec = at("spec", 120, [P, 2, 2, 4, CH])
        decay = at("decay", 152, [P, 4, CH])
        zt = at("zt", 152, [P, 4, CH])
        ep = at("ep", 160, [P, 4, CH])
        mlp_arg = at("mlp_arg", 172, [FF, T])
        mlp_k = at("mlp_k", 174, [FF, T])
        l1sum = at("l1sum", 168, [P, CH])
        rnorm = at("rnorm", 170, [P, CH])
        fabs = at("fabs", 64, [P, 2, CH])
        ab = at("ab", 168, [P, 4, CH])
        sp = at("sp", 176, [P, 4, CH])
        dm = at("dm", 184, [P, 4, CH])
        sd = at("sd", 176, [P, 2, 4, CH])
        fb = at("fb", 192, [P, 2, CH])
        tmp = at("tmp", 192, [P, 2, CH])
        qT = at("qT", 104, [P, NQ // 2, T])
        kT = at("kT", 112, [P, NKV, T])
        mkT = at("mkT", 116, [P, MH, NM])
        kdup = at("kdup", 160, [P, TT, NKV, 2, HD])
        x2 = at("x2", 120, [P, TT, D])
        yT = at("yT", 136, [P, KT, T])
        att = at("att", 152, [P, TT, 512])
        pr = at("pr", 48, [P, NPR, T])
        pT = at("pT", 56, [P, NPR, T])
        att_sq = at("att_sq", 172, [P, 512])
        y_sq = at("y_sq", 176, [P, CT, CH])
        y_rs = at("y_rs", 184, [P, CT, CH])
        xn = at("xn", 80, [P, TT, D])
        mq = at("mq", 152, [P, TT, 512])
        mqT = at("mqT", 160, [P, MH, T])
        mpT = at("mpT", 176, [P, MH, MT, T])
        moT = at("moT", 104, [P, MH, T])
        slot = [at(f"slot{s}", 16 * s, [P, 4096]) for s in range(6)]
        hg = [at(f"hg{q}", 136 + 4 * q, [P, D]) for q in range(2)]
        hgT = [at(f"hgT{q}", 144 + 4 * q, [P, KT, P]) for q in range(2)]
        sg = [at(f"sg{q}", 152 + 2 * q, [P, FE]) for q in range(2)]
        ga = [at(f"ga{q}", 156 + 2 * q, [P, FE]) for q in range(2)]
        gaT = [at(f"gaT{q}", 160 + 2 * q, [P, 4, P]) for q in range(2)]
        eo = [at(f"eo{q}", 164 + 4 * q, [P, D]) for q in range(2)]
        y_back = at("y_back", 0, [P, 2, TT, D])
        rt = at("rt", 172, [P, 3072])
        rec_sb = at("rec_sb", 184, [P, NB, 4])
        meta_i = at("meta_i", 185, [P, 2, 2], I32)
        meta_g = at("meta_g", 185.125, [P, 2, 1])
        gather_i = at("gather_i", 185.25, [P, 2, 1], I32)
        e_tab = at("e_tab", 185.5, [1, 32], I32)
        slot_i = at("slot_i", 186, [P, 2, TT], I32)
        wr = at("wr", 187, [P, KT, NG + NE])
        rec = at("rec", 188, [P, 2, TT, 4])
        cols = at("cols", 196, [P, NCOLS])
        rows = at("rows", 197, [P, NROWS])
        rope = at("rope", 199, [P, 2, TT, HD])
        ident = at("ident", 201, [P, P])
        ones = at("ones", 201.5, [P, P])
        blk = at("blk", 202, [P, P])
        tri = at("tri", 202.5, [P, P])
        small = at("small", 203, [P, 400])

        banks = [ctx.enter_context(nc.psum_tensor(f"bank{b}", [P, 512], F32)) for b in range(8)]

        def sem(name):
            return ctx.enter_context(nc.semaphore(name))

        jobs = psum_jobs()
        number, place, uses = {}, {}, [0] * 8
        turn, first_s = 0, jobs.index(("S", 0))
        last_s = max(n for n, j in enumerate(jobs) if j[0] == "PT")
        for n, j in enumerate(jobs):
            if j[0] == "O":
                b = 6 + j[1] % 2
            else:
                number[j] = len(number)
                span = 6 if first_s <= n <= last_s else 8
                b, turn = turn % span, (turn + 1) % span
            place[j] = (b, uses[b])
            uses[b] += 1
        filled = sem("psum_filled")
        freed = [sem(f"bank{b}_freed") for b in range(8)]
        def bank(job):
            return banks[place[job][0]]

        def wait_filled(eng, job):
            eng.wait_ge(filled, number[job] + 1)

        def free(ins, job):
            ins.then_inc(freed[place[job][0]], 1)

        def wait_freed(eng, job):
            eng.wait_ge(freed[place[job][0]], place[job][1] + 1)

        def open_bank(pe, job):
            b, use = place[job]
            if use:
                pe.wait_ge(freed[b], use)

        ld = {k: sem(f"ld_{k}") for k in ("x", "mem", "cols", "rows", "rope", "mats", "w12", "w3", "zemb", "decay",
                                          "dft", "idft", "x2", "wr", "rec0", "rec", "back")}
        ring_ld = [sem(f"ring_ld{s}") for s in range(2)]
        ring_used = sem("ring_used")
        s_xn = sem("xn_ready")
        s_arg = sem("mlp_arg_ready")
        s_sin = sem("mlp_sin_done")
        s_spdm = sem("spdm_ready")
        s_l1 = sem("l1_added")
        s_rn = sem("rnorm_ready")
        s_ke = sem("spec_parts_ready")
        s_kab = sem("spec_ready")
        s_conv = sem("conv_ready")
        s_a = sem("fwd_sum_ready")
        s_b = sem("fwd_diff_ready")
        s_pb = sem("prod_b_ready")
        s_ab = sem("prod_used")
        s_z = sem("z_ready")
        s_sq = sem("square_done")
        s_rms = sem("rms_ready")
        s_ms = sem("head_sums_ready")
        s_hrms = sem("head_rms_ready")
        s_abs = sem("filt_abs_ready")
        s_hroot = sem("hyena_rms_ready")
        s_rope = sem("rope_ready")
        s_kdup = sem("kdup_ready")
        s_mkn = sem("mk_normed")
        s_ysq = sem("y_square_ready")
        s_max = sem("score_max_ready")
        s_exp = sem("exp_done")
        s_att = sem("att_normed")
        s_yh = sem("y_hyena_ready")
        s_mqn = sem("mq_normed")
        s_mnorm = sem("mem_probs_ready")
        s_gq = sem("gq_scaled")
        s_asq = sem("att_square_done")
        s_store = sem("xn_stored")
        s_r1 = sem("route_group_logits")
        s_r2 = sem("route_group_exp")
        s_r3 = sem("route_expert_diff")
        s_r4 = sem("route_expert_exp")
        s_oh = sem("onehots_ready")
        s_slot = sem("slots_ready")
        s_scat = sem("records_scattered")
        s_tab = sem("tables_ready")
        dchain, achain, pchain = sem("dve_step"), sem("act_step"), sem("pool_step")
        w_ld = [sem(f"expert_w_ld{s}") for s in range(6)]
        s_gate, s_up, s_down0, s_down = sem("gate_done"), sem("up_done"), sem("down0_done"), sem("down_done")
        s_gath = [sem(f"gathered{q}") for q in range(2)]
        s_gi = sem("gather_index_ready")
        s_t = sem("rows_transposed")
        s_ta, s_td = sem("rowsT_evac_act"), sem("rowsT_evac_dve")
        s_silu, s_mul = sem("silu_done"), sem("act_mul_done")
        s_at, s_ate = sem("actT_filled"), sem("actT_evac")
        s_oa, s_od = sem("out_evac_act"), sem("out_evac_dve")
        s_meta = sem("meta_ready")
        s_sc = [sem(f"rows_scattered{q}") for q in range(2)]
        s_fin = sem("sum_ready")
        s_out = sem("stored")
        waited_pool, waited_sp = sem("waited_pool"), sem("waited_sp")

        def col(name, i=0, n=P):
            c = COLS[name] + i
            return cols[0:n, c:c + 1]

        def row(name):
            lo, hi = ROWS[name]
            return rows[:, lo:hi]

        w_in = a["w_in"][0].rearrange("(t p) n -> p t n", p=P)

        def mat(name):
            return a[name][0].rearrange("(t p) n -> p t n", p=P)

        chunks = [("v", w_in[:, :, 0:512]), ("g1", w_in[:, :, 512:1024]), ("g2", w_in[:, :, 1024:1536]),
                  ("q", w_in[:, :, 1536:2048]), ("kv", w_in[:, :, 2048:2304]),
                  ("mk", mat("w_k_mem")), ("mv", mat("w_v_mem")),
                  ("wo0", mat("w_out")[:, :, 0:512]), ("wo1", mat("w_out")[:, :, 512:1024]),
                  ("wq", mat("w_q_mem")), ("wom", mat("w_o_mem"))]
        order = {name: n for n, (name, _) in enumerate(chunks)}

        def chunk(name):
            src = chunks[order[name]][1]
            kt, n = src.shape[1], src.shape[2]
            return ring[order[name] % 2][:, 0:kt * n].rearrange("p (t n) -> p t n", t=kt)

        def wait_chunk(eng, name):
            eng.wait_ge(ring_ld[order[name] % 2], 16 * (order[name] // 2 + 1))

        wg_v = a["w_gate"][0].rearrange("e (t p) n -> p e t n", p=P)
        wu_v = a["w_up"][0].rearrange("e (t p) n -> p e t n", p=P)
        wd_v = a["w_down"][0].rearrange("e (t p) n -> p e t n", p=P)

        NSEQ = TT * NQ
        MSEQ = TT * 2
        block = ctx.enter_context(nc.Block())

        @block.sync
        def _(sp_):
            sp_.dma_start(cols[:], a["cols"]).then_inc(ld["cols"], 16)
            sp_.dma_start(zemb[:], a["zemb"]).then_inc(ld["zemb"], 16)
            sp_.dma_start(w1[:], a["filt_w1"][0]).then_inc(ld["w12"], 16)
            sp_.dma_start(w2[:], a["filt_w2"][0]).then_inc(ld["w12"], 16)
            x_src = a["x"][0].rearrange("(i p) d -> p i d", p=P)
            for i in range(TT):
                sp_.dma_start(x_in[:, i, :], x_src[:, i, :]).then_inc(ld["x"], 16)
            sp_.dma_start(ident[:], a["mats"][:, 0, :]).then_inc(ld["mats"], 16)
            sp_.dma_start(ones[:], a["mats"][:, 1, :]).then_inc(ld["mats"], 16)
            sp_.dma_start(blk[:], a["mats"][:, 2, :]).then_inc(ld["mats"], 16)
            sp_.dma_start(tri[:], a["mats"][:, 3, :]).then_inc(ld["mats"], 16)
            sp_.dma_start(w3[:], a["filt_w3"][0]).then_inc(ld["w3"], 16)
            sp_.dma_start(decay[:], a["decay"]).then_inc(ld["decay"], 16)
            sp_.dma_start(mem_raw[:], a["mem"][0].rearrange("(j p) d -> p j d", p=P)).then_inc(ld["mem"], 16)
            sp_.dma_start(dft[:], a["dft"]).then_inc(ld["dft"], 16)
            sp_.dma_start(rows[:], a["rows"]).then_inc(ld["rows"], 16)
            sp_.dma_start(rope[:], a["rope"]).then_inc(ld["rope"], 16)
            sp_.dma_start(idft[:], a["idft"]).then_inc(ld["idft"], 16)
            sp_.dma_start(rec_dram, a["rec_init"]).then_inc(ld["rec0"], 16)
            for n, (name, src) in enumerate(chunks):
                if n >= 2:
                    sp_.wait_ge(ring_used, n - 1)
                sp_.dma_start(chunk(name), src).then_inc(ring_ld[n % 2], 16)
                if name == "wo1":
                    wait_freed(sp_, ("inv", 1, CT - 1))
                    sp_.wait_ge(s_z, 2 * CT)
                    for i in range(TT):
                        sp_.dma_start(x2[:, i, :], x_src[:, i, :]).then_inc(ld["x2"], 16)
            views = [wg_v, wu_v, wd_v]

            def slot_view(s):
                return slot[s][:].rearrange("p (t n) -> p t n", t=(8, 8, 4)[s % 3])

            wait_freed(sp_, ("mk", MT - 1))
            wait_freed(sp_, ("mv", MT - 1))
            wait_freed(sp_, ("mo", MH - 1))
            sp_.wait_ge(ring_used, len(chunks))
            sp_.dma_start(wr[:], a["w_router"]).then_inc(ld["wr"], 16)
            for s in range(3):
                sp_.dma_start(slot_view(s), views[s][:, 0]).then_inc(w_ld[s], 16)
            wait_freed(sp_, ("router",))
            sp_.wait_ge(s_store, 16 * TT)
            for s in range(3, 6):
                sp_.dma_start(slot_view(s), views[s - 3][:, 1]).then_inc(w_ld[s], 16)
            sp_.wait_ge(s_scat, 16 * 2 * TT)
            sp_.dma_start(rec_sb[:], rec_dram.rearrange("(p b) c -> p b c", p=P)).then_inc(ld["rec"], 16)
            sp_.wait_ge(s_tab, 1)
            nb = sp_.value_load(e_tab[0:1, 31:32], min_val=0, max_val=MAXB - NE) + NE
            with sp_.Fori(2, nb, 2) as b:
                for q in range(2):
                    e = sp_.value_load(e_tab[0:1, bass.ds(b + q, 1)], min_val=0, max_val=NE - 1)
                    for c, used_by in enumerate((s_gate, s_up, s_down)):
                        sp_.wait_ge(used_by, b + q - 1)
                        sp_.sem_inc(waited_sp, 1)
                        s = 3 * q + c
                        sp_.dma_start(slot_view(s), views[c][:, bass.ds(e, 1)].rearrange("p e t n -> p (e t) n"))\
                            .then_inc(w_ld[s], 16)
            sp_.wait_ge(s_down, nb)
            sp_.sem_inc(waited_sp, 1)
            for q in range(2):
                sp_.wait_ge(s_sc[q], nb * 8)
            for i in range(TT):
                for r in range(2):
                    sp_.dma_start(y_back[:, r, i, :], y_dram[r * T + i * P:r * T + (i + 1) * P, :])\
                        .then_inc(ld["back"], 16)
            for i in range(TT):
                sp_.wait_ge(s_fin, 2 * (i + 1))
                sp_.dma_start(out[0, i * P:(i + 1) * P, :], x2[:, i, :]).then_inc(s_out, 16)
            sp_.wait_ge(s_out, 16 * TT)

        @block.gpsimd
        def _(pool):
            steps = [0]

            def link(ins):
                steps[0] += 1
                ins.then_inc(pchain, 1)
                pool.wait_ge(pchain, steps[0])

            for o in range(2):
                for t in range(4):
                    wait_freed(pool, ("filt", o, t, 0))
                    wait_freed(pool, ("filt", o, t, 1))
                    if o == 1 and t == 0:
                        wait_filled(pool, ("spec", 0, 1, 3))
                    pool.tensor_tensor(sp[:, t, :], fb[:, 0, :], fb[:, 1, :], ALU.add)
                    pool.tensor_tensor(dm[:, t, :], fb[:, 0, :], fb[:, 1, :], ALU.subtract).then_inc(s_spdm, 1)
                for f in range(2):
                    pool.wait_ge(s_ke, 2 * o + f + 1)
                    for c in range(2):
                        pool.tensor_tensor(spec[:, o, f, c, :], ep[:, c, :], ep[:, 2 + c, :], ALU.add)
                        last = pool.tensor_tensor(spec[:, o, f, 2 + c, :], ep[:, c, :], ep[:, 2 + c, :], ALU.subtract)
                    last.then_inc(s_kab, 1)
            for o in range(2):
                for f in range(2):
                    n = 2 * o + f
                    for c in range(4):
                        wait_freed(pool, ("fwd", o, f, c))
                    if n:
                        pool.wait_ge(s_ab, n)
                    pool.tensor_tensor(ab[:, 0, :], ep[:, 0, :], ep[:, 2, :], ALU.add)
                    pool.tensor_tensor(ab[:, 1, :], ep[:, 1, :], ep[:, 3, :], ALU.add).then_inc(s_a, 1)
                    pool.wait_ge(s_a, n + 1)
                    pool.wait_ge(s_b, n + 1)
                    kre, kim = spec[:, o, f, 2, :], spec[:, o, f, 3, :]
                    pool.tensor_tensor(ep[:, 1, :], ab[:, 2, :], kre, ALU.mult)
                    pool.tensor_tensor(ep[:, 3, :], ab[:, 3, :], kim, ALU.mult)
                    pool.tensor_tensor(tmp[:, 0, :], ab[:, 2, :], kim, ALU.mult)
                    pool.tensor_tensor(tmp[:, 1, :], ab[:, 3, :], kre, ALU.mult).then_inc(s_pb, 1)
            wait_filled(pool, ("inv", 1, CT - 1))
            for c in range(CT):
                pool.wait_ge(s_z, CT + c + 1)
                pool.tensor_tensor(y_sq[:, c, :], u[:, c, :], u[:, c, :], ALU.mult).then_inc(s_ysq, 1)
            for i in range(TT):
                pool.wait_ge(s_xn, 10 + i + 1)
                pool.dma_start(xn_dram[i * P:(i + 1) * P, :], xn[:, i, :]).then_inc(s_store, 16)
            pool.wait_ge(ld["rec0"], 16)
            pool.wait_ge(s_slot, 1)
            for r in range(2):
                for i in range(TT):
                    pool.indirect_dma_start(rec_dram, bass.IndirectOffsetOnAxis(ap=slot_i[:, r, i:i + 1], axis=0),
                                            rec[:, r, i, :], None).then_inc(s_scat, 16)
            pool.wait_ge(ld["rec"], 16)
            pool.wait_ge(s_store, 16 * TT)
            pool.wait_ge(s_tab, 1)

            def meta(b, q):
                if not isinstance(b, int) or b >= 2:
                    pool.wait_ge(s_oa, b - 1)
                    pool.wait_ge(s_od, b - 1)
                    pool.wait_ge(s_sc[q], (b - q) * 8)
                pool.tensor_copy(meta_i[:, q, 0:1], rec_sb[:, bass.ds(b, 1), 1:2].rearrange("p b c -> p (b c)"))
                pool.tensor_copy(meta_g[:, q, :], rec_sb[:, bass.ds(b, 1), 2:3].rearrange("p b c -> p (b c)"))\
                    .then_inc(s_meta, 1)

            def gather(b, q):
                if not isinstance(b, int) or b >= 2:
                    pool.wait_ge(s_t, 2 * b - 2)
                pool.tensor_copy(gather_i[:, q, :], rec_sb[:, bass.ds(b, 1), 0:1].rearrange("p b c -> p (b c)"))\
                    .then_inc(s_gi, 1)
                pool.wait_ge(s_gi, b + 1)
                pool.sem_inc(waited_pool, 1)
                pool.indirect_dma_start(hg[q][:], None, xn_dram,
                                        bass.IndirectOffsetOnAxis(ap=gather_i[:, q, :], axis=0)).then_inc(s_gath[q], 16)

            def scatter(b, q):
                pool.wait_ge(s_oa, b + 1)
                pool.wait_ge(s_od, b + 1)
                pool.wait_ge(s_meta, b + 1)
                if not isinstance(b, int) or b >= 1:
                    pool.wait_ge(s_sc[1 - q], (b + q) * 8)
                pool.sem_inc(waited_pool, 1)
                pool.indirect_dma_start(y_dram, bass.IndirectOffsetOnAxis(ap=meta_i[:, q, 0:1], axis=0),
                                        eo[q][:], None).then_inc(s_sc[q], 16)

            gather(0, 0)
            gather(1, 1)
            meta(0, 0)
            gather(2, 0)
            meta(1, 1)
            gather(3, 1)
            scatter(0, 0)
            nb = pool.value_load(e_tab[0:1, 31:32], min_val=0, max_val=MAXB - NE) + NE
            with pool.Fori(2, nb, 2) as b:
                meta(b, 0)
                gather(b + 2, 0)
                scatter(b - 1, 1)
                meta(b + 1, 1)
                gather(b + 3, 1)
                scatter(b, 0)
            scatter(nb - 1, 1)
            for q in range(2):
                pool.wait_ge(s_gath[q], (nb + 2) * 8)

        @block.scalar
        def _(act):
            steps = [0]

            def link(ins):
                steps[0] += 1
                ins.then_inc(achain, 1)
                act.wait_ge(achain, steps[0])

            def sine(j, dst):
                act.wait_ge(s_arg, j + 1)
                act.activation(dst[:], mlp_arg[:], ACT.Sin).then_inc(s_sin, 1)

            fb_flat = at("junk", 192, [P, D])[:]

            eps = small[:, 395:396]

            def rms(src, first, n, count):
                for i in range(n):
                    act.activation(fb_flat, src[:, i, :], ACT.Square, accum_out=small[:, first + i:first + i + 1])\
                        .then_inc(s_sq, 1)
                    act.wait_ge(s_sq, count - n + i + 1)
                act.activation(small[:, 16 + first:16 + first + n], small[:, first:first + n], ACT.Sqrt,
                               bias=eps, scale=1.0 / D).then_inc(s_rms, 1)

            act.wait_ge(ld["cols"], 16)
            link(act.activation(eps, col("token"), ACT.Copy, scale=0.0, bias=EPS))
            act.wait_ge(ld["x"], 16 * TT)
            rms(x_in, 0, TT, TT)
            act.wait_ge(ld["mem"], 16)
            rms(mem_raw, 4, MT, TT + MT)

            def abs_pair(o, t):
                wait_freed(act, ("filt", o, t, 0))
                wait_freed(act, ("filt", o, t, 1))
                if 4 * o + t:
                    act.wait_ge(s_l1, 4 * o + t)
                else:
                    wait_filled(act, ("hT", 0, KT - 1))
                act.activation(fabs[:], fb[:], ACT.Abs).then_inc(s_abs, 1)

            def head_rms(first, n, width, count):
                act.wait_ge(s_ms, count)
                act.activation(small[:, first:first + n], small[:, first:first + n], ACT.Sqrt, bias=eps,
                               scale=1.0 / width).then_inc(s_hrms, 1)

            sine(0, a1)
            for k in range(0, KT, 2):
                wait_filled(act, ("hT", 0, k))
                free(act.activation(hT[:, k, :], bank(("hT", 0, k))[:], ACT.Copy, scale=col("norm_mix", k)), ("hT", 0, k))
            sine(1, a2)
            for j in range(KT // 2):
                job = ("memT", j)
                wait_filled(act, job)
                for c in range(2):
                    k = 2 * j + c
                    ins = act.activation(memT[:, k, :], bank(job)[:, c * NM:(c + 1) * NM], ACT.Copy, scale=col("norm_mem", k))
                free(ins, job)
            for o in range(2):
                for t in range(4):
                    abs_pair(o, t)
            act.wait_ge(ld["rows"], 16)
            act.activation(row("gq"), row("gq"), ACT.Copy, scale=HD ** -0.5).then_inc(s_gq, 1)
            for c in range(12):
                job = ("u", c)
                wait_filled(act, job)
                act.activation(u[:, c, :].rearrange("p (two m) -> p two m", two=2),
                               bank(job)[:].rearrange("p (m two) -> p two m", two=2), ACT.Identity,
                               bias=col("short_b", c), scale=col("short_w", 12 + c)).then_inc(s_conv, 1)

            def evac_z(o):
                for k in range(4):
                    job = ("zT", o, k)
                    wait_filled(act, job)
                    if o == 0 and k == 0:
                        wait_freed(act, ("filt", 1, 3, 1))
                    if o == 1 and k == 0:
                        wait_filled(act, ("fwd", 0, 1, 3))
                    free(act.activation(zt[:, k, :], bank(job)[:], ACT.Copy), job)

            def evac_fwd(o):
                for f in range(2):
                    for c in range(4):
                        job = ("fwd", o, f, c)
                        wait_filled(act, job)
                        if c == 0:
                            if o == 0 and f == 0:
                                act.wait_ge(s_kab, 4)
                            else:
                                act.wait_ge(s_ab, 2 * o + f)
                        free(act.activation(ep[:, c, :], bank(job)[:], ACT.Copy), job)

            evac_z(0)
            evac_fwd(0)
            for i in range(TT):
                job = ("q", i)
                wait_filled(act, job)
                if i == 0:
                    wait_filled(act, ("hT", 0, KT - 1))
                free(act.activation(qkv[:, i, 0:512], bank(job)[:], ACT.Copy), job)
            for i in range(TT):
                job = ("kv", i)
                wait_filled(act, job)
                free(act.activation(qkv[:, i, 512:768], bank(job)[:, 0:256], ACT.Copy), job)
            evac_z(1)
            evac_fwd(1)
            for j in range(MT):
                wait_filled(act, ("mk", j))
                free(act.activation(mk[:, j, :], bank(("mk", j))[:], ACT.Copy), ("mk", j))
            for j in range(MT):
                wait_filled(act, ("mv", j))
                free(act.activation(mv[:, j, :], bank(("mv", j))[:], ACT.Copy), ("mv", j))
            head_rms(230, TT * (NQ + NKV), HD, 1)
            head_rms(40, MT * MH, MHD, 2)
            for j in range(2):
                wait_filled(act, ("mkT", j))
                if j == 0:
                    wait_filled(act, ("inv", 1, CT - 1))
                free(act.activation(mkT[:, 2 * j:2 * j + 2, :].rearrange("p h m -> p (h m)"), bank(("mkT", j))[:], ACT.Copy),
                     ("mkT", j))
            for p in range(NQ // 2):
                wait_filled(act, ("qT", p))
                free(act.activation(qT[:, p, :], bank(("qT", p))[:], ACT.Copy), ("qT", p))
            for g in range(NKV):
                wait_filled(act, ("kT", g))
                free(act.activation(kT[:, g, :], bank(("kT", g))[:], ACT.Copy), ("kT", g))

            for c in range(CT):
                job = ("hn", c)
                wait_filled(act, job)
                if c == 0:
                    wait_filled(act, ("inv", 1, CT - 1))
                free(act.activation(y_rs[:, c, :], bank(job)[:], ACT.Sqrt, bias=eps, scale=1.0 / HD), job)

            def gqa_exp(s):
                act.wait_ge(s_max, s + 1)
                if s >= NPR:
                    wait_filled(act, ("PT", s - NPR))
                free(act.activation(pr[:, s % NPR, :], bank(("S", s))[:], ACT.Exp, bias=small[:, 100 + s:101 + s],
                                    accum_out=small[:, 140 + s:141 + s]), ("S", s))

            def gqa_pt(s):
                wait_filled(act, ("PT", s))
                if s >= NPR:
                    act.wait_ge(s_asq, s - NPR + 1)
                free(act.activation(pT[:, s % NPR, :], bank(("PT", s))[:], ACT.Copy), ("PT", s))

            for s in range(AHEAD):
                gqa_exp(s)
            for s in range(NSEQ):
                gqa_pt(s)
                if s + AHEAD < NSEQ:
                    gqa_exp(s + AHEAD)
            head_rms(340, TT * NQ, HD, 3)
            for k in range(CT):
                wait_filled(act, ("yT", k))
                free(act.activation(yT[:, CT + k, :], bank(("yT", k))[:], ACT.Copy, scale=col("attn_norm", k)), ("yT", k))

            def x_norm_squares(first, jobkey, count):
                for i in range(TT):
                    wait_freed(act, (jobkey, 0, i))
                    wait_freed(act, (jobkey, 1, i))
                    act.activation(fb_flat, x2[:, i, :], ACT.Square, accum_out=small[:, first + i:first + i + 1])\
                        .then_inc(s_sq, 1)
                    act.wait_ge(s_sq, count + i + 1)
                    act.activation(small[:, 16 + first + i:17 + first + i], small[:, first + i:first + i + 1], ACT.Sqrt,
                                   bias=eps, scale=1.0 / D).then_inc(s_rms, 1)

            x_norm_squares(8, "wout", 6)
            for k in range(0, KT, 2):
                wait_filled(act, ("hT", 1, k))
                free(act.activation(hT[:, k, :], bank(("hT", 1, k))[:], ACT.Copy, scale=col("norm_xattn", k)), ("hT", 1, k))
            for i in range(TT):
                wait_filled(act, ("mq", i))
                free(act.activation(mq[:, i, :], bank(("mq", i))[:], ACT.Copy), ("mq", i))
            head_rms(40, TT * MH, MHD, 4)
            for h in range(MH):
                wait_filled(act, ("mqT", h))
                free(act.activation(mqT[:, h, :], bank(("mqT", h))[:], ACT.Copy), ("mqT", h))

            def mem_exp(s):
                act.wait_ge(s_max, NSEQ + s + 1)
                if s >= NPR:
                    wait_filled(act, ("MPT", s - NPR))
                for c in range(2):
                    ins = act.activation(pr[:, s % NPR, c * NM:(c + 1) * NM], bank(("MS", s))[:, c * NM:(c + 1) * NM], ACT.Exp,
                                         bias=small[:, 180 + 2 * s + c:181 + 2 * s + c], scale=MHD ** -0.5,
                                         accum_out=small[:, 200 + 2 * s + c:201 + 2 * s + c])
                free(ins, ("MS", s))

            def mem_pt(s):
                i, hp = s // 2, s % 2
                job = ("MPT", s)
                wait_filled(act, job)
                free(act.activation(mpT[:, 2 * hp:2 * hp + 2, :, i * P:(i + 1) * P],
                                    bank(job)[:].rearrange("p (h t n) -> p h t n", h=2, t=MT), ACT.Copy), job)

            for s in range(AHEAD):
                mem_exp(s)
            for s in range(MSEQ):
                if s + AHEAD < MSEQ:
                    mem_exp(s + AHEAD)
                mem_pt(s)
            for h in range(MH):
                wait_filled(act, ("mo", h))
                free(act.activation(moT[:, h, :], bank(("mo", h))[:], ACT.Copy), ("mo", h))
            x_norm_squares(12, "wom", 10)
            for k in range(0, KT, 2):
                wait_filled(act, ("hT", 2, k))
                free(act.activation(hT[:, k, :], bank(("hT", 2, k))[:], ACT.Copy, scale=col("norm_moe", k)), ("hT", 2, k))
            act.wait_ge(s_r1, 1)
            act.activation(rt[:, 100:116], rt[:, 84:100], ACT.Exp).then_inc(s_r2, 1)
            act.wait_ge(s_r3, 1)
            act.activation(rt[:, 204:208], rt[:, 200:204], ACT.Exp).then_inc(s_r4, 1)

            def rows_evac(b, q):
                act.wait_ge(s_t, 2 * b + 1)
                if not isinstance(b, int) or b >= 2:
                    act.wait_ge(s_up, b - 1)
                for k in range(4):
                    ins = act.activation(hgT[q][:, k, :], banks[0][:, k * P:(k + 1) * P], ACT.Copy, scale=col("norm_moe", k))
                ins.then_inc(s_ta, 1)

            def silu(b, q):
                act.wait_ge(s_gate, b + 1)
                if not isinstance(b, int) or b >= 2:
                    act.wait_ge(s_mul, b - 1)
                act.activation(sg[q][:], banks[2][:], ACT.Silu).then_inc(s_silu, 1)

            def actT_evac(b, q):
                act.wait_ge(s_at, b + 1)
                if not isinstance(b, int) or b >= 2:
                    act.wait_ge(s_down, b - 1)
                act.activation(gaT[q][:].rearrange("p k n -> p (k n)"), banks[4][:], ACT.Copy).then_inc(s_ate, 1)

            def out_evac(b, q):
                act.wait_ge(s_down0, b + 1)
                act.wait_ge(s_meta, b + 1)
                act.activation(eo[q][:, 0:512], banks[5][:], ACT.Copy, scale=meta_g[:, q, :]).then_inc(s_oa, 1)

            rows_evac(0, 0)
            silu(0, 0)
            rows_evac(1, 1)
            actT_evac(0, 0)
            silu(1, 1)
            rows_evac(2, 0)
            out_evac(0, 0)
            actT_evac(1, 1)
            act.wait_ge(s_tab, 1)
            nb = act.value_load(e_tab[0:1, 31:32], min_val=0, max_val=MAXB - NE) + NE
            with act.Fori(2, nb, 2) as b:
                silu(b, 0)
                rows_evac(b + 1, 1)
                out_evac(b - 1, 1)
                actT_evac(b, 0)
                silu(b + 1, 1)
                rows_evac(b + 2, 0)
                out_evac(b, 0)
                actT_evac(b + 1, 1)
            out_evac(nb - 1, 1)

        @block.vector
        def _(dve):
            steps = [0]

            def link(ins):
                steps[0] += 1
                ins.then_inc(dchain, 1)
                dve.wait_ge(dchain, steps[0])

            def range_reduce(j):
                job = ("mlp", j)
                wait_filled(dve, job)
                if j:
                    dve.wait_ge(s_sin, 1)
                link(dve.tensor_scalar(mlp_arg[:], bank(job)[0:FF, :], col("b1" if j == 0 else "b2", 0, FF),
                                       col("freq", j, FF), ALU.add, ALU.mult))
                link(dve.tensor_scalar(mlp_k[:], mlp_arg[:], 1.0 / (2 * np.pi), 12582912.0, ALU.mult, ALU.add))
                link(dve.tensor_scalar(mlp_k[:], mlp_k[:], 12582912.0, None, ALU.subtract))
                hi = 6.28125
                link(dve.scalar_tensor_tensor(mlp_arg[:], mlp_k[:], -hi, mlp_arg[:], ALU.mult, ALU.add))
                link(dve.scalar_tensor_tensor(mlp_arg[:], mlp_k[:], -(2 * np.pi - hi), mlp_arg[:], ALU.mult, ALU.add))
                dve.tensor_scalar(mlp_arg[:], mlp_arg[:], float(np.float32(-3.1415925)), float(np.float32(3.1415925)),
                                  ALU.max, ALU.min).then_inc(s_arg, 1)

            dve.wait_ge(ld["cols"], 16)
            dve.wait_ge(s_rms, 1)
            link(dve.reciprocal(small[:, 16:20], small[:, 16:20]))
            for i in range(TT):
                dve.tensor_scalar(x_in[:, i, :], x_in[:, i, :], small[:, 16 + i:17 + i], None, ALU.mult).then_inc(s_xn, 1)
            range_reduce(0)
            dve.wait_ge(s_arg, 1)
            free(dve.tensor_copy(small[0:1, 399:400], small[0:1, 16:17]), ("mlp", 0))
            dve.wait_ge(s_rms, 2)
            link(dve.reciprocal(small[:, 20:22], small[:, 20:22]))
            for j in range(MT):
                dve.tensor_scalar(mem_raw[:, j, :], mem_raw[:, j, :], small[:, 20 + j:21 + j], None, ALU.mult).then_inc(s_xn, 1)

            def hT_evac(n, name):
                for k in range(1, KT, 2):
                    job = ("hT", n, k)
                    wait_filled(dve, job)
                    free(dve.tensor_scalar(hT[:, k, :], bank(job)[:], col(name, k), None, ALU.mult), job)

            hT_evac(0, "norm_mix")
            range_reduce(1)
            dve.wait_ge(s_arg, 2)
            free(dve.tensor_copy(small[0:1, 399:400], small[0:1, 16:17]), ("mlp", 1))
            dve.wait_ge(ld["decay"], 16)
            for o in range(2):
                if o == 1:
                    dve.wait_ge(s_rn, 1)
                for t in range(4):
                    fwd, bwd = ("filt", o, t, 0), ("filt", o, t, 1)
                    if 4 * o + t:
                        dve.wait_ge(s_spdm, 4 * o + t)
                        dve.wait_ge(s_abs, 4 * o + t)
                    wait_filled(dve, fwd)
                    free(dve.tensor_tensor(fb[:, 0, :], bank(fwd)[:], decay[:, t, :], ALU.mult), fwd)
                    wait_filled(dve, bwd)
                    mask = col("not_first") if t == 0 else 1.0
                    free(dve.scalar_tensor_tensor(fb[:, 1, :], bank(bwd)[:], mask, decay[:, t, :], ALU.mult, ALU.mult), bwd)
                    dve.wait_ge(s_abs, 4 * o + t + 1)
                    if t == 0:
                        dve.tensor_tensor(l1sum[:], fabs[:, 0, :], fabs[:, 1, :], ALU.add).then_inc(s_l1, 1)
                    else:
                        link(dve.tensor_tensor(l1sum[:], l1sum[:], fabs[:, 0, :], ALU.add))
                        dve.tensor_tensor(l1sum[:], l1sum[:], fabs[:, 1, :], ALU.add).then_inc(s_l1, 1)
                    dve.wait_ge(s_l1, 4 * o + t + 1)
                wait_filled(dve, ("l1", o))
                free(dve.tensor_scalar(rnorm[:], bank(("l1", o))[:], EPS, None, ALU.add), ("l1", o))
                wait_freed(dve, ("l1", o))
                dve.reciprocal(rnorm[:], rnorm[:]).then_inc(s_rn, 1)
                dve.wait_ge(s_rn, o + 1)
                for f in range(2):
                    if 2 * o + f:
                        dve.wait_ge(s_kab, 2 * o + f)
                    for c in range(4):
                        job = ("spec", o, f, c)
                        wait_filled(dve, job)
                        free(dve.tensor_tensor(ep[:, c, :], bank(job)[:], rnorm[:], ALU.mult), job)
                    wait_freed(dve, ("spec", o, f, 3))
                    dve.tensor_copy(small[0:1, 398:399], small[0:1, 16:17]).then_inc(s_ke, 1)
            for c in range(12):
                job = ("u", c)
                dve.wait_ge(s_conv, c + 1)
                pe_, po = bank(job)[:, 0::2], bank(job)[:, 1::2]
                ue, uo = u[:, c, 0:HALF], u[:, c, HALF:T]
                w_prev, w_next = col("short_w", c), col("short_w", 24 + c)
                dve.scalar_tensor_tensor(ue, po, w_next, ue, ALU.mult, ALU.add)
                link(dve.scalar_tensor_tensor(uo, pe_, w_prev, uo, ALU.mult, ALU.add))
                dve.scalar_tensor_tensor(ue[:, 1:HALF], po[:, 0:HALF - 1], w_prev, ue[:, 1:HALF], ALU.mult, ALU.add)
                free(dve.scalar_tensor_tensor(uo[:, 0:HALF - 1], pe_[:, 1:HALF], w_next, uo[:, 0:HALF - 1],
                                              ALU.mult, ALU.add), job)

            def pointwise(o, f):
                n = 2 * o + f
                for c in range(4):
                    wait_freed(dve, ("fwd", o, f, c))
                if n == 0:
                    dve.wait_ge(s_kab, 4)
                if o == 1 and f == 0:
                    wait_filled(dve, ("inv", 0, CT - 1))
                dve.tensor_tensor(ab[:, 2, :], ep[:, 0, :], ep[:, 2, :], ALU.subtract)
                dve.tensor_tensor(ab[:, 3, :], ep[:, 1, :], ep[:, 3, :], ALU.subtract).then_inc(s_b, 1)
                dve.wait_ge(s_a, n + 1)
                kre, kim = spec[:, o, f, 0, :], spec[:, o, f, 1, :]
                are, aim = ab[:, 0, :], ab[:, 1, :]
                s_ = sd[:, f]
                dve.wait_ge(s_b, n + 1)
                dve.tensor_tensor(s_[:, 0, :], are, kre, ALU.mult)
                dve.tensor_tensor(s_[:, 1, :], aim, kim, ALU.mult)
                dve.tensor_tensor(s_[:, 2, :], are, kim, ALU.mult)
                link(dve.tensor_tensor(s_[:, 3, :], aim, kre, ALU.mult))
                dve.tensor_tensor(ep[:, 0, :], s_[:, 0, :], s_[:, 1, :], ALU.subtract)
                link(dve.tensor_tensor(ep[:, 2, :], s_[:, 2, :], s_[:, 3, :], ALU.add))
                dve.wait_ge(s_pb, n + 1)
                dve.tensor_tensor(ab[:, 0, :], ep[:, 1, :], ep[:, 3, :], ALU.subtract)
                link(dve.tensor_tensor(ab[:, 1, :], tmp[:, 0, :], tmp[:, 1, :], ALU.add))
                dve.tensor_tensor(s_[:, 0, :], ep[:, 0, :], ab[:, 0, :], ALU.add)
                dve.tensor_tensor(s_[:, 2, :], ep[:, 0, :], ab[:, 0, :], ALU.subtract)
                dve.tensor_tensor(s_[:, 1, :], ep[:, 2, :], ab[:, 1, :], ALU.add)
                dve.tensor_tensor(s_[:, 3, :], ep[:, 2, :], ab[:, 1, :], ALU.subtract).then_inc(s_ab, 1)

            def gated(o):
                for c in range(CT):
                    job = ("inv", o, c)
                    wait_filled(dve, job)
                    free(dve.scalar_tensor_tensor(u[:, c, :], u[:, c, :], col("skip", o * CT + c), bank(job)[:],
                                                  ALU.mult, ALU.add), job)
                    wait_freed(dve, job)
                    dve.tensor_tensor(u[:, c, :], u[:, c, :], u[:, CT * (o + 1) + c, :], ALU.mult).then_inc(s_z, 1)

            def head_sums(x3, sq3, ss):
                link(dve.tensor_tensor(sq3, x3, x3, ALU.mult))
                return dve.tensor_reduce(ss, sq3, AX.X, ALU.add)

            def qk(i):
                return qkv[:, i, 0:640].rearrange("p (h d) -> p h d", d=HD)

            def roped(i):
                nh = NQ + NKV
                x3 = qk(i)
                t3 = rope_tmp[:].rearrange("p (h d) -> p h d", d=HD)
                inv = small[:, 230 + nh * i:230 + nh * (i + 1)]
                link(dve.tensor_tensor(x3, x3, inv.unsqueeze(2).to_broadcast([P, nh, HD]), ALU.mult))
                dve.tensor_tensor(x3[:, 0:NQ, :], x3[:, 0:NQ, :], row("gq").unsqueeze(1).to_broadcast([P, NQ, HD]), ALU.mult)
                link(dve.tensor_tensor(x3[:, NQ:, :], x3[:, NQ:, :], row("gk").unsqueeze(1).to_broadcast([P, NKV, HD]), ALU.mult))
                x5 = qkv[:, i, 0:640].rearrange("p (h s w d) -> p h s w d", s=2, w=2, d=HD // 4)
                t5 = rope_tmp[:].rearrange("p (h s w d) -> p h s w d", s=2, w=2, d=HD // 4)
                sn = rope[:, 1, i, :].rearrange("p (s w d) -> p s w d", s=2, w=2)
                for w in range(2):
                    for s in range(2):
                        ins = dve.tensor_tensor(t5[:, :, s, w, :], x5[:, :, s, 1 - w, :],
                                                sn[:, s, w, :].unsqueeze(1).to_broadcast([P, nh, HD // 4]), ALU.mult)
                link(ins)
                link(dve.tensor_tensor(x3, x3, rope[:, 0, i, :].unsqueeze(1).to_broadcast([P, nh, HD]), ALU.mult))
                dve.tensor_tensor(x3, x3, t3, ALU.add).then_inc(s_rope, 1)
                dve.wait_ge(s_rope, i + 1)

            pointwise(0, 0)
            pointwise(0, 1)
            gated(0)
            pointwise(1, 0)
            pointwise(1, 1)
            dve.wait_ge(ld["rows"], 16)
            dve.wait_ge(ld["rope"], 16)
            dve.wait_ge(s_gq, 1)
            for i in range(TT):
                wait_freed(dve, ("kv", i))
                wait_freed(dve, ("q", i))
                ins = head_sums(qk(i), rope_tmp[:].rearrange("p (h d) -> p h d", d=HD), small[:, 230 + 10 * i:240 + 10 * i])
                if i < TT - 1:
                    link(ins)
            ins.then_inc(s_ms, 1)
            for j in range(MT):
                wait_freed(dve, ("mk", j))
                dve.wait_ge(s_ms, 1)
                ins = head_sums(mk[:, j, :].rearrange("p (h d) -> p h d", d=MHD),
                                rope_tmp[:, 0:512].rearrange("p (h d) -> p h d", d=MHD), small[:, 40 + MH * j:44 + MH * j])
                if j < MT - 1:
                    link(ins)
            ins.then_inc(s_ms, 1)
            dve.wait_ge(s_ms, 2)
            dve.wait_ge(s_hrms, 1)
            link(dve.reciprocal(small[:, 230:270], small[:, 230:270]))
            for i in range(TT):
                roped(i)
            dve.wait_ge(s_hrms, 2)
            link(dve.reciprocal(small[:, 40:48], small[:, 40:48]))
            for j in range(MT):
                x3 = mk[:, j, :].rearrange("p (h d) -> p h d", d=MHD)
                link(dve.tensor_tensor(x3, x3, small[:, 40 + MH * j:44 + MH * j].unsqueeze(2).to_broadcast([P, MH, MHD]), ALU.mult))
                dve.tensor_tensor(x3, x3, row("gmk").unsqueeze(1).to_broadcast([P, MH, MHD]), ALU.mult).then_inc(s_mkn, 1)
            gated(1)
            dve.wait_ge(s_rope, TT)
            for w in range(2):
                ins = dve.tensor_copy(kdup[:, :, :, w, :], qkv[:, :, 512:640].rearrange("p i (g d) -> p i g d", d=HD))
            ins.then_inc(s_kdup, 1)
            def hyena_recip(n):
                c, piece = n // 4, y_rs[:, n // 4, (n % 4) * P:(n % 4 + 1) * P]
                if n % 4 == 0:
                    wait_freed(dve, ("hn", c))
                link(dve.reciprocal(piece, piece))

            def hyena_norm(c):
                dve.scalar_tensor_tensor(yT[:, c, :].rearrange("p (m two) -> p two m", two=2),
                                         u[:, c, :].rearrange("p (two m) -> p two m", two=2), col("hyena_norm", c),
                                         y_rs[:, c, :].rearrange("p (two m) -> p two m", two=2), ALU.mult, ALU.mult)\
                    .then_inc(s_yh, 1)

            def gqa_max(s):
                wait_filled(dve, ("S", s))
                dve.tensor_reduce(small[:, 100 + s:101 + s], bank(("S", s))[:], AX.X, ALU.max, negate=True)\
                    .then_inc(s_max, 1)

            def att_out(i):
                job = ("O", i)
                for h in range(NQ):
                    wait_freed(dve, ("S", i * NQ + h))
                link(dve.reciprocal(small[:, 50:58], small[:, 140 + i * NQ:148 + i * NQ]))
                dve.wait_ge(s_asq, (i + 1) * NQ)
                o3 = att[:, i, :].rearrange("p (h d) -> p h d", d=HD)
                free(dve.tensor_tensor(o3, bank(job)[:].rearrange("p (h d) -> p h d", d=HD),
                                       small[:, 50:58].unsqueeze(2).to_broadcast([P, NQ, HD]), ALU.mult), job)
                wait_freed(dve, job)
                ins = head_sums(o3, att_sq[:].rearrange("p (h d) -> p h d", d=HD), small[:, 340 + NQ * i:340 + NQ * (i + 1)])
                if i < TT - 1:
                    link(ins)
                else:
                    ins.then_inc(s_ms, 1)

            for s in range(AHEAD + 1):
                gqa_max(s)
            for s in range(NSEQ):
                if s + AHEAD + 1 < NSEQ:
                    gqa_max(s + AHEAD + 1)
                if s % NQ == 3 and s > NQ:
                    att_out(s // NQ - 1)
                if s < 4 * CT:
                    hyena_recip(s)
                    if s % 4 == 3:
                        hyena_norm(s // 4)
            att_out(TT - 1)
            dve.wait_ge(s_hrms, 3)
            link(dve.reciprocal(small[:, 340:372], small[:, 340:372]))
            for i in range(TT):
                o3 = att[:, i, :].rearrange("p (h d) -> p h d", d=HD)
                dve.tensor_tensor(o3, o3, small[:, 340 + NQ * i:340 + NQ * (i + 1)].unsqueeze(2).to_broadcast([P, NQ, HD]),
                                  ALU.mult).then_inc(s_att, 1)

            def residual(jobkey):
                for h in range(2):
                    for i in range(TT):
                        job = (jobkey, h, i)
                        wait_filled(dve, job)
                        xs = x2[:, i, h * 512:(h + 1) * 512]
                        free(dve.tensor_tensor(xs, xs, bank(job)[:], ALU.add), job)

            def x_norm(first, roots):
                for i in range(TT):
                    dve.wait_ge(s_rms, roots + i + 1)
                    inv = small[:, 16 + first + i:17 + first + i]
                    link(dve.reciprocal(inv, inv))
                    dve.tensor_scalar(xn[:, i, :], x2[:, i, :], inv, None, ALU.mult).then_inc(s_xn, 1)

            dve.wait_ge(ld["x2"], 16 * TT)
            residual("wout")
            x_norm(8, 2)
            hT_evac(1, "norm_xattn")
            for i in range(TT):
                wait_freed(dve, ("mq", i))
                ins = head_sums(mq[:, i, :].rearrange("p (h d) -> p h d", d=MHD),
                                att_sq[:].rearrange("p (h d) -> p h d", d=MHD), small[:, 40 + MH * i:44 + MH * i])
                if i < TT - 1:
                    link(ins)
            ins.then_inc(s_ms, 1)
            dve.wait_ge(s_hrms, 4)
            link(dve.reciprocal(small[:, 40:56], small[:, 40:56]))
            for i in range(TT):
                x3 = mq[:, i, :].rearrange("p (h d) -> p h d", d=MHD)
                link(dve.tensor_tensor(x3, x3, small[:, 40 + MH * i:44 + MH * i].unsqueeze(2).to_broadcast([P, MH, MHD]), ALU.mult))
                dve.tensor_tensor(x3, x3, row("gmq").unsqueeze(1).to_broadcast([P, MH, MHD]), ALU.mult).then_inc(s_mqn, 1)

            def mem_max(s):
                wait_filled(dve, ("MS", s))
                if s:
                    dve.wait_ge(s_max, NSEQ + s)
                link(dve.tensor_reduce(small[:, 220:222], bank(("MS", s))[:].rearrange("p (h m) -> p h m", h=2), AX.X, ALU.max))
                dve.tensor_scalar(small[:, 180 + 2 * s:182 + 2 * s], small[:, 220:222], -(MHD ** -0.5), None, ALU.mult)\
                    .then_inc(s_max, 1)

            def mem_probs(s):
                wait_freed(dve, ("MS", s))
                if s:
                    dve.wait_ge(s_mnorm, s)
                link(dve.reciprocal(small[:, 224:226], small[:, 200 + 2 * s:202 + 2 * s]))
                for c in range(2):
                    ins = dve.tensor_scalar(pr[:, s % NPR, c * NM:(c + 1) * NM], pr[:, s % NPR, c * NM:(c + 1) * NM],
                                            small[:, 224 + c:225 + c], None, ALU.mult)
                ins.then_inc(s_mnorm, 1)

            for s in range(AHEAD):
                mem_max(s)
            for s in range(MSEQ):
                if s + AHEAD < MSEQ:
                    mem_max(s + AHEAD)
                mem_probs(s)
            residual("wom")
            x_norm(12, 6)
            hT_evac(2, "norm_moe")

            def R(lo, n):
                return rt[:, lo:lo + n]

            def R3(lo, w, n=TT):
                return rt[:, lo:lo + n * w].rearrange("p (t w) -> p t w", w=w)

            def bc(x, w):
                return x.unsqueeze(2).to_broadcast([P, TT, w])

            lg = R3(0, NG + NE)
            job = ("router",)
            wait_filled(dve, job)
            free(dve.tensor_tensor(lg, bank(job)[:, 0:TT * 20].rearrange("p (t w) -> p t w", w=20),
                                   row("b_router").unsqueeze(1).to_broadcast([P, TT, 20]), ALU.add), job)
            wait_freed(dve, job)
            gl = lg[:, :, 0:NG]
            link(dve.tensor_reduce(R(80, 4), gl, AX.X, ALU.max))
            dve.tensor_tensor(R3(84, 4), gl, bc(R(80, 4), 4), ALU.subtract).then_inc(s_r1, 1)
            first4 = row("first4").unsqueeze(1).to_broadcast([P, TT, 4])

            def first_only(dst, x, top, scratch, scratch1):
                link(dve.tensor_tensor(dst, x, bc(top, 4), ALU.is_equal))
                link(dve.tensor_tensor(scratch, dst, first4, ALU.mult))
                link(dve.tensor_reduce(scratch1, scratch, AX.X, ALU.max))
                link(dve.tensor_tensor(dst, scratch, bc(scratch1, 4), ALU.is_equal))

            ohg = R3(120, 4)
            first_only(ohg, gl, R(80, 4), R3(136, 4), R(152, 4))
            pick = rt[:, 640:640 + 64].rearrange("p (t e g) -> p t e g", t=TT, e=EPG)
            el = lg[:, :, NG:].rearrange("p t (g e) -> p t e g", g=NG)
            for t in range(TT):
                ins = dve.tensor_tensor(pick[:, t], el[:, t], ohg[:, t, :].unsqueeze(1).to_broadcast([P, EPG, NG]), ALU.mult)
            link(ins)
            sel = R3(160, 4)
            link(dve.tensor_reduce(sel, pick, AX.X, ALU.add))
            link(dve.tensor_reduce(R(176, 4), sel, AX.X, ALU.max))
            oh1, oh2 = R3(210, 4), R3(226, 4)
            first_only(oh1, sel, R(176, 4), R3(136, 4), R(152, 4))
            rest = R3(242, 4)
            link(dve.scalar_tensor_tensor(rest, oh1, -3.0e38, sel, ALU.mult, ALU.add))
            link(dve.tensor_reduce(R(180, 4), rest, AX.X, ALU.max))
            dve.tensor_tensor(R(200, 4), R(180, 4), R(176, 4), ALU.subtract).then_inc(s_r3, 1)
            first_only(oh2, rest, R(180, 4), R3(136, 4), R(152, 4))
            dve.wait_ge(s_r2, 1)
            link(dve.tensor_reduce(R(260, 4), R3(100, 4), AX.X, ALU.add))
            link(dve.reciprocal(R(260, 4), R(260, 4)))
            dve.wait_ge(s_r4, 1)
            link(dve.tensor_scalar(R(264, 4), R(204, 4), 1.0, None, ALU.add))
            link(dve.reciprocal(R(264, 4), R(264, 4)))
            link(dve.tensor_tensor(R(268, 4), R(260, 4), R(264, 4), ALU.mult))
            link(dve.tensor_tensor(R(272, 4), R(268, 4), R(204, 4), ALU.mult))
            E1 = rt[:, 300:364].rearrange("p (t g e) -> p t g e", t=TT, g=NG)
            E2 = rt[:, 364:428].rearrange("p (t g e) -> p t g e", t=TT, g=NG)
            for oh, E in ((oh1, E1), (oh2, E2)):
                for t in range(TT):
                    ins = dve.tensor_tensor(E[:, t], ohg[:, t, :].unsqueeze(2).to_broadcast([P, NG, EPG]),
                                            oh[:, t, :].unsqueeze(1).to_broadcast([P, NG, EPG]), ALU.mult)
            link(ins)
            dve.tensor_tensor(R(428, 64), R(300, 64), R(364, 64), ALU.add).then_inc(s_oh, 1)
            job = ("count",)
            wait_filled(dve, job)
            free(dve.tensor_copy(R(500, 80), bank(job)[:, 0:80]), job)
            wait_freed(dve, job)
            pos, cnt = R(500, 64), R(564, 16)

            def above(dst, x, bounds, op, scratch):
                link(dve.tensor_scalar(dst, x, float(bounds[0]), None, op))
                for v in bounds[1:]:
                    link(dve.scalar_tensor_tensor(dst, x, float(v), dst, op, ALU.add))

            ov, inc, nxt = R(720, 16), R(736, 16), R(752, 16)
            above(ov, cnt, (128, 256, 384), ALU.is_gt, None)
            link(dve.tensor_copy(inc, ov))
            for s in (1, 2, 4, 8):
                dve.tensor_copy(nxt[:, 0:s], inc[:, 0:s])
                link(dve.tensor_tensor(nxt[:, s:], inc[:, s:], inc[:, 0:NE - s], ALU.add))
                inc, nxt = nxt, inc
            hi = R(780, 64)
            above(hi, pos, (128, 256, 384), ALU.is_ge, None)
            far, lo, blkn = R(850, 64), R(920, 64), R(990, 64)
            link(dve.scalar_tensor_tensor(lo, hi, -128.0, pos, ALU.mult, ALU.add))
            link(dve.tensor_scalar(far, hi, 0.0, None, ALU.is_gt))
            exp4 = row("expert").unsqueeze(1).to_broadcast([P, TT, NE])
            link(dve.tensor_tensor(R(1060, 16), inc, ov, ALU.subtract))
            link(dve.tensor_tensor(R(1060, 16), R(1060, 16), row("expert"), ALU.subtract))
            b3 = R3(990, NE)
            link(dve.scalar_tensor_tensor(b3, R3(780, NE), float(NE - 1), R(1060, 16).unsqueeze(1).to_broadcast([P, TT, NE]),
                                          ALU.add, ALU.add))
            link(dve.tensor_tensor(blkn, blkn, far, ALU.mult))
            link(dve.tensor_tensor(b3, b3, exp4, ALU.add))
            link(dve.scalar_tensor_tensor(lo, lo, float(NB), blkn, ALU.mult, ALU.add))
            link(dve.tensor_tensor(R(1100, 64), lo, R(300, 64), ALU.mult))
            link(dve.tensor_tensor(R(1170, 64), lo, R(364, 64), ALU.mult))
            link(dve.tensor_reduce(R(1240, 4), R3(1100, NE), AX.X, ALU.add))
            link(dve.tensor_reduce(R(1244, 4), R3(1170, NE), AX.X, ALU.add))
            link(dve.tensor_copy(slot_i[:].rearrange("p r t -> p (r t)"), R(1240, 8)))
            tok = cols[:, COLS["token"]:COLS["token"] + TT]
            for r in range(2):
                dve.tensor_copy(rec[:, r, :, 0], tok)
                dve.tensor_scalar(rec[:, r, :, 1], tok, float(r * T), None, ALU.add)
                dve.tensor_copy(rec[:, r, :, 3], tok)
                ins = dve.tensor_copy(rec[:, r, :, 2], R(268 + 4 * r, 4))
            ins.then_inc(s_slot, 1)
            tab = rt[0:1, 1300:1332]
            tot = inc[0:1, 15:16]
            cmp = rt[0:1, 1340:1468].rearrange("p (i e) -> p i e", e=NE)
            link(dve.tensor_tensor(cmp, inc[0:1, :].unsqueeze(1).to_broadcast([1, 8, NE]),
                                   rows[0:1, ROWS["extra"][0]:ROWS["extra"][1]].unsqueeze(2).to_broadcast([1, 8, NE]), ALU.is_le))
            link(dve.memset(tab, 0.0))
            dve.tensor_copy(tab[:, 0:NE], rows[0:1, ROWS["expert"][0]:ROWS["expert"][1]])
            link(dve.tensor_reduce(tab[:, NE:NE + 8], cmp, AX.X, ALU.add))
            link(dve.tensor_scalar(tab[:, NE:NE + 8], tab[:, NE:NE + 8], float(NE - 1), None, ALU.min))
            half = rt[0:1, 1480:1481]
            above(half, tot, (1, 3, 5, 7), ALU.is_ge, None)
            link(dve.tensor_scalar(tab[:, 31:32], half, 2.0, None, ALU.mult))
            dve.tensor_copy(e_tab[:], tab).then_inc(s_tab, 1)

            def rows_evac(b, q):
                dve.wait_ge(s_t, 2 * b + 2)
                if not isinstance(b, int) or b >= 2:
                    dve.wait_ge(s_up, b - 1)
                for k in range(4, 8):
                    ins = dve.tensor_scalar(hgT[q][:, k, :], banks[1][:, (k - 4) * P:(k - 3) * P], col("norm_moe", k), None, ALU.mult)
                ins.then_inc(s_td, 1)

            def act_mul(b, q):
                dve.wait_ge(s_silu, b + 1)
                dve.wait_ge(s_up, b + 1)
                if not isinstance(b, int) or b >= 2:
                    dve.wait_ge(s_at, b - 1)
                dve.tensor_tensor(ga[q][:], sg[q][:], banks[3][:], ALU.mult).then_inc(s_mul, 1)

            def out_evac(b, q):
                dve.wait_ge(s_down, b + 1)
                dve.wait_ge(s_meta, b + 1)
                dve.tensor_scalar(eo[q][:, 512:D], banks[6][:], meta_g[:, q, :], None, ALU.mult).then_inc(s_od, 1)

            dve.wait_ge(s_tab, 1)
            rows_evac(0, 0)
            act_mul(0, 0)
            rows_evac(1, 1)
            act_mul(1, 1)
            rows_evac(2, 0)
            out_evac(0, 0)
            nb = dve.value_load(e_tab[0:1, 31:32], min_val=0, max_val=MAXB - NE) + NE
            with dve.Fori(2, nb, 2) as b:
                act_mul(b, 0)
                rows_evac(b + 1, 1)
                out_evac(b - 1, 1)
                act_mul(b + 1, 1)
                rows_evac(b + 2, 0)
                out_evac(b, 0)
            out_evac(nb - 1, 1)
            dve.wait_ge(ld["back"], 16 * 2 * TT)
            for i in range(TT):
                dve.tensor_tensor(x2[:, i, :], x2[:, i, :], y_back[:, 0, i, :], ALU.add).then_inc(s_fin, 1)
                dve.wait_ge(s_fin, 2 * i + 1)
                dve.tensor_tensor(x2[:, i, :], x2[:, i, :], y_back[:, 1, i, :], ALU.add).then_inc(s_fin, 1)

        @block.tensor
        def _(pe):
            def done(ins):
                ins.then_inc(filled, 1)

            def accumulate(job, dst, pairs):
                for n, (l, r) in enumerate(pairs):
                    ins = pe.matmul(dst, l, r, start=(n == 0), stop=(n == len(pairs) - 1))
                return ins

            def transposes(job, srcs, width=P):
                open_bank(pe, job)
                for n, s in enumerate(srcs):
                    ins = pe.transpose(bank(job)[:, n * width:(n + 1) * width], s, ident[:])
                done(ins)

            def mlp(j):
                job = ("mlp", j)
                open_bank(pe, job)
                if j == 0:
                    pe.wait_ge(ld["w12"], 32)
                    pe.wait_ge(ld["zemb"], 16)
                    done(pe.matmul(bank(job)[0:FF, :], w1[:], zemb[:], start=True, stop=True))
                else:
                    pe.wait_ge(s_sin, 1)
                    done(pe.matmul(bank(job)[0:FF, :], w2[:], a1[:], start=True, stop=True))

            def hT_jobs(n, src, count):
                for k in range(KT):
                    if k == 0:
                        pe.wait_ge(s_xn, count + TT)
                    transposes(("hT", n, k), [src[:, i, k * P:(k + 1) * P] for i in range(TT)])

            mlp(0)
            pe.wait_ge(ld["mats"], 64)
            hT_jobs(0, x_in, 0)
            mlp(1)
            pe.wait_ge(s_xn, TT + MT)
            for j in range(KT // 2):
                transposes(("memT", j), [mem_raw[:, m, k * P:(k + 1) * P] for k in (2 * j, 2 * j + 1) for m in range(MT)])
            pe.wait_ge(s_sin, 2)
            pe.wait_ge(ld["w3"], 16)
            pe.wait_ge(ld["dft"], 16)
            for o in range(2):
                for t in range(4):
                    for way in range(2):
                        job = ("filt", o, t, way)
                        open_bank(pe, job)
                        c0 = (2 * o + way) * CH
                        done(pe.matmul(bank(job)[:], a2[:, t * P:(t + 1) * P], w3[:, c0:c0 + CH], start=True, stop=True))
                job = ("l1", o)
                open_bank(pe, job)
                pe.wait_ge(s_l1, 4 * o + 4)
                done(pe.matmul(bank(job)[:], ones[:], l1sum[:], start=True, stop=True))
                pe.wait_ge(s_spdm, 4 * o + 4)
                for f in range(2):
                    for c in range(4):
                        job = ("spec", o, f, c)
                        open_bank(pe, job)
                        src = sp if c % 2 == 0 else dm
                        par = c // 2
                        done(accumulate(job, bank(job)[:], [(dft[:, k, c, f * P:(f + 1) * P], src[:, 2 * par + k, :])
                                                            for k in range(2)]))
            for n, name in enumerate(("v", "g1", "g2")):
                wait_chunk(pe, name)
                if n == 0:
                    for k in range(KT):
                        wait_freed(pe, ("hT", 0, k))
                w = chunk(name)
                for c in range(CT):
                    job = ("u", CT * n + c)
                    open_bank(pe, job)
                    done(accumulate(job, bank(job)[:], [(w[:, k, c * P:(c + 1) * P], hT[:, k, :]) for k in range(KT)]))
                pe.wait_ge(filled, number[job] + 1)
                pe.sem_inc(ring_used, 1)

            def z_jobs(o):
                for k in range(4):
                    if k == 0:
                        if o == 0:
                            for c in range(CT):
                                wait_freed(pe, ("u", c))
                        else:
                            pe.wait_ge(s_z, CT)
                    transposes(("zT", o, k), [u[:, c, k * P:(k + 1) * P] for c in range(CT)])

            def fwd_jobs(o):
                for f in range(2):
                    for c in range(4):
                        job = ("fwd", o, f, c)
                        open_bank(pe, job)
                        if f == 0 and c == 0:
                            for k in range(4):
                                wait_freed(pe, ("zT", o, k))
                        par = c // 2
                        done(accumulate(job, bank(job)[:], [(dft[:, k, c, f * P:(f + 1) * P], zt[:, 2 * par + k, :])
                                                            for k in range(2)]))

            def inv_jobs(o):
                pe.wait_ge(s_ab, 2 * o + 2)
                if o == 0:
                    pe.wait_ge(ld["idft"], 16)
                for c in range(CT):
                    job = ("inv", o, c)
                    open_bank(pe, job)
                    for par in range(2):
                        ins = accumulate(job, bank(job)[:, par * HALF:(par + 1) * HALF],
                                         [(sd[:, f, 2 * par + ri, c * P:(c + 1) * P], idft[:, f, 2 * par + ri, :])
                                          for f in range(2) for ri in range(2)])
                    done(ins)

            def token_jobs(key, n, lhs, w, width=512, kt=KT):
                for i in range(n):
                    job = (key, i)
                    open_bank(pe, job)
                    done(accumulate(job, bank(job)[:, 0:width], [(lhs[:, k, i * P:(i + 1) * P], w[:, k, :]) for k in range(kt)]))

            def chunk_done(job):
                pe.wait_ge(filled, number[job] + 1)
                pe.sem_inc(ring_used, 1)

            z_jobs(0)
            fwd_jobs(0)
            wait_chunk(pe, "q")
            token_jobs("q", TT, hT, chunk("q"))
            chunk_done(("q", TT - 1))
            wait_chunk(pe, "kv")
            token_jobs("kv", TT, hT, chunk("kv"), 256)
            chunk_done(("kv", TT - 1))
            inv_jobs(0)
            z_jobs(1)
            fwd_jobs(1)
            for j in range(KT // 2):
                wait_freed(pe, ("memT", j))
            wait_chunk(pe, "mk")
            token_jobs("mk", MT, memT, chunk("mk"))
            chunk_done(("mk", MT - 1))
            wait_chunk(pe, "mv")
            token_jobs("mv", MT, memT, chunk("mv"))
            chunk_done(("mv", MT - 1))
            inv_jobs(1)
            pe.wait_ge(s_mkn, MT)
            for j in range(2):
                transposes(("mkT", j), [mk[:, m, h * MHD:(h + 1) * MHD] for h in (2 * j, 2 * j + 1) for m in range(MT)])
            pe.wait_ge(s_rope, TT)
            for p in range(NQ // 2):
                transposes(("qT", p), [qkv[:, i, p * P:(p + 1) * P] for i in range(TT)])
            pe.wait_ge(s_kdup, 1)
            for g in range(NKV):
                transposes(("kT", g), [kdup[:, i, g].rearrange("p w d -> p (w d)") for i in range(TT)])
            for c in range(CT):
                job = ("hn", c)
                open_bank(pe, job)
                pe.wait_ge(s_ysq, c + 1)
                done(pe.matmul(bank(job)[:], blk[:], y_sq[:, c, :], start=True, stop=True))

            def score(s):
                i, h = s // NQ, s % NQ
                job = ("S", s)
                open_bank(pe, job)
                if s == 0:
                    for p in range(NQ // 2):
                        wait_freed(pe, ("qT", p))
                    for g in range(NKV):
                        wait_freed(pe, ("kT", g))
                lo = HD * (h % 2)
                done(pe.matmul(bank(job)[:], qT[lo:lo + HD, h // 2, i * P:(i + 1) * P], kT[lo:lo + HD, h // 4, :],
                               start=True, stop=True))

            def pt(s):
                wait_freed(pe, ("S", s))
                transposes(("PT", s), [pr[:, s % NPR, k * P:(k + 1) * P] for k in range(4)])

            def pv(s):
                i, h = s // NQ, s % NQ
                job = ("O", i)
                if h == 0:
                    open_bank(pe, job)
                wait_freed(pe, ("PT", s))
                v0 = 640 + HD * (h // 4)
                ins = accumulate(job, bank(job)[:, h * HD:(h + 1) * HD],
                                 [(pT[:, s % NPR, k * P:(k + 1) * P], qkv[:, k, v0:v0 + HD]) for k in range(4)])
                ins.then_inc(s_asq, 1)

            for s in range(AHEAD):
                score(s)
            for s in range(-1, NSEQ):
                if s + 1 + AHEAD < NSEQ:
                    score(s + 1 + AHEAD)
                if s + 1 < NSEQ:
                    pt(s + 1)
                if s >= 0:
                    pv(s)
            pe.wait_ge(s_att, TT)
            for k in range(CT):
                transposes(("yT", k), [att[:, i, k * P:(k + 1) * P] for i in range(TT)])
            pe.wait_ge(s_yh, CT)
            for k in range(CT):
                wait_freed(pe, ("yT", k))
            for h in range(2):
                wait_chunk(pe, f"wo{h}")
                w = chunk(f"wo{h}")
                for i in range(TT):
                    job = ("wout", h, i)
                    open_bank(pe, job)
                    done(accumulate(job, bank(job)[:], [(yT[:, k, i * P:(i + 1) * P], w[:, k, :]) for k in range(KT)]))
                chunk_done(job)
            hT_jobs(1, xn, 6)
            for k in range(KT):
                wait_freed(pe, ("hT", 1, k))
            wait_chunk(pe, "wq")
            token_jobs("mq", TT, hT, chunk("wq"))
            chunk_done(("mq", TT - 1))
            pe.wait_ge(s_mqn, TT)
            for h in range(MH):
                transposes(("mqT", h), [mq[:, i, h * MHD:(h + 1) * MHD] for i in range(TT)])

            def mem_score(s):
                i, hp = s // 2, s % 2
                job = ("MS", s)
                open_bank(pe, job)
                if s == 0:
                    for h in range(MH):
                        wait_freed(pe, ("mqT", h))
                    for j in range(2):
                        wait_freed(pe, ("mkT", j))
                for c in range(2):
                    h = 2 * hp + c
                    ins = pe.matmul(bank(job)[:, c * NM:(c + 1) * NM], mqT[:, h, i * P:(i + 1) * P], mkT[:, h, :],
                                    start=True, stop=True)
                done(ins)

            for s in range(AHEAD):
                mem_score(s)
            for s in range(MSEQ):
                if s + AHEAD < MSEQ:
                    mem_score(s + AHEAD)
                pe.wait_ge(s_mnorm, s + 1)
                transposes(("MPT", s), [pr[:, s % NPR, k * P:(k + 1) * P] for k in range(4)])
            for s in range(MSEQ):
                wait_freed(pe, ("MPT", s))
            for j in range(MT):
                wait_freed(pe, ("mv", j))
            for h in range(MH):
                job = ("mo", h)
                open_bank(pe, job)
                done(accumulate(job, bank(job)[:], [(mv[:, k, h * MHD:(h + 1) * MHD], mpT[:, h, k, :]) for k in range(MT)]))
            for h in range(MH):
                wait_freed(pe, ("mo", h))
            wait_chunk(pe, "wom")
            w = chunk("wom")
            for h in range(2):
                for i in range(TT):
                    job = ("wom", h, i)
                    open_bank(pe, job)
                    done(accumulate(job, bank(job)[:], [(moT[:, k, i * P:(i + 1) * P], w[:, k, h * 512:(h + 1) * 512])
                                                        for k in range(MH)]))
            chunk_done(job)
            hT_jobs(2, xn, 10)
            for k in range(KT):
                wait_freed(pe, ("hT", 2, k))
            job = ("router",)
            open_bank(pe, job)
            pe.wait_ge(ld["wr"], 16)
            for i in range(TT):
                ins = accumulate(job, bank(job)[:, i * 20:(i + 1) * 20],
                                 [(hT[:, k, i * P:(i + 1) * P], wr[:, k, :]) for k in range(KT)])
            done(ins)
            job = ("count",)
            open_bank(pe, job)
            pe.wait_ge(s_oh, 1)
            for i in range(TT + 1):
                pairs = [(ones[:], rt[:, 428 + NE * j:428 + NE * (j + 1)]) for j in range(i)]
                if i < TT:
                    pairs += [(tri[:], rt[:, 428 + NE * i:428 + NE * (i + 1)])]
                ins = accumulate(job, bank(job)[:, i * NE:(i + 1) * NE], pairs)
            done(ins)

            for b in range(7):
                pe.wait_ge(freed[b], uses[b])
            pe.wait_ge(s_tab, 1)

            def view(s):
                return slot[s][:].rearrange("p (t n) -> p t n", t=(8, 8, 4)[s % 3])

            def rows_T(b, q):
                pe.wait_ge(s_gath[q], (b - q) * 8 + 16)
                if not isinstance(b, int) or b >= 1:
                    pe.wait_ge(s_ta, b)
                    pe.wait_ge(s_td, b)
                for half in range(2):
                    for k in range(4):
                        c = 4 * half + k
                        ins = pe.transpose(banks[half][:, k * P:(k + 1) * P], hg[q][:, c * P:(c + 1) * P], ident[:])
                    ins.then_inc(s_t, 1)

            def gate_up(b, q):
                pe.wait_ge(s_ta, b + 1)
                pe.wait_ge(s_td, b + 1)
                if not isinstance(b, int) or b >= 1:
                    pe.wait_ge(s_mul, b)
                for c, sem_ in ((0, s_gate), (1, s_up)):
                    pe.wait_ge(w_ld[3 * q + c], (b - q) * 8 + 16)
                    w = view(3 * q + c)
                    accumulate(None, banks[2 + c][:], [(hgT[q][:, k, :], w[:, k, :]) for k in range(KT)]).then_inc(sem_, 1)

            def acts_T(b, q):
                pe.wait_ge(s_mul, b + 1)
                if not isinstance(b, int) or b >= 1:
                    pe.wait_ge(s_ate, b)
                for k in range(4):
                    ins = pe.transpose(banks[4][:, k * P:(k + 1) * P], ga[q][:, k * P:(k + 1) * P], ident[:])
                ins.then_inc(s_at, 1)

            def down(b, q):
                pe.wait_ge(s_ate, b + 1)
                pe.wait_ge(w_ld[3 * q + 2], (b - q) * 8 + 16)
                if not isinstance(b, int) or b >= 1:
                    pe.wait_ge(s_oa, b)
                    pe.wait_ge(s_od, b)
                w = view(3 * q + 2)
                for half, sem_ in ((0, s_down0), (1, s_down)):
                    accumulate(None, banks[5 + half][:], [(gaT[q][:, k, :], w[:, k, half * 512:(half + 1) * 512])
                                                          for k in range(4)]).then_inc(sem_, 1)

            rows_T(0, 0)
            gate_up(0, 0)
            rows_T(1, 1)
            acts_T(0, 0)
            gate_up(1, 1)
            rows_T(2, 0)
            down(0, 0)
            acts_T(1, 1)
            nb = pe.value_load(e_tab[0:1, 31:32], min_val=0, max_val=MAXB - NE) + NE
            with pe.Fori(2, nb, 2) as b:
                gate_up(b, 0)
                rows_T(b + 1, 1)
                down(b - 1, 1)
                acts_T(b, 0)
                gate_up(b + 1, 1)
                rows_T(b + 2, 0)
                down(b, 0)
                acts_T(b + 1, 1)
            down(nb - 1, 1)


def _constants():
    t = np.arange(T)
    half = np.arange(HALF)
    freq = (half + 0.5) * 2.0 * np.pi / (2 * T)
    parity = np.concatenate([t[0::2], t[1::2]])
    ang = parity[:, None] * freq[None, :]
    cs, sn = np.cos(ang), -np.sin(ang)
    dft = np.zeros((P, 2, 4, HALF))
    for par in range(2):
        for k in range(2):
            r = par * HALF + k * P
            dft[:, k, 2 * par] = cs[r:r + P]
            dft[:, k, 2 * par + 1] = sn[r:r + P]
    idft = np.zeros((P, 2, 4, HALF))
    for f in range(2):
        for par in range(2):
            r = slice(par * HALF, (par + 1) * HALF)
            idft[:, f, 2 * par] = cs[r, f * P:(f + 1) * P].T / T
            idft[:, f, 2 * par + 1] = sn[r, f * P:(f + 1) * P].T / T
    f32 = np.float32
    tl = np.linspace(0.0, 1.0, T, dtype=f32)
    bands = np.linspace(1e-4, 15, 16, dtype=f32)
    w = (f32(2.0 * np.pi / T) * t.astype(f32))[:, None] * bands[None, :]
    w = w.astype(f32)
    zemb = np.concatenate([tl[:, None], np.cos(w.astype(np.float64)), np.sin(w.astype(np.float64))], 1)[parity].T
    deltas = np.abs(np.linspace(np.log(1e-2) / 1.5, np.log(1e-2) / 0.3, CH, dtype=f32))
    decay = np.exp((-tl[:, None] * deltas[None, :]).astype(f32).astype(np.float64))[parity].reshape(4, P, CH).transpose(1, 0, 2)
    inv = 10000.0 ** (-np.arange(16) / 16.0)
    rope = np.zeros((P, 2, TT, HD))
    for i in range(TT):
        tok = i * P + np.arange(P)
        for s, pos in enumerate((tok // 64, tok % 64)):
            a = pos[:, None] * inv[None, :]
            for wv in range(2):
                c0 = 32 * s + 16 * wv
                rope[:, 0, i, c0:c0 + 16] = np.cos(a)
                rope[:, 1, i, c0:c0 + 16] = np.sin(a) * (1 if wv else -1)
    mats = np.zeros((P, 4, P))
    mats[:, 0] = np.eye(P)
    mats[:, 1] = 1.0
    mats[:, 2] = np.kron(np.eye(2), np.ones((HD, HD)))
    mats[:, 3] = np.triu(np.ones((P, P)), 1)
    rec = np.zeros((P, NB, 4))
    rec[:, :, 1] = SPARE + np.arange(P)[:, None]
    return {k: np.ascontiguousarray(v, dtype=f32) for k, v in
            dict(dft=dft, idft=idft, zemb=zemb, decay=decay, rope=rope, mats=mats, rec_init=rec.reshape(P * NB, 4)).items()}


_DIRECT = ["x", "mem", "w_in", "filt_w1", "filt_w2", "filt_w3", "w_out", "w_q_mem", "w_k_mem", "w_v_mem", "w_o_mem",
           "w_gate", "w_up", "w_down"]


def kernel(**inputs):
    import concourse.bacc as _bacc
    from concourse.bass_utils import run_bass_kernel_spmd as _run

    v = {k: np.ascontiguousarray(x) for k, x in inputs.items()}
    arrays = {k: v[k] for k in _DIRECT}
    arrays.update(_constants())

    def column(x):
        x = np.asarray(x).reshape(-1)
        if x.size < P:
            x = np.concatenate([x, np.zeros(P - x.size, x.dtype)])
        return x.reshape(-1, P).T

    not_first = np.ones((P, 1), np.float32)
    not_first[0] = 0.0
    token = (np.arange(P)[:, None] + P * np.arange(TT)[None, :]).astype(np.float32)
    arrays["cols"] = np.ascontiguousarray(np.concatenate(
        [column(v[k]) for k in ("norm_mix", "norm_xattn", "norm_mem", "norm_moe", "hyena_short_w", "hyena_short_b",
                                "hyena_skip", "out_norm_hyena", "out_norm_attn", "filt_b1", "filt_b2")]
        + [column(v["filt_sin_freq"][0, j]) for j in range(2)] + [not_first, token], axis=1))
    one_row = np.concatenate([v["attn_q_norm"][0], v["attn_k_norm"][0], v["mem_q_norm"][0], v["mem_k_norm"][0],
                              v["b_router_grp"][0], v["b_router_exp"][0],
                              np.array([4, 3, 2, 1], np.float32), np.arange(NE, dtype=np.float32),
                              np.arange(8, dtype=np.float32)])
    arrays["rows"] = np.ascontiguousarray(np.broadcast_to(one_row, (P, one_row.size)))
    arrays["w_router"] = np.ascontiguousarray(
        np.concatenate([v["w_router_grp"][0], v["w_router_exp"][0]], axis=1).reshape(KT, P, NG + NE).transpose(1, 0, 2))

    nc = _bacc.Bacc("TRN2", target_bir_lowering=False, num_devices=1)
    aps = {k: nc.dram_tensor(f"in_{k}", x.shape, mybir.dt.from_np(x.dtype), kind="ExternalInput").ap()
           for k, x in arrays.items()}
    out = nc.dram_tensor("out_0_dram", (1, T, D), F32, kind="ExternalOutput").ap()
    rec_dram = nc.dram_tensor("rec_dram", (P * NB, 4), F32, kind="Internal").ap()
    xn_dram = nc.dram_tensor("xn_dram", (T, D), F32, kind="Internal").ap()
    y_dram = nc.dram_tensor("y_dram", (2 * T + P, D), F32, kind="Internal").ap()
    build(nc, aps, out, rec_dram, xn_dram, y_dram)
    r = _run(nc, [{f"in_{k}": x for k, x in arrays.items()}], core_ids=[0])
    return r.results[0]["out_0_dram"]
```

```python
from contextlib import ExitStack

import numpy as np
import concourse.bass as bass
from concourse import mybir

F32 = mybir.dt.float32
F32R = mybir.dt.float32r
I32 = mybir.dt.int32
ALU = mybir.AluOpType
ACT = mybir.ActivationFunctionType
AX = mybir.AxisListType

P = 128
T, D = 512, 1024
TT, KT = T // P, D // P
NM = 256
MT = NM // P
CH = 512
CT = CH // P
HALF = T // 2
NQ, NKV, HD = 8, 2, 64
MH, MHD = 4, 128
NG, EPG = 4, 4
NE = NG * EPG
FE = 512
FB, FF = 33, 64
EPS = 1e-6
NB = 28
MAXB = 24
SPARE = 2 * T
AHEAD = 4
MAHEAD = 3
HN_STEP = 6
NSLOT = 3
NPR = 4
KB = 1024

COLS = {}
_at = 0
for _name, _n in (("norm_mix", KT), ("norm_xattn", KT), ("norm_mem", KT), ("norm_moe", KT),
                  ("short_w", 3 * 12), ("short_b", 12), ("skip", 2 * CT), ("hyena_norm", CT),
                  ("attn_norm", CT), ("b1", 1), ("b2", 1), ("freq", 2), ("gmq", 1), ("not_first", 1), ("token", TT)):
    COLS[_name] = _at
    _at += _n
NCOLS = _at
ROWS = {}
_at = 0
for _name, _n in (("gq", HD), ("gk", HD), ("gmq", MHD), ("gmk", MHD), ("b_router", NG + NE),
                  ("first4", 4), ("expert", NE), ("extra", 8)):
    ROWS[_name] = (_at, _at + _n)
    _at += _n
NROWS = _at


def psum_jobs():
    jobs = [("mlp", 0)] + [("memT", j) for j in range(KT // 2)] + [("mlp", 1)]

    def filt(o, tiles):
        return [("filt", o, t, way) for t in tiles for way in range(2)]

    def spec(o, f):
        return [("spec", o, f, c) for c in range(4)]

    jobs += [("mk", j) for j in range(MT)] + [("hT", 0, k) for k in range(KT)] + filt(0, range(4))
    jobs += [("mv", j) for j in range(MT)]
    jobs += [("l1", 0)] + spec(0, 0) + filt(1, (0, 1)) + spec(0, 1) + filt(1, (2, 3))
    jobs += [("u", c) for c in range(4)] + [("l1", 1)] + spec(1, 0) + spec(1, 1)
    jobs += [("zT", 0, k) for k in range(4)] + [("u", c) for c in range(4, 8)]
    for o in range(2):
        jobs += ([("zT", o, k) for k in range(4)] if o else []) + [("fwd", o, f, c) for f in range(2) for c in range(4)]
        jobs += [("u", c) for c in range(8, 12)] if o == 0 else [(key, i) for key in ("q", "kv") for i in range(TT)]
        jobs += [("inv", o, c) for c in range(CT)]
    jobs += [("mkT", j) for j in range(2)]
    jobs += [("qT", p) for p in range(NQ // 2)] + [("kT", g) for g in range(NKV)] + [("hn", c) for c in range(CT)]
    n = TT * NQ
    jobs += [("S", s) for s in range(AHEAD)]
    for s in range(-1, n):
        if s >= 0 and s % NQ == 0:
            jobs += [("O", s // NQ)]
        if s + 1 + AHEAD < n:
            jobs += [("S", s + 1 + AHEAD)]
        if s + 1 < n:
            jobs += [("PT", s + 1)]
    jobs += [("yT", k) for k in range(CT)]
    jobs += [("wout", h, i) for h in range(2) for i in range(TT)]
    jobs += [("hT", 1, k) for k in range(KT)]
    jobs += [("mq", i) for i in range(TT)] + [("mqT", h) for h in range(MH)]
    n = TT * 2
    jobs += [("MS", s) for s in range(MAHEAD)]
    for s in range(n):
        if s + MAHEAD < n:
            jobs += [("MS", s + MAHEAD)]
        jobs += [("MPT", s)]
    jobs += [("mo", h) for h in range(MH)]
    jobs += [("wom", h, i) for h in range(2) for i in range(TT)]
    jobs += [("hT", 2, k) for k in range(KT)]
    jobs += [("router",), ("count",)]
    return jobs


def build(nc, a, out, rec_dram, xn_dram, y_dram):
    with ExitStack() as ctx:
        base = nc.sbuf_base + (-nc.sbuf_base) % 64
        used = []

        def at(name, kb, shape, dt=F32):
            return nc.alloc_sbuf_tensor_at(name, shape, dt, offset=base + int(kb * KB))

        fence = ctx.enter_context(nc.sbuf_tensor("fence", [P, 205 * 256], F32))

        w_raw = [at(f"w_raw{s}", 4 * s, [P, 1024]) for s in range(NSLOT)]
        w_lo = [at(f"w_lo{s}", 4 * s, [P, 1024], F32R) for s in range(NSLOT)]
        w_hi = [at(f"w_hi{s}", 12 + 4 * s, [P, 1024], F32R) for s in range(NSLOT)]
        sum_diff1 = at("sum_diff1", 24, [P, 2, 4, CH])
        qkv = at("qkv", 24, [P, TT, 768])
        rope_tmp = at("rope_tmp", 36, [P, 640])
        mk = at("mk", 40, [P, MT, 512])
        mv = at("mv", 44, [P, MT, 512])
        hT_hi = at("hT_hi", 48, [P, KT, T], F32R)
        hT_lo = at("hT_lo", 64, [P, KT, T], F32R)
        hT = at("hT", 48, [P, KT, T])
        memT_hi = at("memT_hi", 80, [P, KT, NM], F32R)
        memT_lo = at("memT_lo", 88, [P, KT, NM], F32R)
        w3 = at("w3", 96, [FF, 2048])
        x_in = at("x_in", 120, [P, TT, D])
        mem_raw = at("mem_raw", 136, [P, MT, D])
        w1 = at("w1", 144, [FB, FF])
        w2 = at("w2", 144.5, [FF, FF])
        zemb = at("zemb", 146, [FB, T])
        a1 = at("a1", 148, [FF, T])
        a2 = at("a2", 150, [FF, T])
        u = at("u", 80, [P, 12, T])
        dft = at("dft", 104, [P, 2, 4, HALF])
        idft = at("idft", 112, [P, 2, 4, HALF])
        spec = at("spec", 120, [P, 2, 2, 4, CH])
        decay = at("decay", 152, [P, 4, CH])
        zt = at("zt", 152, [P, 4, CH])
        q_sq = at("q_sq", 152, [P, TT, 512])
        ep = at("ep", 160, [P, 4, CH])
        mlp_arg = at("mlp_arg", 172, [FF, T])
        mlp_k = at("mlp_k", 174, [FF, T])
        l1sum = at("l1sum", 168, [P, CH])
        rnorm = at("rnorm", 170, [P, CH])
        fabs = [at("fabs0", 172, [P, 2, CH]), at("fabs1", 140, [P, 2, CH])]
        ab = at("ab", 168, [P, 4, CH])
        sum_diff0 = at("sum_diff0", 176, [P, 2, 4, CH])
        sum_diff = [sum_diff0, sum_diff1]
        sd = at("sd", 176, [P, 2, 4, CH])
        fb = [at("fb0", 192, [P, 2, CH]), at("fb1", 136, [P, 2, CH])]
        tmp = at("tmp", 192, [P, 2, CH])
        qT = at("qT", 104, [P, NQ // 2, T])
        kT = at("kT", 112, [P, NKV, T])
        mkT = at("mkT", 116, [P, MH, NM])
        kdup = at("kdup", 160, [P, TT, NKV, 2, HD])
        x2 = at("x2", 120, [P, TT, D])
        yT_hi = at("yT_hi", 136, [P, KT, T], F32R)
        yT_lo = at("yT_lo", 64, [P, KT, T], F32R)
        att = at("att", 152, [P, TT, 512])
        pr = at("pr", 48, [P, NPR, T])
        pT = at("pT", 56, [P, NPR, T])
        att_sq = at("att_sq", 172, [P, 512])
        y_sq = at("y_sq", 176, [P, CT, CH])
        y_rs = at("y_rs", 184, [P, CT, CH])
        xn = at("xn", 80, [P, TT, D])
        mq = at("mq", 152, [P, TT, 512])
        mqT = at("mqT", 160, [P, MH, T])
        mpT = at("mpT", 176, [P, MH, MT, T])
        moT_hi = at("moT_hi", 104, [P, MH, T], F32R)
        moT_lo = at("moT_lo", 112, [P, MH, T], F32R)
        slot = [at(f"slot{s}", 16 * s, [P, 4096]) for s in range(6)]
        hg = [at(f"hg{q}", 136 + 4 * q, [P, D]) for q in range(2)]
        hgT = [at(f"hgT{q}", 144 + 4 * q, [P, KT, P]) for q in range(2)]
        sg = [at(f"sg{q}", 152 + 2 * q, [P, FE]) for q in range(2)]
        ga = [at(f"ga{q}", 156 + 2 * q, [P, FE]) for q in range(2)]
        gaT = [at(f"gaT{q}", 160 + 2 * q, [P, 4, P]) for q in range(2)]
        eo = [at(f"eo{q}", 164 + 4 * q, [P, D]) for q in range(2)]
        y_back = at("y_back", 0, [P, 2, TT, D])
        rt = at("rt", 172, [P, 3072])
        rec_sb = at("rec_sb", 184, [P, NB, 4])
        meta_i = at("meta_i", 185, [P, 2, 2], I32)
        meta_g = at("meta_g", 185.125, [P, 2, 1])
        gather_i = at("gather_i", 185.25, [P, 2, 1], I32)
        e_tab = at("e_tab", 185.5, [1, 32], I32)
        slot_i = at("slot_i", 186, [P, 2, TT], I32)
        wr = at("wr", 187, [P, KT, NG + NE])
        rec = at("rec", 188, [P, 2, TT, 4])
        cols = at("cols", 196, [P, NCOLS])
        rows = at("rows", 197, [P, NROWS])
        rope = at("rope", 199, [P, 2, TT, HD])
        ident = at("ident", 201, [P, P])
        ones = at("ones", 201.5, [P, P])
        blk = at("blk", 202, [P, P])
        tri = at("tri", 202.5, [P, P])
        small = at("small", 203, [P, 400])

        banks = [ctx.enter_context(nc.psum_tensor(f"bank{b}", [P, 512], F32)) for b in range(8)]

        def sem(name):
            return ctx.enter_context(nc.semaphore(name))

        jobs = psum_jobs()
        number, place, uses = {}, {}, [0] * 8
        turn, first_s = 0, jobs.index(("S", 0))
        last_s = max(n for n, j in enumerate(jobs) if j[0] == "PT")
        for n, j in enumerate(jobs):
            if j[0] == "O":
                b = 6 + j[1] % 2
            else:
                number[j] = len(number)
                span = 6 if first_s <= n <= last_s else 8
                b, turn = turn % span, (turn + 1) % span
            place[j] = (b, uses[b])
            uses[b] += 1
        filled = sem("psum_filled")
        freed = [sem(f"bank{b}_freed") for b in range(8)]
        def bank(job):
            return banks[place[job][0]]

        def wait_filled(eng, job):
            eng.wait_ge(filled, number[job] + 1)

        def free(ins, job):
            ins.then_inc(freed[place[job][0]], 1)

        def wait_freed(eng, job):
            eng.wait_ge(freed[place[job][0]], place[job][1] + 1)

        def open_bank(pe, job):
            b, use = place[job]
            if use:
                pe.wait_ge(freed[b], use)

        ld = {k: sem(f"ld_{k}") for k in ("x", "mem", "cols", "rows", "rope", "mats", "w12", "w3", "zemb", "decay",
                                          "dft", "idft", "x2", "wr", "rec0", "rec", "back")}
        ring_ld = [sem(f"ring_ld{s}") for s in range(NSLOT)]
        s_wh = sem("weight_hi_ready")
        s_wl = sem("weight_lo_ready")
        ring_used = sem("ring_used")
        s_hi = sem("hi_ready")
        s_xn = sem("xn_ready")
        s_arg = sem("mlp_arg_ready")
        s_sin = sem("mlp_sin_done")
        s_spdm = sem("spdm_ready")
        s_l1 = sem("l1_added")
        s_rn = sem("rnorm_ready")
        s_ke = sem("spec_parts_ready")
        s_kab = sem("spec_ready")
        s_conv = sem("conv_ready")
        s_a = sem("fwd_sum_ready")
        s_b = sem("fwd_diff_ready")
        s_pb = sem("prod_b_ready")
        s_ab = sem("prod_used")
        s_z = sem("z_ready")
        s_sq = sem("square_done")
        s_rms = sem("rms_ready")
        s_ms = sem("head_sums_ready")
        s_hrms = sem("head_rms_ready")
        s_abs = sem("filt_abs_ready")
        s_hroot = sem("hyena_rms_ready")
        s_rope = sem("rope_ready")
        s_kdup = sem("kdup_ready")
        s_qinv = sem("qk_norms_ready")
        s_mkn = sem("mk_normed")
        s_ysq = sem("y_square_ready")
        s_qsq = sem("q_square_ready")
        s_max = sem("score_max_ready")
        s_exp = sem("exp_done")
        s_att = sem("att_normed")
        s_yh = sem("y_hyena_ready")
        s_mqn = sem("mq_normed")
        s_mnorm = sem("mem_probs_ready")
        s_gq = sem("gq_scaled")
        s_asq = sem("att_square_done")
        s_store = sem("xn_stored")
        s_r1 = sem("route_group_logits")
        s_r2 = sem("route_group_exp")
        s_r3 = sem("route_expert_diff")
        s_r4 = sem("route_expert_exp")
        s_oh = sem("onehots_ready")
        s_slot = sem("slots_ready")
        s_scat = sem("records_scattered")
        s_tab = sem("tables_ready")
        dchain, achain, pchain = sem("dve_step"), sem("act_step"), sem("pool_step")
        w_ld = [sem(f"expert_w_ld{s}") for s in range(6)]
        s_gate, s_up, s_down0, s_down = sem("gate_done"), sem("up_done"), sem("down0_done"), sem("down_done")
        s_gath = [sem(f"gathered{q}") for q in range(2)]
        s_gi = sem("gather_index_ready")
        s_t = sem("rows_transposed")
        s_ta, s_td = sem("rowsT_evac_act"), sem("rowsT_evac_dve")
        s_silu, s_mul = sem("silu_done"), sem("act_mul_done")
        s_at, s_ate = sem("actT_filled"), sem("actT_evac")
        s_oa, s_od = sem("out_evac_act"), sem("out_evac_dve")
        s_meta = sem("meta_ready")
        s_sc = [sem(f"rows_scattered{q}") for q in range(2)]
        s_fin = sem("sum_ready")
        s_out = sem("stored")
        waited_pool, waited_sp = sem("waited_pool"), sem("waited_sp")

        def col(name, i=0, n=P):
            c = COLS[name] + i
            return cols[0:n, c:c + 1]

        def row(name):
            lo, hi = ROWS[name]
            return rows[:, lo:hi]

        w_in = a["w_in"][0].rearrange("(t p) n -> p t n", p=P)

        def mat(name):
            return a[name][0].rearrange("(t p) n -> p t n", p=P)

        w_out, w_om = mat("w_out"), mat("w_o_mem")
        chunks = [("mk", mat("w_k_mem"), 2, [("mk", j) for j in range(MT)]), ("mv", mat("w_v_mem"), 2, [("mv", j) for j in range(MT)]),
                  ("v", w_in[:, :, 0:512], 2, [("u", c) for c in range(4)]),
                  ("g1", w_in[:, :, 512:1024], 2, [("u", c) for c in range(4, 8)]),
                  ("g2", w_in[:, :, 1024:1536], 2, [("u", c) for c in range(8, 12)]),
                  ("q", w_in[:, :, 1536:2048], 2, [("q", i) for i in range(TT)]),
                  ("kv", w_in[:, :, 2048:2304], 4, [("kv", i) for i in range(TT)]),
                  ("wo0", w_out[:, :, 0:512], 2, [("wout", 0, i) for i in range(TT)]),
                  ("wo1", w_out[:, :, 512:1024], 2, [("wout", 1, i) for i in range(TT)]),
                  ("wq", mat("w_q_mem"), 2, [("mq", i) for i in range(TT)]),
                  ("wom0", w_om[:, :, 0:512], 2, [("wom", 0, i) for i in range(TT)]),
                  ("wom1", w_om[:, :, 512:1024], 2, [("wom", 1, i) for i in range(TT)])]
        pieces = [(name, k0, nk, src[:, k0:k0 + nk, :], jobs_) for name, src, nk, jobs_ in chunks
                  for k0 in range(0, src.shape[1], nk)]
        first_piece, last_piece = {}, {}
        for n, piece in enumerate(pieces):
            first_piece.setdefault(piece[0], n)
            last_piece[piece[0]] = n

        def wait_used(eng, n):
            name, jobs_ = pieces[n][0], pieces[n][4]
            if last_piece[name] == n:
                wait_filled(eng, jobs_[-1])
            else:
                eng.wait_ge(ring_used, sum(last_piece[p[0]] != m for m, p in enumerate(pieces[:n + 1])))

        def piece_view(buf, n):
            return buf[n % NSLOT][:].rearrange("p (t n) -> p t n", t=pieces[n][2])

        splits = [("memT", j) for j in range(KT // 2)] + [("hT", 0, k) for k in range(KT)]
        splits += [("yT", k) for k in range(CT)] + [("hT", 1, k) for k in range(KT)] + [("mo", h) for h in range(MH)]

        wg_v = a["w_gate"][0].rearrange("e (t p) n -> p e t n", p=P)
        wu_v = a["w_up"][0].rearrange("e (t p) n -> p e t n", p=P)
        wd_v = a["w_down"][0].rearrange("e (t p) n -> p e t n", p=P)

        NSEQ = TT * NQ
        MSEQ = TT * 2
        block = ctx.enter_context(nc.Block())

        @block.sync
        def _(sp_):
            def load_piece(n):
                if n >= NSLOT:
                    wait_used(sp_, n - NSLOT)
                sp_.dma_start(piece_view(w_raw, n), pieces[n][3]).then_inc(ring_ld[n % NSLOT], 16)

            sp_.dma_start(cols[:], a["cols"]).then_inc(ld["cols"], 16)
            sp_.dma_start(zemb[:], a["zemb"]).then_inc(ld["zemb"], 16)
            sp_.dma_start(w1[:], a["filt_w1"][0]).then_inc(ld["w12"], 16)
            sp_.dma_start(w2[:], a["filt_w2"][0]).then_inc(ld["w12"], 16)
            x_src = a["x"][0].rearrange("(i p) d -> p i d", p=P)
            for n, m in enumerate((ident, ones, blk, tri)):
                sp_.dma_start(m[:], a["mats"][:, n, :]).then_inc(ld["mats"], 16)
            sp_.dma_start(mem_raw[:], a["mem"][0].rearrange("(j p) d -> p j d", p=P)).then_inc(ld["mem"], 16)
            for n in range(NSLOT):
                load_piece(n)
            for i in range(TT):
                sp_.dma_start(x_in[:, i, :], x_src[:, i, :]).then_inc(ld["x"], 16)
            sp_.dma_start(w3[:], a["filt_w3"][0]).then_inc(ld["w3"], 16)
            sp_.dma_start(decay[:], a["decay"]).then_inc(ld["decay"], 16)
            sp_.dma_start(dft[:], a["dft"]).then_inc(ld["dft"], 16)
            sp_.dma_start(rows[:], a["rows"]).then_inc(ld["rows"], 16)
            sp_.dma_start(rope[:], a["rope"]).then_inc(ld["rope"], 16)
            sp_.dma_start(idft[:], a["idft"]).then_inc(ld["idft"], 16)
            sp_.dma_start(rec_dram, a["rec_init"]).then_inc(ld["rec0"], 16)
            for n in range(NSLOT, len(pieces)):
                load_piece(n)
                if n == last_piece["kv"] + NSLOT:
                    wait_freed(sp_, ("inv", 1, CT - 1))
                    sp_.wait_ge(s_z, 2 * CT)
                    for i in range(TT):
                        sp_.dma_start(x2[:, i, :], x_src[:, i, :]).then_inc(ld["x2"], 16)
            views = [wg_v, wu_v, wd_v]

            def slot_view(s):
                return slot[s][:].rearrange("p (t n) -> p t n", t=(8, 8, 4)[s % 3])

            wait_freed(sp_, ("mk", MT - 1))
            wait_freed(sp_, ("mv", MT - 1))
            wait_freed(sp_, ("mo", MH - 1))
            wait_used(sp_, len(pieces) - 1)
            sp_.dma_start(wr[:], a["w_router"]).then_inc(ld["wr"], 16)
            for s in range(3):
                sp_.dma_start(slot_view(s), views[s][:, 0]).then_inc(w_ld[s], 16)
            wait_freed(sp_, ("router",))
            sp_.wait_ge(s_store, 16 * TT)
            for s in range(3, 6):
                sp_.dma_start(slot_view(s), views[s - 3][:, 1]).then_inc(w_ld[s], 16)
            sp_.wait_ge(s_scat, 16 * 2 * TT)
            sp_.dma_start(rec_sb[:], rec_dram.rearrange("(p b) c -> p b c", p=P)).then_inc(ld["rec"], 16)
            sp_.wait_ge(s_tab, 1)
            nb = sp_.value_load(e_tab[0:1, 31:32], min_val=0, max_val=MAXB - NE) + NE
            with sp_.Fori(2, nb, 2) as b:
                for q in range(2):
                    e = sp_.value_load(e_tab[0:1, bass.ds(b + q, 1)], min_val=0, max_val=NE - 1)
                    for c, used_by in enumerate((s_gate, s_up, s_down)):
                        sp_.wait_ge(used_by, b + q - 1)
                        sp_.sem_inc(waited_sp, 1)
                        s = 3 * q + c
                        sp_.dma_start(slot_view(s), views[c][:, bass.ds(e, 1)].rearrange("p e t n -> p (e t) n"))\
                            .then_inc(w_ld[s], 16)
            sp_.wait_ge(s_down, nb)
            sp_.sem_inc(waited_sp, 1)
            for q in range(2):
                sp_.wait_ge(s_sc[q], nb * 8)
            for i in range(TT):
                for r in range(2):
                    sp_.dma_start(y_back[:, r, i, :], y_dram[r * T + i * P:r * T + (i + 1) * P, :])\
                        .then_inc(ld["back"], 16)
            for i in range(TT):
                sp_.wait_ge(s_fin, 2 * (i + 1))
                sp_.dma_start(out[0, i * P:(i + 1) * P, :], x2[:, i, :]).then_inc(s_out, 16)
            sp_.wait_ge(s_out, 16 * TT)

        @block.gpsimd
        def _(pool):
            steps = [0]

            def link(ins):
                steps[0] += 1
                ins.then_inc(pchain, 1)
                pool.wait_ge(pchain, steps[0])

            def filter_parts(o, t):
                wait_freed(pool, ("filt", o, t, 0))
                wait_freed(pool, ("filt", o, t, 1))
                fwd, bwd = fb[t % 2][:, 0, :], fb[t % 2][:, 1, :]
                pool.tensor_tensor(sum_diff[o][:, 0, t, :], fwd, bwd, ALU.add)
                pool.tensor_tensor(sum_diff[o][:, 1, t, :], fwd, bwd, ALU.subtract).then_inc(s_spdm, 1)

            def spec_parts(o, f):
                pool.wait_ge(s_ke, 2 * o + f + 1)
                for c in range(2):
                    pool.tensor_tensor(spec[:, o, f, c, :], ep[:, c, :], ep[:, 2 + c, :], ALU.add)
                    last = pool.tensor_tensor(spec[:, o, f, 2 + c, :], ep[:, c, :], ep[:, 2 + c, :], ALU.subtract)
                last.then_inc(s_kab, 1)

            for t in range(4):
                filter_parts(0, t)
            for f in range(2):
                spec_parts(0, f)
                filter_parts(1, 2 * f)
                filter_parts(1, 2 * f + 1)
            for f in range(2):
                spec_parts(1, f)
            for o in range(2):
                for f in range(2):
                    n = 2 * o + f
                    for c in range(4):
                        wait_freed(pool, ("fwd", o, f, c))
                    if n:
                        pool.wait_ge(s_ab, n)
                    pool.tensor_tensor(ab[:, 0, :], ep[:, 0, :], ep[:, 2, :], ALU.add)
                    pool.tensor_tensor(ab[:, 1, :], ep[:, 1, :], ep[:, 3, :], ALU.add).then_inc(s_a, 1)
                    pool.wait_ge(s_a, n + 1)
                    pool.wait_ge(s_b, n + 1)
                    kre, kim = spec[:, o, f, 2, :], spec[:, o, f, 3, :]
                    pool.tensor_tensor(ep[:, 1, :], ab[:, 2, :], kre, ALU.mult)
                    pool.tensor_tensor(ep[:, 3, :], ab[:, 3, :], kim, ALU.mult)
                    pool.tensor_tensor(tmp[:, 0, :], ab[:, 2, :], kim, ALU.mult)
                    pool.tensor_tensor(tmp[:, 1, :], ab[:, 3, :], kre, ALU.mult).then_inc(s_pb, 1)
            for i in range(TT):
                pool.wait_ge(s_xn, TT + 3 + i + 1)
                pool.dma_start(xn_dram[i * P:(i + 1) * P, :], xn[:, i, :]).then_inc(s_store, 16)
            pool.wait_ge(ld["rec0"], 16)
            pool.wait_ge(s_slot, 1)
            for r in range(2):
                for i in range(TT):
                    pool.indirect_dma_start(rec_dram, bass.IndirectOffsetOnAxis(ap=slot_i[:, r, i:i + 1], axis=0),
                                            rec[:, r, i, :], None).then_inc(s_scat, 16)
            pool.wait_ge(ld["rec"], 16)
            pool.wait_ge(s_store, 16 * TT)
            pool.wait_ge(s_tab, 1)

            def meta(b, q):
                if not isinstance(b, int) or b >= 2:
                    pool.wait_ge(s_oa, b - 1)
                    pool.wait_ge(s_od, b - 1)
                    pool.wait_ge(s_sc[q], (b - q) * 8)
                pool.tensor_copy(meta_i[:, q, 0:1], rec_sb[:, bass.ds(b, 1), 1:2].rearrange("p b c -> p (b c)"))
                pool.tensor_copy(meta_g[:, q, :], rec_sb[:, bass.ds(b, 1), 2:3].rearrange("p b c -> p (b c)"))\
                    .then_inc(s_meta, 1)

            def gather(b, q):
                if not isinstance(b, int) or b >= 2:
                    pool.wait_ge(s_t, 2 * b - 2)
                pool.tensor_copy(gather_i[:, q, :], rec_sb[:, bass.ds(b, 1), 0:1].rearrange("p b c -> p (b c)"))\
                    .then_inc(s_gi, 1)
                pool.wait_ge(s_gi, b + 1)
                pool.sem_inc(waited_pool, 1)
                pool.indirect_dma_start(hg[q][:], None, xn_dram,
                                        bass.IndirectOffsetOnAxis(ap=gather_i[:, q, :], axis=0)).then_inc(s_gath[q], 16)

            def scatter(b, q):
                pool.wait_ge(s_oa, b + 1)
                pool.wait_ge(s_od, b + 1)
                pool.wait_ge(s_meta, b + 1)
                if not isinstance(b, int) or b >= 1:
                    pool.wait_ge(s_sc[1 - q], (b + q) * 8)
                pool.sem_inc(waited_pool, 1)
                pool.indirect_dma_start(y_dram, bass.IndirectOffsetOnAxis(ap=meta_i[:, q, 0:1], axis=0),
                                        eo[q][:], None).then_inc(s_sc[q], 16)

            gather(0, 0)
            gather(1, 1)
            meta(0, 0)
            gather(2, 0)
            meta(1, 1)
            gather(3, 1)
            scatter(0, 0)
            nb = pool.value_load(e_tab[0:1, 31:32], min_val=0, max_val=MAXB - NE) + NE
            with pool.Fori(2, nb, 2) as b:
                meta(b, 0)
                gather(b + 2, 0)
                scatter(b - 1, 1)
                meta(b + 1, 1)
                gather(b + 3, 1)
                scatter(b, 0)
            scatter(nb - 1, 1)
            for q in range(2):
                pool.wait_ge(s_gath[q], (nb + 2) * 8)

        @block.scalar
        def _(act):
            steps = [0]

            def link(ins):
                steps[0] += 1
                ins.then_inc(achain, 1)
                act.wait_ge(achain, steps[0])

            def sine(j, dst):
                act.wait_ge(s_arg, j + 1)
                act.activation(dst[:], mlp_arg[:], ACT.Sin).then_inc(s_sin, 1)

            fb_flat = at("junk", 192, [P, D])[:]

            eps = small[:, 395:396]

            def rms(src, first, n, count):
                for i in range(n):
                    act.activation(fb_flat, src[:, i, :], ACT.Square, accum_out=small[:, first + i:first + i + 1])\
                        .then_inc(s_sq, 1)
                    act.wait_ge(s_sq, count - n + i + 1)
                act.activation(small[:, 16 + first:16 + first + n], small[:, first:first + n], ACT.Sqrt,
                               bias=eps, scale=1.0 / D).then_inc(s_rms, 1)

            act.wait_ge(ld["cols"], 16)
            link(act.activation(eps, col("token"), ACT.Copy, scale=0.0, bias=EPS))
            def abs_pair(o, t):
                wait_freed(act, ("filt", o, t, 0))
                wait_freed(act, ("filt", o, t, 1))
                if 4 * o + t >= 2:
                    act.wait_ge(s_l1, 4 * o + t - 1)
                act.activation(fabs[t % 2][:], fb[t % 2][:], ACT.Abs).then_inc(s_abs, 1)

            def head_rms(first, n, width, count):
                act.wait_ge(s_ms, count)
                act.activation(small[:, first:first + n], small[:, first:first + n], ACT.Sqrt, bias=eps,
                               scale=1.0 / width).then_inc(s_hrms, 1)

            def weight_hi(lo, n):
                for m in range(lo, lo + n):
                    act.wait_ge(ring_ld[m % NSLOT], 16 * (m // NSLOT + 1))
                    if m >= NSLOT:
                        wait_used(act, m - NSLOT)
                    act.activation(w_hi[m % NSLOT][:], w_raw[m % NSLOT][:], ACT.Copy).then_inc(s_wh, 1)

            def split_hi(job, dst, scale=1.0):
                wait_filled(act, job)
                act.activation(dst, bank(job)[:], ACT.Copy, scale=scale).then_inc(s_hi, 1)

            def centre_tap(lo):
                for c in range(lo, lo + 4):
                    job = ("u", c)
                    wait_filled(act, job)
                    act.activation(u[:, c, :].rearrange("p (two m) -> p two m", two=2),
                                   bank(job)[:].rearrange("p (m two) -> p two m", two=2), ACT.Identity,
                                   bias=col("short_b", c), scale=col("short_w", 12 + c)).then_inc(s_conv, 1)

            def evac(key, n, dst, scale=None):
                for j in range(n):
                    wait_filled(act, (key, j))
                    out_ = dst(j)
                    by = 1.0 if scale is None else small[:, scale + j:scale + j + 1]
                    free(act.activation(out_, bank((key, j))[:, 0:out_.shape[1]], ACT.Copy, scale=by), (key, j))

            def evac_z(o):
                for k in range(4):
                    job = ("zT", o, k)
                    wait_filled(act, job)
                    if o == 0 and k == 0:
                        wait_freed(act, ("filt", 1, 3, 1))
                    if o == 1 and k == 0:
                        wait_filled(act, ("fwd", 0, 1, 3))
                    free(act.activation(zt[:, k, :], bank(job)[:], ACT.Copy), job)

            def evac_fwd(o):
                for f in range(2):
                    for c in range(4):
                        job = ("fwd", o, f, c)
                        wait_filled(act, job)
                        if c == 0:
                            if o == 0 and f == 0:
                                act.wait_ge(s_kab, 4)
                            else:
                                act.wait_ge(s_ab, 2 * o + f)
                        free(act.activation(ep[:, c, :], bank(job)[:], ACT.Copy), job)

            for j in range(KT // 2):
                job = ("memT", j)
                wait_filled(act, job)
                for c in range(2):
                    k = 2 * j + c
                    ins = act.activation(memT_hi[:, k, :], bank(job)[:, c * NM:(c + 1) * NM], ACT.Copy, scale=col("norm_mem", k))
                ins.then_inc(s_hi, 1)
            sine(0, a1)
            weight_hi(0, 3)
            act.wait_ge(ld["x"], 16 * TT)
            rms(x_in, 4, TT, TT)
            act.wait_ge(ld["mem"], 16)
            rms(mem_raw, 0, MT, TT + MT)
            sine(1, a2)
            weight_hi(3, 1)
            for k in range(4):
                split_hi(("hT", 0, k), hT_hi[:, k, :], col("norm_mix", k))
            act.wait_ge(s_xn, TT + 1)
            evac("mk", MT, lambda j: mk[:, j, :], 16)
            for k in range(4, KT):
                split_hi(("hT", 0, k), hT_hi[:, k, :], col("norm_mix", k))
            weight_hi(4, 3)
            abs_pair(0, 0)
            abs_pair(0, 1)
            weight_hi(7, 1)
            abs_pair(0, 2)
            abs_pair(0, 3)
            evac("mv", MT, lambda j: mv[:, j, :], 16)
            weight_hi(8, 3)
            abs_pair(1, 0)
            abs_pair(1, 1)
            abs_pair(1, 2)
            weight_hi(11, 1)
            abs_pair(1, 3)
            weight_hi(12, 2)
            centre_tap(0)
            weight_hi(14, 1)
            evac_z(0)
            weight_hi(15, 2)
            act.wait_ge(ld["rows"], 16)
            act.activation(row("gq"), row("gq"), ACT.Copy, scale=HD ** -0.5).then_inc(s_gq, 1)
            weight_hi(17, 1)
            centre_tap(4)
            weight_hi(18, 1)

            evac_fwd(0)
            weight_hi(19, 3)
            centre_tap(8)
            weight_hi(22, 1)
            evac_z(1)
            evac_fwd(1)
            head_rms(40, MT * MH, MHD, 1)
            weight_hi(23, 3)
            for i in range(TT):
                job = ("q", i)
                wait_filled(act, job)
                if i == 0:
                    wait_filled(act, ("fwd", 1, 1, 3))
                act.activation(q_sq[:, i, :], bank(job)[:], ACT.Square).then_inc(s_qsq, 1)
                free(act.activation(qkv[:, i, 0:512], bank(job)[:], ACT.Copy), job)
            weight_hi(26, 1)
            evac("kv", TT, lambda i: qkv[:, i, 512:768])
            weight_hi(27, 1)
            head_rms(230, TT * NKV, HD, 2)
            head_rms(240, TT * NQ, HD, 3)
            weight_hi(28, 1)
            act.wait_ge(s_rope, 4)
            for w in range(2):
                ins = act.activation(kdup[:, :, :, w, :], qkv[:, :, 512:640].rearrange("p i (g d) -> p i g d", d=HD), ACT.Copy)
            ins.then_inc(s_kdup, 1)
            for j in range(2):
                wait_filled(act, ("mkT", j))
                free(act.activation(mkT[:, 2 * j:2 * j + 2, :].rearrange("p h m -> p (h m)"), bank(("mkT", j))[:], ACT.Copy),
                     ("mkT", j))
            for c in range(CT):
                act.wait_ge(s_z, CT + c + 1)
                act.activation(y_sq[:, c, :], u[:, c, :], ACT.Square).then_inc(s_ysq, 1)
            for p in range(NQ // 2):
                wait_filled(act, ("qT", p))
                free(act.activation(qT[:, p, :], bank(("qT", p))[:], ACT.Copy), ("qT", p))
            for g in range(NKV):
                wait_filled(act, ("kT", g))
                free(act.activation(kT[:, g, :], bank(("kT", g))[:], ACT.Copy), ("kT", g))

            for c in range(CT):
                job = ("hn", c)
                wait_filled(act, job)
                free(act.activation(y_rs[:, c, :], bank(job)[:], ACT.Identity, bias=eps, scale=1.0 / HD), job)

            def hyena_roots():
                for c in range(CT):
                    wait_freed(act, ("hn", c))
                act.activation(y_rs[:], y_rs[:], ACT.Sqrt).then_inc(s_hroot, 1)

            def gqa_exp(s):
                act.wait_ge(s_max, s + 1)
                if s >= NPR:
                    wait_filled(act, ("PT", s - NPR))
                c0 = 240 + s
                free(act.activation(pr[:, s % NPR, :], bank(("S", s))[:], ACT.Exp, bias=small[:, 100 + s:101 + s],
                                    scale=small[:, c0:c0 + 1],
                                    accum_out=small[:, 140 + s:141 + s]), ("S", s))

            def gqa_pt(s):
                wait_filled(act, ("PT", s))
                if s >= NPR:
                    act.wait_ge(s_asq, s - NPR + 1)
                free(act.activation(pT[:, s % NPR, :], bank(("PT", s))[:], ACT.Copy), ("PT", s))

            for s in range(AHEAD):
                gqa_exp(s)
            for s in range(NSEQ):
                gqa_pt(s)
                if s + AHEAD < NSEQ:
                    gqa_exp(s + AHEAD)
                if s == HN_STEP + 1:
                    hyena_roots()
            head_rms(340, TT * NQ, HD, 4)
            for k in range(CT):
                split_hi(("yT", k), yT_hi[:, CT + k, :], col("attn_norm", k))
            weight_hi(29, 6)

            def x_norm_squares(first, jobkey, count):
                for i in range(TT):
                    wait_freed(act, (jobkey, 0, i))
                    wait_freed(act, (jobkey, 1, i))
                    act.activation(fb_flat, x2[:, i, :], ACT.Square, accum_out=small[:, first + i:first + i + 1])\
                        .then_inc(s_sq, 1)
                    act.wait_ge(s_sq, count + i + 1)
                    act.activation(small[:, 16 + first + i:17 + first + i], small[:, first + i:first + i + 1], ACT.Sqrt,
                                   bias=eps, scale=1.0 / D).then_inc(s_rms, 1)

            weight_hi(35, 2)
            for k in range(KT):
                split_hi(("hT", 1, k), hT_hi[:, k, :], col("norm_xattn", k))
            x_norm_squares(8, "wout", 6)
            weight_hi(37, 3)
            act.wait_ge(s_xn, TT + 2)
            evac("mq", TT, lambda i: mq[:, i, :], 24)
            weight_hi(40, 1)
            for h in range(MH):
                wait_filled(act, ("mqT", h))
                free(act.activation(mqT[:, h, :], bank(("mqT", h))[:], ACT.Copy, scale=col("gmq")), ("mqT", h))

            head_rms(40, TT * MH, MHD, 5)
            act.wait_ge(s_mqn, 1)

            def mem_exp(s):
                i, hp = s // 2, s % 2
                act.wait_ge(s_max, NSEQ + s + 1)
                if s >= NPR:
                    wait_filled(act, ("MPT", s - NPR))
                for c in range(2):
                    ins = act.activation(pr[:, s % NPR, c * NM:(c + 1) * NM], bank(("MS", s))[:, c * NM:(c + 1) * NM], ACT.Exp,
                                         bias=small[:, 180 + 2 * s + c:181 + 2 * s + c],
                                         scale=small[:, 40 + MH * i + 2 * hp + c:41 + MH * i + 2 * hp + c],
                                         accum_out=small[:, 200 + 2 * s + c:201 + 2 * s + c])
                free(ins, ("MS", s))

            def mem_pt(s):
                i, hp = s // 2, s % 2
                job = ("MPT", s)
                wait_filled(act, job)
                free(act.activation(mpT[:, 2 * hp:2 * hp + 2, :, i * P:(i + 1) * P],
                                    bank(job)[:].rearrange("p (h t n) -> p h t n", h=2, t=MT), ACT.Copy), job)

            for s in range(MAHEAD):
                mem_exp(s)
            for s in range(MSEQ):
                mem_pt(s)
                if s + MAHEAD < MSEQ:
                    mem_exp(s + MAHEAD)
            for h in range(MH):
                split_hi(("mo", h), moT_hi[:, h, :])
            weight_hi(41, 1)
            for k in range(0, KT, 2):
                wait_filled(act, ("hT", 2, k))
                free(act.activation(hT[:, k, :], bank(("hT", 2, k))[:], ACT.Copy, scale=col("norm_moe", k)), ("hT", 2, k))
            x_norm_squares(12, "wom", 10)
            act.wait_ge(s_r1, 1)
            act.activation(rt[:, 100:116], rt[:, 84:100], ACT.Exp).then_inc(s_r2, 1)
            act.wait_ge(s_r3, 1)
            act.activation(rt[:, 204:208], rt[:, 200:204], ACT.Exp).then_inc(s_r4, 1)

            def rows_evac(b, q):
                act.wait_ge(s_t, 2 * b + 1)
                if not isinstance(b, int) or b >= 2:
                    act.wait_ge(s_up, b - 1)
                for k in range(4):
                    ins = act.activation(hgT[q][:, k, :], banks[0][:, k * P:(k + 1) * P], ACT.Copy, scale=col("norm_moe", k))
                ins.then_inc(s_ta, 1)

            def silu(b, q):
                act.wait_ge(s_gate, b + 1)
                if not isinstance(b, int) or b >= 2:
                    act.wait_ge(s_mul, b - 1)
                act.activation(sg[q][:], banks[2][:], ACT.Silu).then_inc(s_silu, 1)

            def actT_evac(b, q):
                act.wait_ge(s_at, b + 1)
                if not isinstance(b, int) or b >= 2:
                    act.wait_ge(s_down, b - 1)
                act.activation(gaT[q][:].rearrange("p k n -> p (k n)"), banks[4][:], ACT.Copy).then_inc(s_ate, 1)

            def out_evac(b, q):
                act.wait_ge(s_down0, b + 1)
                act.wait_ge(s_meta, b + 1)
                act.activation(eo[q][:, 0:512], banks[5][:], ACT.Copy, scale=meta_g[:, q, :]).then_inc(s_oa, 1)

            rows_evac(0, 0)
            silu(0, 0)
            rows_evac(1, 1)
            actT_evac(0, 0)
            silu(1, 1)
            rows_evac(2, 0)
            out_evac(0, 0)
            actT_evac(1, 1)
            act.wait_ge(s_tab, 1)
            nb = act.value_load(e_tab[0:1, 31:32], min_val=0, max_val=MAXB - NE) + NE
            with act.Fori(2, nb, 2) as b:
                silu(b, 0)
                rows_evac(b + 1, 1)
                out_evac(b - 1, 1)
                actT_evac(b, 0)
                silu(b + 1, 1)
                rows_evac(b + 2, 0)
                out_evac(b, 0)
                actT_evac(b + 1, 1)
            out_evac(nb - 1, 1)

        @block.vector
        def _(dve):
            steps = [0]

            def link(ins):
                steps[0] += 1
                ins.then_inc(dchain, 1)
                dve.wait_ge(dchain, steps[0])

            def range_reduce(j):
                job = ("mlp", j)
                wait_filled(dve, job)
                if j:
                    dve.wait_ge(s_sin, 1)
                link(dve.tensor_scalar(mlp_arg[:], bank(job)[0:FF, :], col("b1" if j == 0 else "b2", 0, FF),
                                       col("freq", j, FF), ALU.add, ALU.mult))
                link(dve.tensor_scalar(mlp_k[:], mlp_arg[:], 1.0 / (2 * np.pi), 12582912.0, ALU.mult, ALU.add))
                link(dve.tensor_scalar(mlp_k[:], mlp_k[:], 12582912.0, None, ALU.subtract))
                hi = 6.28125
                link(dve.scalar_tensor_tensor(mlp_arg[:], mlp_k[:], -hi, mlp_arg[:], ALU.mult, ALU.add))
                link(dve.scalar_tensor_tensor(mlp_arg[:], mlp_k[:], -(2 * np.pi - hi), mlp_arg[:], ALU.mult, ALU.add))
                dve.tensor_scalar(mlp_arg[:], mlp_arg[:], float(np.float32(-3.1415925)), float(np.float32(3.1415925)),
                                  ALU.max, ALU.min).then_inc(s_arg, 1)

            dve.wait_ge(ld["cols"], 16)
            def weight_lo(lo, n):
                for m in range(lo, lo + n):
                    dve.wait_ge(s_wh, m + 1)
                    slot_ = m % NSLOT
                    dve.tensor_tensor(w_lo[slot_][:], w_raw[slot_][:], w_hi[slot_][:].bitcast(F32), ALU.subtract)\
                        .then_inc(s_wl, 1)

            def split_lo(job, dst, hi, scale):
                dve.wait_ge(s_hi, splits.index(job) + 1)
                free(dve.scalar_tensor_tensor(dst, bank(job)[:], scale, hi.bitcast(F32), ALU.mult, ALU.subtract), job)

            range_reduce(0)
            dve.wait_ge(s_arg, 1)
            free(dve.tensor_copy(small[0:1, 399:400], cols[0:1, 0:1]), ("mlp", 0))
            for j in range(KT // 2):
                job = ("memT", j)
                dve.wait_ge(s_hi, splits.index(job) + 1)
                for c in range(2):
                    k = 2 * j + c
                    ins = dve.scalar_tensor_tensor(memT_lo[:, k, :], bank(job)[:, c * NM:(c + 1) * NM], col("norm_mem", k),
                                                   memT_hi[:, k, :].bitcast(F32), ALU.mult, ALU.subtract)
                free(ins, job)
            weight_lo(0, 3)
            range_reduce(1)
            dve.wait_ge(s_rms, 1)
            link(dve.reciprocal(small[:, 20:24], small[:, 20:24]))
            for i in range(TT):
                dve.tensor_scalar(x_in[:, i, :], x_in[:, i, :], small[:, 20 + i:21 + i], None, ALU.mult).then_inc(s_xn, 1)
            dve.wait_ge(s_rms, 2)
            dve.reciprocal(small[:, 16:18], small[:, 16:18]).then_inc(s_xn, 1)
            dve.wait_ge(s_arg, 2)
            free(dve.tensor_copy(small[0:1, 399:400], cols[0:1, 0:1]), ("mlp", 1))
            weight_lo(3, 1)
            for k in range(KT):
                split_lo(("hT", 0, k), hT_lo[:, k, :], hT_hi[:, k, :], col("norm_mix", k))
            weight_lo(4, 3)
            dve.wait_ge(ld["decay"], 16)

            def filters(o, t):
                fwd, bwd = ("filt", o, t, 0), ("filt", o, t, 1)
                if 4 * o + t >= 2:
                    dve.wait_ge(s_spdm, 4 * o + t - 1)
                    dve.wait_ge(s_abs, 4 * o + t - 1)
                if o == 0 and t == 1:
                    dve.wait_ge(s_hi, KT // 2)
                wait_filled(dve, fwd)
                free(dve.tensor_tensor(fb[t % 2][:, 0, :], bank(fwd)[:], decay[:, t, :], ALU.mult), fwd)
                wait_filled(dve, bwd)
                mask = col("not_first") if t == 0 else 1.0
                free(dve.scalar_tensor_tensor(fb[t % 2][:, 1, :], bank(bwd)[:], mask, decay[:, t, :], ALU.mult, ALU.mult), bwd)

            def l1_add(o, t):
                dve.wait_ge(s_abs, 4 * o + t + 1)
                fwd, bwd = fabs[t % 2][:, 0, :], fabs[t % 2][:, 1, :]
                if t == 0:
                    if o == 1:
                        wait_filled(dve, ("l1", 0))
                    dve.tensor_tensor(l1sum[:], fwd, bwd, ALU.add).then_inc(s_l1, 1)
                else:
                    link(dve.tensor_tensor(l1sum[:], l1sum[:], fwd, ALU.add))
                    dve.tensor_tensor(l1sum[:], l1sum[:], bwd, ALU.add).then_inc(s_l1, 1)
                dve.wait_ge(s_l1, 4 * o + t + 1)

            def l1_norm(o):
                wait_filled(dve, ("l1", o))
                if o == 1:
                    dve.wait_ge(s_ke, 2)
                free(dve.tensor_scalar(rnorm[:], bank(("l1", o))[:], EPS, None, ALU.add), ("l1", o))
                wait_freed(dve, ("l1", o))
                dve.reciprocal(rnorm[:], rnorm[:]).then_inc(s_rn, 1)
                dve.wait_ge(s_rn, o + 1)

            def normed_spec(o, f):
                if 2 * o + f:
                    dve.wait_ge(s_kab, 2 * o + f)
                for c in range(4):
                    job = ("spec", o, f, c)
                    wait_filled(dve, job)
                    free(dve.tensor_tensor(ep[:, c, :], bank(job)[:], rnorm[:], ALU.mult), job)
                wait_freed(dve, ("spec", o, f, 3))
                dve.tensor_copy(small[0:1, 398:399], cols[0:1, 0:1]).then_inc(s_ke, 1)

            def outer_taps(lo):
                for c in range(lo, lo + 4):
                    job = ("u", c)
                    dve.wait_ge(s_conv, c + 1)
                    pe_, po = bank(job)[:, 0::2], bank(job)[:, 1::2]
                    ue, uo = u[:, c, 0:HALF], u[:, c, HALF:T]
                    w_prev, w_next = col("short_w", c), col("short_w", 24 + c)
                    dve.scalar_tensor_tensor(ue, po, w_next, ue, ALU.mult, ALU.add)
                    link(dve.scalar_tensor_tensor(uo, pe_, w_prev, uo, ALU.mult, ALU.add))
                    dve.scalar_tensor_tensor(ue[:, 1:HALF], po[:, 0:HALF - 1], w_prev, ue[:, 1:HALF], ALU.mult, ALU.add)
                    free(dve.scalar_tensor_tensor(uo[:, 0:HALF - 1], pe_[:, 1:HALF], w_next, uo[:, 0:HALF - 1],
                                                  ALU.mult, ALU.add), job)

            filters(0, 0)
            filters(0, 1)
            for t in range(4):
                l1_add(0, t)
                if t < 2:
                    filters(0, t + 2)
                if t == 1:
                    weight_lo(7, 1)
            l1_norm(0)
            weight_lo(8, 3)
            normed_spec(0, 0)
            filters(1, 0)
            filters(1, 1)
            l1_add(1, 0)
            normed_spec(0, 1)
            filters(1, 2)
            l1_add(1, 1)
            weight_lo(11, 1)
            filters(1, 3)
            l1_add(1, 2)
            l1_add(1, 3)
            weight_lo(12, 2)
            l1_norm(1)
            outer_taps(0)
            weight_lo(14, 1)
            normed_spec(1, 0)
            normed_spec(1, 1)
            weight_lo(15, 3)

            def head_sums(x3, sq3, ss):
                link(dve.tensor_tensor(sq3, x3, x3, ALU.mult))
                return dve.tensor_reduce(ss, sq3, AX.X, ALU.add)

            for j in range(MT):
                wait_freed(dve, ("mk", j))
                ins = head_sums(mk[:, j, :].rearrange("p (h d) -> p h d", d=MHD),
                                rope_tmp[:, 0:512].rearrange("p (h d) -> p h d", d=MHD), small[:, 40 + MH * j:44 + MH * j])
                if j < MT - 1:
                    link(ins)
            ins.then_inc(s_ms, 1)
            outer_taps(4)
            weight_lo(18, 1)

            def pointwise(o, f):
                n = 2 * o + f
                for c in range(4):
                    wait_freed(dve, ("fwd", o, f, c))
                if n == 0:
                    dve.wait_ge(s_kab, 4)
                if o == 1 and f == 0:
                    wait_filled(dve, ("inv", 0, CT - 1))
                dve.tensor_tensor(ab[:, 2, :], ep[:, 0, :], ep[:, 2, :], ALU.subtract)
                dve.tensor_tensor(ab[:, 3, :], ep[:, 1, :], ep[:, 3, :], ALU.subtract).then_inc(s_b, 1)
                dve.wait_ge(s_a, n + 1)
                kre, kim = spec[:, o, f, 0, :], spec[:, o, f, 1, :]
                are, aim = ab[:, 0, :], ab[:, 1, :]
                s_ = sd[:, f]
                dve.wait_ge(s_b, n + 1)
                dve.tensor_tensor(s_[:, 0, :], are, kre, ALU.mult)
                dve.tensor_tensor(s_[:, 1, :], aim, kim, ALU.mult)
                dve.tensor_tensor(s_[:, 2, :], are, kim, ALU.mult)
                link(dve.tensor_tensor(s_[:, 3, :], aim, kre, ALU.mult))
                dve.tensor_tensor(ep[:, 0, :], s_[:, 0, :], s_[:, 1, :], ALU.subtract)
                link(dve.tensor_tensor(ep[:, 2, :], s_[:, 2, :], s_[:, 3, :], ALU.add))
                dve.wait_ge(s_pb, n + 1)
                dve.tensor_tensor(ab[:, 0, :], ep[:, 1, :], ep[:, 3, :], ALU.subtract)
                link(dve.tensor_tensor(ab[:, 1, :], tmp[:, 0, :], tmp[:, 1, :], ALU.add))
                dve.tensor_tensor(s_[:, 0, :], ep[:, 0, :], ab[:, 0, :], ALU.add)
                dve.tensor_tensor(s_[:, 2, :], ep[:, 0, :], ab[:, 0, :], ALU.subtract)
                dve.tensor_tensor(s_[:, 1, :], ep[:, 2, :], ab[:, 1, :], ALU.add)
                dve.tensor_tensor(s_[:, 3, :], ep[:, 2, :], ab[:, 1, :], ALU.subtract).then_inc(s_ab, 1)

            def gated(o):
                for c in range(CT):
                    job = ("inv", o, c)
                    wait_filled(dve, job)
                    free(dve.scalar_tensor_tensor(u[:, c, :], u[:, c, :], col("skip", o * CT + c), bank(job)[:],
                                                  ALU.mult, ALU.add), job)
                    wait_freed(dve, job)
                    dve.tensor_tensor(u[:, c, :], u[:, c, :], u[:, CT * (o + 1) + c, :], ALU.mult).then_inc(s_z, 1)

            def qk(i):
                return qkv[:, i, 0:640].rearrange("p (h d) -> p h d", d=HD)

            def roped(i, keys_done):
                x3 = qk(i)[:, 0:NQ, :]
                t3 = rope_tmp[:, 0:NQ * HD].rearrange("p (h d) -> p h d", d=HD)
                link(dve.tensor_tensor(x3, x3, row("gq").unsqueeze(1).to_broadcast([P, NQ, HD]), ALU.mult))
                x5 = qkv[:, i, 0:NQ * HD].rearrange("p (h s w d) -> p h s w d", s=2, w=2, d=HD // 4)
                t5 = rope_tmp[:, 0:NQ * HD].rearrange("p (h s w d) -> p h s w d", s=2, w=2, d=HD // 4)
                sn = rope[:, 1, i, :].rearrange("p (s w d) -> p s w d", s=2, w=2)
                for w in range(2):
                    for s in range(2):
                        ins = dve.tensor_tensor(t5[:, :, s, w, :], x5[:, :, s, 1 - w, :],
                                                sn[:, s, w, :].unsqueeze(1).to_broadcast([P, NQ, HD // 4]), ALU.mult)
                link(ins)
                link(dve.tensor_tensor(x3, x3, rope[:, 0, i, :].unsqueeze(1).to_broadcast([P, NQ, HD]), ALU.mult))
                dve.tensor_tensor(x3, x3, t3, ALU.add).then_inc(s_rope, 1)
                dve.wait_ge(s_rope, i + 1 + keys_done)

            pointwise(0, 0)
            weight_lo(19, 1)
            pointwise(0, 1)
            weight_lo(20, 2)
            outer_taps(8)
            gated(0)
            weight_lo(22, 1)
            pointwise(1, 0)
            weight_lo(23, 1)
            pointwise(1, 1)
            weight_lo(24, 1)
            dve.wait_ge(ld["rows"], 16)
            dve.wait_ge(ld["rope"], 16)
            dve.wait_ge(s_gq, 1)
            dve.wait_ge(s_hrms, 1)
            link(dve.reciprocal(small[:, 40:48], small[:, 40:48]))
            for j in range(MT):
                x3 = mk[:, j, :].rearrange("p (h d) -> p h d", d=MHD)
                link(dve.tensor_tensor(x3, x3, small[:, 40 + MH * j:44 + MH * j].unsqueeze(2).to_broadcast([P, MH, MHD]), ALU.mult))
                dve.tensor_tensor(x3, x3, row("gmk").unsqueeze(1).to_broadcast([P, MH, MHD]), ALU.mult).then_inc(s_mkn, 1)
            weight_lo(25, 1)
            dve.wait_ge(s_ms, 1)

            def keys_roped():
                x4 = qkv[:, :, NQ * HD:(NQ + NKV) * HD].rearrange("p i (h d) -> p i h d", d=HD)
                x6 = qkv[:, :, NQ * HD:(NQ + NKV) * HD].rearrange("p i (h s w d) -> p i h s w d", s=2, w=2, d=HD // 4)
                t4 = rope_tmp[:, 0:512].rearrange("p (i h d) -> p i h d", i=TT, d=HD)
                t6 = rope_tmp[:, 0:512].rearrange("p (i h s w d) -> p i h s w d", i=TT, s=2, w=2, d=HD // 4)
                cs = rope[:, 0, :, :]
                sn = rope[:, 1, :, :].rearrange("p i (s w d) -> p i s w d", s=2, w=2)
                inv = small[:, 230:238].rearrange("p (i h) -> p i h", i=TT)
                link(dve.tensor_tensor(x4, x4, inv.unsqueeze(3).to_broadcast([P, TT, NKV, HD]), ALU.mult))
                link(dve.tensor_tensor(x4, x4, row("gk").unsqueeze(1).unsqueeze(1).to_broadcast([P, TT, NKV, HD]), ALU.mult))
                for w in range(2):
                    for s in range(2):
                        ins = dve.tensor_tensor(t6[:, :, :, s, w, :], x6[:, :, :, s, 1 - w, :],
                                                sn[:, :, s, w, :].unsqueeze(2).to_broadcast([P, TT, NKV, HD // 4]), ALU.mult)
                link(ins)
                link(dve.tensor_tensor(x4, x4, cs.unsqueeze(2).to_broadcast([P, TT, NKV, HD]), ALU.mult))
                dve.tensor_tensor(x4, x4, t4, ALU.add).then_inc(s_rope, 1)
                dve.wait_ge(s_rope, 4)

            dve.wait_ge(s_qsq, TT)
            for i in range(TT):
                wait_freed(dve, ("q", i))
            link(dve.tensor_reduce(small[:, 240:272], q_sq[:].rearrange("p i (h d) -> p (i h) d", d=HD), AX.X, ALU.add))
            weight_lo(26, 1)
            roped(0, 0)
            roped(1, 0)
            for i in range(TT):
                wait_freed(dve, ("kv", i))
            keys = qkv[:, :, NQ * HD:(NQ + NKV) * HD].rearrange("p i (h d) -> p i h d", d=HD)
            sq = rope_tmp[:, 0:512].rearrange("p (i h d) -> p i h d", i=TT, d=HD)
            link(dve.tensor_tensor(sq, keys, keys, ALU.mult))
            dve.tensor_reduce(small[:, 230:238], rope_tmp[:, 0:512].rearrange("p (h d) -> p h d", d=HD), AX.X, ALU.add)\
                .then_inc(s_ms, 1)
            dve.wait_ge(s_ms, 2)
            weight_lo(27, 1)
            roped(2, 0)
            dve.tensor_copy(small[0:1, 396:397], small[0:1, 240:241]).then_inc(s_ms, 1)
            dve.wait_ge(s_hrms, 2)
            link(dve.reciprocal(small[:, 230:238], small[:, 230:238]))
            keys_roped()
            roped(3, 1)
            dve.wait_ge(s_hrms, 3)
            dve.reciprocal(small[:, 240:272], small[:, 240:272]).then_inc(s_qinv, 1)
            gated(1)
            weight_lo(28, 1)
            def hyena_recip(n):
                c, piece = n // 4, y_rs[:, n // 4, (n % 4) * P:(n % 4 + 1) * P]
                if n == 0:
                    dve.wait_ge(s_hroot, 1)
                link(dve.reciprocal(piece, piece))

            def hyena_norm(c):
                src = u[:, c, :].rearrange("p (two m) -> p two m", two=2)
                rs = y_rs[:, c, :].rearrange("p (two m) -> p two m", two=2)
                link(dve.scalar_tensor_tensor(src, src, col("hyena_norm", c), rs, ALU.mult, ALU.mult))
                in_time = u[:, c, :].rearrange("p (two m) -> p m two", two=2)

                def pairs(ap):
                    return ap.rearrange("p (m two) -> p m two", two=2)

                link(dve.tensor_copy(pairs(yT_hi[:, c, :]), in_time))
                dve.tensor_tensor(pairs(yT_lo[:, c, :]), in_time, pairs(yT_hi[:, c, :].bitcast(F32)), ALU.subtract)\
                    .then_inc(s_yh, 1)

            def gqa_max(s):
                wait_filled(dve, ("S", s))
                c0 = 240 + s
                top = small[:, 100 + s:101 + s]
                link(dve.tensor_reduce(top, bank(("S", s))[:], AX.X, ALU.max, negate=True))
                dve.tensor_tensor(top, top, small[:, c0:c0 + 1], ALU.mult).then_inc(s_max, 1)

            def att_out(i):
                job = ("O", i)
                for h in range(NQ):
                    wait_freed(dve, ("S", i * NQ + h))
                link(dve.reciprocal(small[:, 50:58], small[:, 140 + i * NQ:148 + i * NQ]))
                dve.wait_ge(s_asq, (i + 1) * NQ)
                o3 = att[:, i, :].rearrange("p (h d) -> p h d", d=HD)
                free(dve.tensor_tensor(o3, bank(job)[:].rearrange("p (h d) -> p h d", d=HD),
                                       small[:, 50:58].unsqueeze(2).to_broadcast([P, NQ, HD]), ALU.mult), job)
                wait_freed(dve, job)
                ins = head_sums(o3, att_sq[:].rearrange("p (h d) -> p h d", d=HD), small[:, 340 + NQ * i:340 + NQ * (i + 1)])
                if i < TT - 1:
                    link(ins)
                else:
                    ins.then_inc(s_ms, 1)

            dve.wait_ge(s_qinv, 1)
            for s in range(AHEAD + 1):
                gqa_max(s)
            for s in range(NSEQ):
                if s + AHEAD + 1 < NSEQ:
                    gqa_max(s + AHEAD + 1)
                if s % NQ == 3 and s > NQ:
                    att_out(s // NQ - 1)
                n = s - HN_STEP - 3
                if 0 <= n < 4 * CT:
                    hyena_recip(n)
                    if n % 4 == 3:
                        hyena_norm(n // 4)
            att_out(TT - 1)
            dve.wait_ge(s_hrms, 4)
            link(dve.reciprocal(small[:, 340:372], small[:, 340:372]))
            for i in range(TT):
                o3 = att[:, i, :].rearrange("p (h d) -> p h d", d=HD)
                dve.tensor_tensor(o3, o3, small[:, 340 + NQ * i:340 + NQ * (i + 1)].unsqueeze(2).to_broadcast([P, NQ, HD]),
                                  ALU.mult).then_inc(s_att, 1)

            def residual(jobkey, h):
                for i in range(TT):
                    job = (jobkey, h, i)
                    wait_filled(dve, job)
                    xs = x2[:, i, h * 512:(h + 1) * 512]
                    free(dve.tensor_tensor(xs, xs, bank(job)[:], ALU.add), job)

            dve.wait_ge(ld["x2"], 16 * TT)
            for k in range(CT):
                split_lo(("yT", k), yT_lo[:, CT + k, :], yT_hi[:, CT + k, :], col("attn_norm", k))
            weight_lo(29, 3)
            residual("wout", 0)
            weight_lo(32, 4)
            residual("wout", 1)
            weight_lo(36, 1)
            for k in range(KT):
                split_lo(("hT", 1, k), hT_lo[:, k, :], hT_hi[:, k, :], col("norm_xattn", k))
            dve.wait_ge(s_rms, 2 + TT)
            dve.reciprocal(small[:, 24:28], small[:, 24:28]).then_inc(s_xn, 1)
            weight_lo(37, 3)
            for i in range(TT):
                wait_freed(dve, ("mq", i))
                ins = head_sums(mq[:, i, :].rearrange("p (h d) -> p h d", d=MHD),
                                att_sq[:].rearrange("p (h d) -> p h d", d=MHD), small[:, 40 + MH * i:44 + MH * i])
                if i < TT - 1:
                    link(ins)
            ins.then_inc(s_ms, 1)
            weight_lo(40, 1)
            dve.wait_ge(s_hrms, 5)
            link(dve.reciprocal(small[:, 40:56], small[:, 40:56]))
            link(dve.tensor_scalar(small[:, 40:56], small[:, 40:56], MHD ** -0.5, None, ALU.mult))
            dve.tensor_copy(small[0:1, 397:398], small[0:1, 40:41]).then_inc(s_mqn, 1)

            def mem_max(s):
                wait_filled(dve, ("MS", s))
                c0 = 40 + MH * (s // 2) + 2 * (s % 2)
                top = small[:, 180 + 2 * s:182 + 2 * s]
                link(dve.tensor_reduce(top, bank(("MS", s))[:].rearrange("p (h m) -> p h m", h=2), AX.X, ALU.max, negate=True))
                dve.tensor_tensor(top, top, small[:, c0:c0 + 2], ALU.mult).then_inc(s_max, 1)

            def mem_probs(s):
                wait_freed(dve, ("MS", s))
                if s:
                    dve.wait_ge(s_mnorm, s)
                link(dve.reciprocal(small[:, 224:226], small[:, 200 + 2 * s:202 + 2 * s]))
                for c in range(2):
                    ins = dve.tensor_scalar(pr[:, s % NPR, c * NM:(c + 1) * NM], pr[:, s % NPR, c * NM:(c + 1) * NM],
                                            small[:, 224 + c:225 + c], None, ALU.mult)
                ins.then_inc(s_mnorm, 1)

            for s in range(MAHEAD):
                mem_max(s)
            for s in range(MSEQ):
                mem_probs(s)
                if s + MAHEAD < MSEQ:
                    mem_max(s + MAHEAD)
            for h in range(MH):
                split_lo(("mo", h), moT_lo[:, h, :], moT_hi[:, h, :], 1.0)
            weight_lo(41, 1)
            residual("wom", 0)
            residual("wom", 1)
            for k in range(1, KT, 2):
                job = ("hT", 2, k)
                wait_filled(dve, job)
                free(dve.tensor_scalar(hT[:, k, :], bank(job)[:], col("norm_moe", k), None, ALU.mult), job)

            def R(lo, n):
                return rt[:, lo:lo + n]

            def R3(lo, w, n=TT):
                return rt[:, lo:lo + n * w].rearrange("p (t w) -> p t w", w=w)

            def bc(x, w):
                return x.unsqueeze(2).to_broadcast([P, TT, w])

            dve.wait_ge(s_rms, 2 + 2 * TT)
            dve.reciprocal(small[:, 28:32], small[:, 28:32]).then_inc(s_xn, 1)
            dve.wait_ge(s_xn, TT + 3)
            for i in range(TT):
                dve.tensor_scalar(xn[:, i, :], x2[:, i, :], small[:, 28 + i:29 + i], None, ALU.mult).then_inc(s_xn, 1)
            lg = R3(0, NG + NE)
            job = ("router",)
            wait_filled(dve, job)
            for i in range(TT):
                ins = dve.scalar_tensor_tensor(lg[:, i, :], bank(job)[:, i * 20:(i + 1) * 20], small[:, 28 + i:29 + i],
                                               row("b_router"), ALU.mult, ALU.add)
            free(ins, job)
            wait_freed(dve, job)
            gl = lg[:, :, 0:NG]
            link(dve.tensor_reduce(R(80, 4), gl, AX.X, ALU.max))
            dve.tensor_tensor(R3(84, 4), gl, bc(R(80, 4), 4), ALU.subtract).then_inc(s_r1, 1)
            first4 = row("first4").unsqueeze(1).to_broadcast([P, TT, 4])

            def first_only(dst, x, top, scratch, scratch1):
                link(dve.tensor_tensor(dst, x, bc(top, 4), ALU.is_equal))
                link(dve.tensor_tensor(scratch, dst, first4, ALU.mult))
                link(dve.tensor_reduce(scratch1, scratch, AX.X, ALU.max))
                link(dve.tensor_tensor(dst, scratch, bc(scratch1, 4), ALU.is_equal))

            ohg = R3(120, 4)
            first_only(ohg, gl, R(80, 4), R3(136, 4), R(152, 4))
            pick = rt[:, 640:640 + 64].rearrange("p (t e g) -> p t e g", t=TT, e=EPG)
            el = lg[:, :, NG:].rearrange("p t (g e) -> p t e g", g=NG)
            for t in range(TT):
                ins = dve.tensor_tensor(pick[:, t], el[:, t], ohg[:, t, :].unsqueeze(1).to_broadcast([P, EPG, NG]), ALU.mult)
            link(ins)
            sel = R3(160, 4)
            link(dve.tensor_reduce(sel, pick, AX.X, ALU.add))
            link(dve.tensor_reduce(R(176, 4), sel, AX.X, ALU.max))
            oh1, oh2 = R3(210, 4), R3(226, 4)
            first_only(oh1, sel, R(176, 4), R3(136, 4), R(152, 4))
            rest = R3(242, 4)
            link(dve.scalar_tensor_tensor(rest, oh1, -3.0e38, sel, ALU.mult, ALU.add))
            link(dve.tensor_reduce(R(180, 4), rest, AX.X, ALU.max))
            dve.tensor_tensor(R(200, 4), R(180, 4), R(176, 4), ALU.subtract).then_inc(s_r3, 1)
            first_only(oh2, rest, R(180, 4), R3(136, 4), R(152, 4))
            dve.wait_ge(s_r2, 1)
            link(dve.tensor_reduce(R(260, 4), R3(100, 4), AX.X, ALU.add))
            link(dve.reciprocal(R(260, 4), R(260, 4)))
            dve.wait_ge(s_r4, 1)
            link(dve.tensor_scalar(R(264, 4), R(204, 4), 1.0, None, ALU.add))
            link(dve.reciprocal(R(264, 4), R(264, 4)))
            link(dve.tensor_tensor(R(268, 4), R(260, 4), R(264, 4), ALU.mult))
            link(dve.tensor_tensor(R(272, 4), R(268, 4), R(204, 4), ALU.mult))
            E1 = rt[:, 300:364].rearrange("p (t g e) -> p t g e", t=TT, g=NG)
            E2 = rt[:, 364:428].rearrange("p (t g e) -> p t g e", t=TT, g=NG)
            for oh, E in ((oh1, E1), (oh2, E2)):
                for t in range(TT):
                    ins = dve.tensor_tensor(E[:, t], ohg[:, t, :].unsqueeze(2).to_broadcast([P, NG, EPG]),
                                            oh[:, t, :].unsqueeze(1).to_broadcast([P, NG, EPG]), ALU.mult)
            link(ins)
            dve.tensor_tensor(R(428, 64), R(300, 64), R(364, 64), ALU.add).then_inc(s_oh, 1)
            job = ("count",)
            wait_filled(dve, job)
            free(dve.tensor_copy(R(500, 80), bank(job)[:, 0:80]), job)
            wait_freed(dve, job)
            pos, cnt = R(500, 64), R(564, 16)

            def above(dst, x, bounds, op, scratch):
                link(dve.tensor_scalar(dst, x, float(bounds[0]), None, op))
                for v in bounds[1:]:
                    link(dve.scalar_tensor_tensor(dst, x, float(v), dst, op, ALU.add))

            ov, inc, nxt = R(720, 16), R(736, 16), R(752, 16)
            above(ov, cnt, (128, 256, 384), ALU.is_gt, None)
            link(dve.tensor_copy(inc, ov))
            for s in (1, 2, 4, 8):
                dve.tensor_copy(nxt[:, 0:s], inc[:, 0:s])
                link(dve.tensor_tensor(nxt[:, s:], inc[:, s:], inc[:, 0:NE - s], ALU.add))
                inc, nxt = nxt, inc
            hi = R(780, 64)
            above(hi, pos, (128, 256, 384), ALU.is_ge, None)
            far, lo, blkn = R(850, 64), R(920, 64), R(990, 64)
            link(dve.scalar_tensor_tensor(lo, hi, -128.0, pos, ALU.mult, ALU.add))
            link(dve.tensor_scalar(far, hi, 0.0, None, ALU.is_gt))
            exp4 = row("expert").unsqueeze(1).to_broadcast([P, TT, NE])
            link(dve.tensor_tensor(R(1060, 16), inc, ov, ALU.subtract))
            link(dve.tensor_tensor(R(1060, 16), R(1060, 16), row("expert"), ALU.subtract))
            b3 = R3(990, NE)
            link(dve.scalar_tensor_tensor(b3, R3(780, NE), float(NE - 1), R(1060, 16).unsqueeze(1).to_broadcast([P, TT, NE]),
                                          ALU.add, ALU.add))
            link(dve.tensor_tensor(blkn, blkn, far, ALU.mult))
            link(dve.tensor_tensor(b3, b3, exp4, ALU.add))
            link(dve.scalar_tensor_tensor(lo, lo, float(NB), blkn, ALU.mult, ALU.add))
            link(dve.tensor_tensor(R(1100, 64), lo, R(300, 64), ALU.mult))
            link(dve.tensor_tensor(R(1170, 64), lo, R(364, 64), ALU.mult))
            link(dve.tensor_reduce(R(1240, 4), R3(1100, NE), AX.X, ALU.add))
            link(dve.tensor_reduce(R(1244, 4), R3(1170, NE), AX.X, ALU.add))
            link(dve.tensor_copy(slot_i[:].rearrange("p r t -> p (r t)"), R(1240, 8)))
            tok = cols[:, COLS["token"]:COLS["token"] + TT]
            for r in range(2):
                dve.tensor_copy(rec[:, r, :, 0], tok)
                dve.tensor_scalar(rec[:, r, :, 1], tok, float(r * T), None, ALU.add)
                dve.tensor_copy(rec[:, r, :, 3], tok)
                ins = dve.tensor_copy(rec[:, r, :, 2], R(268 + 4 * r, 4))
            ins.then_inc(s_slot, 1)
            tab = rt[0:1, 1300:1332]
            tot = inc[0:1, 15:16]
            cmp = rt[0:1, 1340:1468].rearrange("p (i e) -> p i e", e=NE)
            link(dve.tensor_tensor(cmp, inc[0:1, :].unsqueeze(1).to_broadcast([1, 8, NE]),
                                   rows[0:1, ROWS["extra"][0]:ROWS["extra"][1]].unsqueeze(2).to_broadcast([1, 8, NE]), ALU.is_le))
            link(dve.memset(tab, 0.0))
            dve.tensor_copy(tab[:, 0:NE], rows[0:1, ROWS["expert"][0]:ROWS["expert"][1]])
            link(dve.tensor_reduce(tab[:, NE:NE + 8], cmp, AX.X, ALU.add))
            link(dve.tensor_scalar(tab[:, NE:NE + 8], tab[:, NE:NE + 8], float(NE - 1), None, ALU.min))
            half = rt[0:1, 1480:1481]
            above(half, tot, (1, 3, 5, 7), ALU.is_ge, None)
            link(dve.tensor_scalar(tab[:, 31:32], half, 2.0, None, ALU.mult))
            dve.tensor_copy(e_tab[:], tab).then_inc(s_tab, 1)

            def rows_evac(b, q):
                dve.wait_ge(s_t, 2 * b + 2)
                if not isinstance(b, int) or b >= 2:
                    dve.wait_ge(s_up, b - 1)
                for k in range(4, 8):
                    ins = dve.tensor_scalar(hgT[q][:, k, :], banks[1][:, (k - 4) * P:(k - 3) * P], col("norm_moe", k), None, ALU.mult)
                ins.then_inc(s_td, 1)

            def act_mul(b, q):
                dve.wait_ge(s_silu, b + 1)
                dve.wait_ge(s_up, b + 1)
                if not isinstance(b, int) or b >= 2:
                    dve.wait_ge(s_at, b - 1)
                dve.tensor_tensor(ga[q][:], sg[q][:], banks[3][:], ALU.mult).then_inc(s_mul, 1)

            def out_evac(b, q):
                dve.wait_ge(s_down, b + 1)
                dve.wait_ge(s_meta, b + 1)
                dve.tensor_scalar(eo[q][:, 512:D], banks[6][:], meta_g[:, q, :], None, ALU.mult).then_inc(s_od, 1)

            dve.wait_ge(s_tab, 1)
            rows_evac(0, 0)
            act_mul(0, 0)
            rows_evac(1, 1)
            act_mul(1, 1)
            rows_evac(2, 0)
            out_evac(0, 0)
            nb = dve.value_load(e_tab[0:1, 31:32], min_val=0, max_val=MAXB - NE) + NE
            with dve.Fori(2, nb, 2) as b:
                act_mul(b, 0)
                rows_evac(b + 1, 1)
                out_evac(b - 1, 1)
                act_mul(b + 1, 1)
                rows_evac(b + 2, 0)
                out_evac(b, 0)
            out_evac(nb - 1, 1)
            dve.wait_ge(ld["back"], 16 * 2 * TT)
            for i in range(TT):
                dve.tensor_tensor(x2[:, i, :], x2[:, i, :], y_back[:, 0, i, :], ALU.add).then_inc(s_fin, 1)
                dve.wait_ge(s_fin, 2 * i + 1)
                dve.tensor_tensor(x2[:, i, :], x2[:, i, :], y_back[:, 1, i, :], ALU.add).then_inc(s_fin, 1)

        @block.tensor
        def _(pe):
            def done(ins):
                ins.then_inc(filled, 1)

            def accumulate(job, dst, pairs):
                for n, (l, r) in enumerate(pairs):
                    ins = pe.matmul(dst, l, r, start=(n == 0), stop=(n == len(pairs) - 1))
                return ins

            def transposes(job, srcs, width=P):
                open_bank(pe, job)
                for n, s in enumerate(srcs):
                    ins = pe.transpose(bank(job)[:, n * width:(n + 1) * width], s, ident[:])
                done(ins)

            def mlp(j):
                job = ("mlp", j)
                open_bank(pe, job)
                if j == 0:
                    pe.wait_ge(ld["w12"], 32)
                    pe.wait_ge(ld["zemb"], 16)
                    done(pe.matmul(bank(job)[0:FF, :], w1[:], zemb[:], start=True, stop=True))
                else:
                    pe.wait_ge(s_sin, 1)
                    done(pe.matmul(bank(job)[0:FF, :], w2[:], a1[:], start=True, stop=True))

            def hT_jobs(n, src, ready):
                for k in range(KT):
                    ready(k)
                    transposes(("hT", n, k), [src[:, i, k * P:(k + 1) * P] for i in range(TT)])

            def residual_done(key):
                def ready(k):
                    if k % (KT // 2) == 0:
                        for i in range(TT):
                            wait_freed(pe, (key, 2 * k // KT, i))
                return ready

            def chunk_jobs(name, act_hi, act_lo, weights_first=False, width=512, part=slice(None)):
                for n in range(first_piece[name], last_piece[name] + 1)[part]:
                    _, k0, nk, _, jobs_ = pieces[n]
                    pe.wait_ge(s_wl, n + 1)
                    wh, wl = piece_view(w_hi, n), piece_view(w_lo, n)
                    for j, job in enumerate(jobs_):
                        if k0 == 0:
                            open_bank(pe, job)
                        tile_ = slice(j * P, (j + 1) * P)
                        for kk in range(nk):
                            k = k0 + kk
                            final = n == last_piece[name] and kk == nk - 1
                            for m, (act_, w_) in enumerate(((act_hi, wh), (act_hi, wl), (act_lo, wh))):
                                if weights_first:
                                    left, right = w_[:, kk, tile_], act_[:, k, :]
                                else:
                                    left, right = act_[:, k, tile_], w_[:, kk, :]
                                ins = pe.matmul(bank(job)[:, 0:width], left, right, start=(k == 0 and m == 0),
                                                stop=(final and m == 2))
                            if final:
                                done(ins)
                    if not final:
                        ins.then_inc(ring_used, 1)

            def filter_jobs(o, tiles):
                for t in tiles:
                    for way in range(2):
                        job = ("filt", o, t, way)
                        open_bank(pe, job)
                        c0 = (2 * o + way) * CH
                        done(pe.matmul(bank(job)[:], a2[:, t * P:(t + 1) * P], w3[:, c0:c0 + CH], start=True, stop=True))

            def l1_job(o):
                job = ("l1", o)
                open_bank(pe, job)
                pe.wait_ge(s_l1, 4 * o + 4)
                done(pe.matmul(bank(job)[:], ones[:], l1sum[:], start=True, stop=True))

            def spec_jobs(o, f):
                for c in range(4):
                    job = ("spec", o, f, c)
                    open_bank(pe, job)
                    if c == 0:
                        pe.wait_ge(s_spdm, 4 * o + 4)
                    par = c // 2
                    done(accumulate(job, bank(job)[:], [(dft[:, k, c, f * P:(f + 1) * P], sum_diff[o][:, c % 2, 2 * par + k, :])
                                                        for k in range(2)]))

            def z_jobs(o):
                for k in range(4):
                    if k == 0:
                        if o == 0:
                            for c in range(CT):
                                wait_freed(pe, ("u", c))
                        else:
                            pe.wait_ge(s_z, CT)
                    transposes(("zT", o, k), [u[:, c, k * P:(k + 1) * P] for c in range(CT)])

            mlp(0)
            pe.wait_ge(ld["mats"], 64)
            pe.wait_ge(ld["mem"], 16)
            for j in range(KT // 2):
                transposes(("memT", j), [mem_raw[:, m, k * P:(k + 1) * P] for k in (2 * j, 2 * j + 1) for m in range(MT)])
            mlp(1)
            for j in range(KT // 2):
                wait_freed(pe, ("memT", j))
            chunk_jobs("mk", memT_hi, memT_lo)
            hT_jobs(0, x_in, lambda k: pe.wait_ge(s_xn, TT))
            pe.wait_ge(s_sin, 2)
            pe.wait_ge(ld["w3"], 16)
            filter_jobs(0, range(4))
            chunk_jobs("mv", memT_hi, memT_lo)
            l1_job(0)
            pe.wait_ge(ld["dft"], 16)
            spec_jobs(0, 0)
            filter_jobs(1, (0, 1))
            spec_jobs(0, 1)
            filter_jobs(1, (2, 3))
            for k in range(KT):
                wait_freed(pe, ("hT", 0, k))
            chunk_jobs("v", hT_hi, hT_lo, weights_first=True)
            l1_job(1)
            spec_jobs(1, 0)
            spec_jobs(1, 1)
            z_jobs(0)
            chunk_jobs("g1", hT_hi, hT_lo, weights_first=True)

            def fwd_jobs(o):
                for f in range(2):
                    for c in range(4):
                        job = ("fwd", o, f, c)
                        open_bank(pe, job)
                        if f == 0 and c == 0:
                            for k in range(4):
                                wait_freed(pe, ("zT", o, k))
                        par = c // 2
                        done(accumulate(job, bank(job)[:], [(dft[:, k, c, f * P:(f + 1) * P], zt[:, 2 * par + k, :])
                                                            for k in range(2)]))

            def inv_jobs(o):
                pe.wait_ge(s_ab, 2 * o + 2)
                if o == 0:
                    pe.wait_ge(ld["idft"], 16)
                for c in range(CT):
                    job = ("inv", o, c)
                    open_bank(pe, job)
                    for par in range(2):
                        ins = accumulate(job, bank(job)[:, par * HALF:(par + 1) * HALF],
                                         [(sd[:, f, 2 * par + ri, c * P:(c + 1) * P], idft[:, f, 2 * par + ri, :])
                                          for f in range(2) for ri in range(2)])
                    done(ins)

            fwd_jobs(0)
            chunk_jobs("g2", hT_hi, hT_lo, weights_first=True)
            inv_jobs(0)
            z_jobs(1)
            fwd_jobs(1)
            chunk_jobs("q", hT_hi, hT_lo)
            chunk_jobs("kv", hT_hi, hT_lo, width=256)
            inv_jobs(1)
            pe.wait_ge(s_mkn, MT)
            for j in range(2):
                transposes(("mkT", j), [mk[:, m, h * MHD:(h + 1) * MHD] for h in (2 * j, 2 * j + 1) for m in range(MT)])
            pe.wait_ge(s_rope, TT + 1)
            for p in range(NQ // 2):
                transposes(("qT", p), [qkv[:, i, p * P:(p + 1) * P] for i in range(TT)])
            pe.wait_ge(s_kdup, 1)
            for g in range(NKV):
                transposes(("kT", g), [kdup[:, i, g].rearrange("p w d -> p (w d)") for i in range(TT)])
            for c in range(CT):
                job = ("hn", c)
                open_bank(pe, job)
                pe.wait_ge(s_ysq, c + 1)
                done(pe.matmul(bank(job)[:], blk[:], y_sq[:, c, :], start=True, stop=True))

            def score(s):
                i, h = s // NQ, s % NQ
                job = ("S", s)
                open_bank(pe, job)
                if s == 0:
                    for p in range(NQ // 2):
                        wait_freed(pe, ("qT", p))
                    for g in range(NKV):
                        wait_freed(pe, ("kT", g))
                lo = HD * (h % 2)
                done(pe.matmul(bank(job)[:], qT[lo:lo + HD, h // 2, i * P:(i + 1) * P], kT[lo:lo + HD, h // 4, :],
                               start=True, stop=True))

            def pt(s):
                wait_freed(pe, ("S", s))
                transposes(("PT", s), [pr[:, s % NPR, k * P:(k + 1) * P] for k in range(4)])

            def pv(s):
                i, h = s // NQ, s % NQ
                job = ("O", i)
                if h == 0:
                    open_bank(pe, job)
                wait_freed(pe, ("PT", s))
                v0 = 640 + HD * (h // 4)
                ins = accumulate(job, bank(job)[:, h * HD:(h + 1) * HD],
                                 [(pT[:, s % NPR, k * P:(k + 1) * P], qkv[:, k, v0:v0 + HD]) for k in range(4)])
                ins.then_inc(s_asq, 1)

            for s in range(AHEAD):
                score(s)
            for s in range(-1, NSEQ):
                if s + 1 + AHEAD < NSEQ:
                    score(s + 1 + AHEAD)
                if s + 1 < NSEQ:
                    pt(s + 1)
                if s >= 0:
                    pv(s)
            pe.wait_ge(s_yh, CT)
            chunk_jobs("wo0", yT_hi, yT_lo, part=slice(0, 2))
            pe.wait_ge(s_att, TT)
            for k in range(CT):
                transposes(("yT", k), [att[:, i, k * P:(k + 1) * P] for i in range(TT)])
            for k in range(CT):
                wait_freed(pe, ("yT", k))
            chunk_jobs("wo0", yT_hi, yT_lo, part=slice(2, None))
            chunk_jobs("wo1", yT_hi, yT_lo)
            hT_jobs(1, x2, residual_done("wout"))
            for k in range(KT):
                wait_freed(pe, ("hT", 1, k))
            chunk_jobs("wq", hT_hi, hT_lo)
            for i in range(TT):
                wait_freed(pe, ("mq", i))
            for h in range(MH):
                transposes(("mqT", h), [mq[:, i, h * MHD:(h + 1) * MHD] for i in range(TT)])

            def mem_score(s):
                i, hp = s // 2, s % 2
                job = ("MS", s)
                open_bank(pe, job)
                if s == 0:
                    for h in range(MH):
                        wait_freed(pe, ("mqT", h))
                    for j in range(2):
                        wait_freed(pe, ("mkT", j))
                for c in range(2):
                    h = 2 * hp + c
                    ins = pe.matmul(bank(job)[:, c * NM:(c + 1) * NM], mqT[:, h, i * P:(i + 1) * P], mkT[:, h, :],
                                    start=True, stop=True)
                done(ins)

            for s in range(MAHEAD):
                mem_score(s)
            for s in range(MSEQ):
                if s + MAHEAD < MSEQ:
                    mem_score(s + MAHEAD)
                pe.wait_ge(s_mnorm, s + 1)
                transposes(("MPT", s), [pr[:, s % NPR, k * P:(k + 1) * P] for k in range(4)])
            for s in range(MSEQ):
                wait_freed(pe, ("MPT", s))
            for j in range(MT):
                wait_freed(pe, ("mv", j))
            for h in range(MH):
                job = ("mo", h)
                open_bank(pe, job)
                done(accumulate(job, bank(job)[:], [(mv[:, k, h * MHD:(h + 1) * MHD], mpT[:, h, k, :]) for k in range(MT)]))
            for h in range(MH):
                wait_freed(pe, ("mo", h))
            for h in range(2):
                chunk_jobs(f"wom{h}", moT_hi, moT_lo)
            hT_jobs(2, x2, residual_done("wom"))
            for k in range(KT):
                wait_freed(pe, ("hT", 2, k))
            job = ("router",)
            open_bank(pe, job)
            pe.wait_ge(ld["wr"], 16)
            for i in range(TT):
                ins = accumulate(job, bank(job)[:, i * 20:(i + 1) * 20],
                                 [(hT[:, k, i * P:(i + 1) * P], wr[:, k, :]) for k in range(KT)])
            done(ins)
            job = ("count",)
            open_bank(pe, job)
            pe.wait_ge(s_oh, 1)
            for i in range(TT + 1):
                pairs = [(ones[:], rt[:, 428 + NE * j:428 + NE * (j + 1)]) for j in range(i)]
                if i < TT:
                    pairs += [(tri[:], rt[:, 428 + NE * i:428 + NE * (i + 1)])]
                ins = accumulate(job, bank(job)[:, i * NE:(i + 1) * NE], pairs)
            done(ins)

            for b in range(7):
                pe.wait_ge(freed[b], uses[b])
            pe.wait_ge(s_tab, 1)

            def view(s):
                return slot[s][:].rearrange("p (t n) -> p t n", t=(8, 8, 4)[s % 3])

            def rows_T(b, q):
                pe.wait_ge(s_gath[q], (b - q) * 8 + 16)
                if not isinstance(b, int) or b >= 1:
                    pe.wait_ge(s_ta, b)
                    pe.wait_ge(s_td, b)
                for half in range(2):
                    for k in range(4):
                        c = 4 * half + k
                        ins = pe.transpose(banks[half][:, k * P:(k + 1) * P], hg[q][:, c * P:(c + 1) * P], ident[:])
                    ins.then_inc(s_t, 1)

            def gate_up(b, q):
                pe.wait_ge(s_ta, b + 1)
                pe.wait_ge(s_td, b + 1)
                if not isinstance(b, int) or b >= 1:
                    pe.wait_ge(s_mul, b)
                for c, sem_ in ((0, s_gate), (1, s_up)):
                    pe.wait_ge(w_ld[3 * q + c], (b - q) * 8 + 16)
                    w = view(3 * q + c)
                    accumulate(None, banks[2 + c][:], [(hgT[q][:, k, :], w[:, k, :]) for k in range(KT)]).then_inc(sem_, 1)

            def acts_T(b, q):
                pe.wait_ge(s_mul, b + 1)
                if not isinstance(b, int) or b >= 1:
                    pe.wait_ge(s_ate, b)
                for k in range(4):
                    ins = pe.transpose(banks[4][:, k * P:(k + 1) * P], ga[q][:, k * P:(k + 1) * P], ident[:])
                ins.then_inc(s_at, 1)

            def down(b, q):
                pe.wait_ge(s_ate, b + 1)
                pe.wait_ge(w_ld[3 * q + 2], (b - q) * 8 + 16)
                if not isinstance(b, int) or b >= 1:
                    pe.wait_ge(s_oa, b)
                    pe.wait_ge(s_od, b)
                w = view(3 * q + 2)
                for half, sem_ in ((0, s_down0), (1, s_down)):
                    accumulate(None, banks[5 + half][:], [(gaT[q][:, k, :], w[:, k, half * 512:(half + 1) * 512])
                                                          for k in range(4)]).then_inc(sem_, 1)

            rows_T(0, 0)
            gate_up(0, 0)
            rows_T(1, 1)
            acts_T(0, 0)
            gate_up(1, 1)
            rows_T(2, 0)
            down(0, 0)
            acts_T(1, 1)
            nb = pe.value_load(e_tab[0:1, 31:32], min_val=0, max_val=MAXB - NE) + NE
            with pe.Fori(2, nb, 2) as b:
                gate_up(b, 0)
                rows_T(b + 1, 1)
                down(b - 1, 1)
                acts_T(b, 0)
                gate_up(b + 1, 1)
                rows_T(b + 2, 0)
                down(b, 0)
                acts_T(b + 1, 1)
            down(nb - 1, 1)


def _constants():
    t = np.arange(T)
    half = np.arange(HALF)
    freq = (half + 0.5) * 2.0 * np.pi / (2 * T)
    parity = np.concatenate([t[0::2], t[1::2]])
    ang = parity[:, None] * freq[None, :]
    cs, sn = np.cos(ang), -np.sin(ang)
    dft = np.zeros((P, 2, 4, HALF))
    for par in range(2):
        for k in range(2):
            r = par * HALF + k * P
            dft[:, k, 2 * par] = cs[r:r + P]
            dft[:, k, 2 * par + 1] = sn[r:r + P]
    idft = np.zeros((P, 2, 4, HALF))
    for f in range(2):
        for par in range(2):
            r = slice(par * HALF, (par + 1) * HALF)
            idft[:, f, 2 * par] = cs[r, f * P:(f + 1) * P].T / T
            idft[:, f, 2 * par + 1] = sn[r, f * P:(f + 1) * P].T / T
    f32 = np.float32
    tl = np.linspace(0.0, 1.0, T, dtype=f32)
    bands = np.linspace(1e-4, 15, 16, dtype=f32)
    w = (f32(2.0 * np.pi / T) * t.astype(f32))[:, None] * bands[None, :]
    w = w.astype(f32)
    zemb = np.concatenate([tl[:, None], np.cos(w.astype(np.float64)), np.sin(w.astype(np.float64))], 1)[parity].T
    deltas = np.abs(np.linspace(np.log(1e-2) / 1.5, np.log(1e-2) / 0.3, CH, dtype=f32))
    decay = np.exp((-tl[:, None] * deltas[None, :]).astype(f32).astype(np.float64))[parity].reshape(4, P, CH).transpose(1, 0, 2)
    inv = 10000.0 ** (-np.arange(16) / 16.0)
    rope = np.zeros((P, 2, TT, HD))
    for i in range(TT):
        tok = i * P + np.arange(P)
        for s, pos in enumerate((tok // 64, tok % 64)):
            a = pos[:, None] * inv[None, :]
            for wv in range(2):
                c0 = 32 * s + 16 * wv
                rope[:, 0, i, c0:c0 + 16] = np.cos(a)
                rope[:, 1, i, c0:c0 + 16] = np.sin(a) * (1 if wv else -1)
    mats = np.zeros((P, 4, P))
    mats[:, 0] = np.eye(P)
    mats[:, 1] = 1.0
    mats[:, 2] = np.kron(np.eye(2), np.ones((HD, HD)))
    mats[:, 3] = np.triu(np.ones((P, P)), 1)
    rec = np.zeros((P, NB, 4))
    rec[:, :, 1] = SPARE + np.arange(P)[:, None]
    return {k: np.ascontiguousarray(v, dtype=f32) for k, v in
            dict(dft=dft, idft=idft, zemb=zemb, decay=decay, rope=rope, mats=mats, rec_init=rec.reshape(P * NB, 4)).items()}


_DIRECT = ["x", "mem", "w_in", "filt_w1", "filt_w2", "filt_w3", "w_out", "w_q_mem", "w_k_mem", "w_v_mem", "w_o_mem",
           "w_gate", "w_up", "w_down"]


def kernel(**inputs):
    import concourse.bacc as _bacc
    from concourse.bass_utils import run_bass_kernel_spmd as _run

    v = {k: np.ascontiguousarray(x) for k, x in inputs.items()}
    arrays = {k: v[k] for k in _DIRECT}
    arrays.update(_constants())

    def column(x):
        x = np.asarray(x).reshape(-1)
        if x.size < P:
            x = np.concatenate([x, np.zeros(P - x.size, x.dtype)])
        return x.reshape(-1, P).T

    not_first = np.ones((P, 1), np.float32)
    not_first[0] = 0.0
    token = (np.arange(P)[:, None] + P * np.arange(TT)[None, :]).astype(np.float32)
    arrays["cols"] = np.ascontiguousarray(np.concatenate(
        [column(v[k]) for k in ("norm_mix", "norm_xattn", "norm_mem", "norm_moe", "hyena_short_w", "hyena_short_b",
                                "hyena_skip", "out_norm_hyena", "out_norm_attn", "filt_b1", "filt_b2")]
        + [column(v["filt_sin_freq"][0, j]) for j in range(2)]
        + [column(v["mem_q_norm"]), not_first, token], axis=1))
    one_row = np.concatenate([v["attn_q_norm"][0], v["attn_k_norm"][0], v["mem_q_norm"][0], v["mem_k_norm"][0],
                              v["b_router_grp"][0], v["b_router_exp"][0],
                              np.array([4, 3, 2, 1], np.float32), np.arange(NE, dtype=np.float32),
                              np.arange(8, dtype=np.float32)])
    arrays["rows"] = np.ascontiguousarray(np.broadcast_to(one_row, (P, one_row.size)))
    arrays["w_router"] = np.ascontiguousarray(
        np.concatenate([v["w_router_grp"][0], v["w_router_exp"][0]], axis=1).reshape(KT, P, NG + NE).transpose(1, 0, 2))

    nc = _bacc.Bacc("TRN2", target_bir_lowering=False, num_devices=1)
    aps = {k: nc.dram_tensor(f"in_{k}", x.shape, mybir.dt.from_np(x.dtype), kind="ExternalInput").ap()
           for k, x in arrays.items()}
    out = nc.dram_tensor("out_0_dram", (1, T, D), F32, kind="ExternalOutput").ap()
    rec_dram = nc.dram_tensor("rec_dram", (P * NB, 4), F32, kind="Internal").ap()
    xn_dram = nc.dram_tensor("xn_dram", (T, D), F32, kind="Internal").ap()
    y_dram = nc.dram_tensor("y_dram", (2 * T + P, D), F32, kind="Internal").ap()
    build(nc, aps, out, rec_dram, xn_dram, y_dram)
    r = _run(nc, [{f"in_{k}": x for k, x in arrays.items()}], core_ids=[0])
    return r.results[0]["out_0_dram"]
```

```python
from contextlib import ExitStack

import numpy as np
import concourse.bass as bass
from concourse import mybir

F32 = mybir.dt.float32
F32R = mybir.dt.float32r
I32 = mybir.dt.int32
ALU = mybir.AluOpType
ACT = mybir.ActivationFunctionType
AX = mybir.AxisListType

P = 128
T, D = 512, 1024
TT, KT = T // P, D // P
NM = 256
MT = NM // P
CH = 512
CT = CH // P
HALF = T // 2
NQ, NKV, HD = 8, 2, 64
MH, MHD = 4, 128
NG, EPG = 4, 4
NE = NG * EPG
FE = 512
FB, FF = 33, 64
EPS = 1e-6
NB = 28
MAXB = 24
SPARE = 2 * T
AHEAD = 4
MAHEAD = 3
HN_STEP = 6
NHI = 6
PIECES = 12
NSLOT = 3
NPR = 4
KB = 1024

COLS = {}
_at = 0
for _name, _n in (("norm_mix", KT), ("norm_xattn", KT), ("norm_mem", KT), ("norm_moe", KT),
                  ("short_w", 3 * 12), ("short_b", 12), ("skip", 2 * CT), ("hyena_norm", CT),
                  ("attn_norm", CT), ("b1", 1), ("b2", 1), ("freq", 2), ("gmq", 1), ("not_first", 1), ("spare", 1), ("token", TT)):
    COLS[_name] = _at
    _at += _n
NCOLS = _at
ROWS = {}
_at = 0
for _name, _n in (("gq", HD), ("gk", HD), ("gmq", MHD), ("gmk", MHD), ("b_router", NG + NE),
                  ("first4", 4), ("expert", NE), ("extra", 8)):
    ROWS[_name] = (_at, _at + _n)
    _at += _n
NROWS = _at


def psum_jobs():
    jobs = [("mlp", 0)] + [("memT", j) for j in range(KT // 2)] + [("mlp", 1)]

    def filt(o, tiles):
        return [("filt", o, t, way) for t in tiles for way in range(2)]

    def spec(o, f):
        return [("spec", o, f, c) for c in range(4)]

    jobs += [("mk", j) for j in range(MT)] + [("hT", 0, k) for k in range(KT)] + filt(0, range(4))
    jobs += [("mv", j) for j in range(MT)]
    jobs += [("l1", 0)] + spec(0, 0) + filt(1, (0, 1)) + spec(0, 1) + filt(1, (2, 3))
    jobs += [("u", c) for c in range(4)] + [("l1", 1)] + spec(1, 0) + spec(1, 1)
    jobs += [("zT", 0, k) for k in range(4)] + [("u", c) for c in range(4, 8)]
    for o in range(2):
        jobs += ([("zT", o, k) for k in range(4)] if o else []) + [("fwd", o, f, c) for f in range(2) for c in range(4)]
        jobs += [("u", c) for c in range(8, 12)] if o == 0 else [(key, i) for key in ("q", "kv") for i in range(TT)]
        jobs += [("inv", o, c) for c in range(CT)]
    jobs += [("mkT", j) for j in range(2)]
    jobs += [("qT", p) for p in range(NQ // 2)] + [("kT", g) for g in range(NKV)] + [("hn", c) for c in range(CT)]
    n = TT * NQ
    jobs += [("S", s) for s in range(AHEAD)]
    for s in range(-1, n):
        if s >= 0 and s % NQ == 0:
            jobs += [("O", s // NQ)]
        if s + 1 + AHEAD < n:
            jobs += [("S", s + 1 + AHEAD)]
        if s + 1 < n:
            jobs += [("PT", s + 1)]
    jobs += [("yT", k) for k in range(CT)]
    jobs += [("wout", h, i) for h in range(2) for i in range(TT)]
    jobs += [("hT", 1, k) for k in range(KT)]
    jobs += [("mq", i) for i in range(TT)] + [("mqT", h) for h in range(MH)]
    n = TT * 2
    jobs += [("MS", s) for s in range(MAHEAD)]
    for s in range(n):
        if s + MAHEAD < n:
            jobs += [("MS", s + MAHEAD)]
        jobs += [("MPT", s)]
    jobs += [("mo", h) for h in range(MH)]
    jobs += [("wom", h, i) for h in range(2) for i in range(TT)]
    jobs += [("hT", 2, k) for k in range(KT)]
    jobs += [("router",), ("count",), ("records",)]
    return jobs


def build(nc, a, out, xn_dram, y_dram):
    with ExitStack() as ctx:
        base = nc.sbuf_base + (-nc.sbuf_base) % 64
        used = []

        def at(name, kb, shape, dt=F32):
            return nc.alloc_sbuf_tensor_at(name, shape, dt, offset=base + int(kb * KB))

        fence = ctx.enter_context(nc.sbuf_tensor("fence", [P, 205 * 256], F32))

        w_raw = [at(f"w_raw{s}", 4 * s, [P, 1024]) for s in range(NSLOT)]
        w_lo = [at(f"w_lo{s}", 4 * s, [P, 1024], F32R) for s in range(NSLOT)]
        w_hi = [at(f"w_hi{s}", 12 + 4 * s, [P, 1024], F32R) for s in range(NSLOT)]
        sum_diff1 = at("sum_diff1", 24, [P, 2, 4, CH])
        qkv = at("qkv", 24, [P, TT, 768])
        rope_tmp = at("rope_tmp", 36, [P, 640])
        mk = at("mk", 40, [P, MT, 512])
        mv = at("mv", 44, [P, MT, 512])
        hT_hi = at("hT_hi", 48, [P, KT, T], F32R)
        hT_lo = at("hT_lo", 64, [P, KT, T], F32R)
        hT = at("hT", 48, [P, KT, T])
        memT_hi = at("memT_hi", 80, [P, KT, NM], F32R)
        memT_lo = at("memT_lo", 88, [P, KT, NM], F32R)
        w3 = at("w3", 96, [FF, 2048])
        x_in = at("x_in", 120, [P, TT, D])
        mem_raw = at("mem_raw", 136, [P, MT, D])
        w1 = at("w1", 144, [FB, FF])
        w2 = at("w2", 144.5, [FF, FF])
        zemb = at("zemb", 146, [FB, T])
        a1 = at("a1", 148, [FF, T])
        a2 = at("a2", 150, [FF, T])
        u = at("u", 80, [P, 12, T])
        dft = at("dft", 104, [P, 2, 4, HALF])
        idft = at("idft", 112, [P, 2, 4, HALF])
        spec = at("spec", 120, [P, 2, 2, 4, CH])
        decay = at("decay", 152, [P, 4, CH])
        zt = at("zt", 152, [P, 4, CH])
        q_sq = at("q_sq", 152, [P, TT, 512])
        ep = at("ep", 160, [P, 4, CH])
        mlp_arg = at("mlp_arg", 172, [FF, T])
        mlp_k = at("mlp_k", 174, [FF, T])
        l1sum = at("l1sum", 168, [P, CH])
        rnorm = at("rnorm", 170, [P, CH])
        fabs = [at("fabs0", 172, [P, 2, CH]), at("fabs1", 140, [P, 2, CH])]
        ab = at("ab", 168, [P, 4, CH])
        sum_diff0 = at("sum_diff0", 176, [P, 2, 4, CH])
        sum_diff = [sum_diff0, sum_diff1]
        sd = at("sd", 176, [P, 2, 4, CH])
        fb = [at("fb0", 192, [P, 2, CH]), at("fb1", 136, [P, 2, CH])]
        tmp = at("tmp", 192, [P, 2, CH])
        qT = at("qT", 104, [P, NQ // 2, T])
        kT = at("kT", 112, [P, NKV, T])
        mkT = at("mkT", 116, [P, MH, NM])
        kdup = at("kdup", 160, [P, TT, NKV, 2, HD])
        x2 = at("x2", 120, [P, TT, D])
        yT_hi = at("yT_hi", 136, [P, KT, T], F32R)
        yT_lo = at("yT_lo", 64, [P, KT, T], F32R)
        att = at("att", 152, [P, TT, 512])
        pr = at("pr", 48, [P, NPR, T])
        pT = at("pT", 56, [P, NPR, T])
        att_sq = at("att_sq", 172, [P, 512])
        y_sq = at("y_sq", 176, [P, CT, CH])
        y_rs = at("y_rs", 184, [P, CT, CH])
        xn = at("xn", 80, [P, TT, D])
        mq = at("mq", 152, [P, TT, 512])
        mqT = at("mqT", 160, [P, MH, T])
        mpT = at("mpT", 176, [P, MH, MT, T])
        moT_hi = at("moT_hi", 104, [P, MH, T], F32R)
        moT_lo = at("moT_lo", 112, [P, MH, T], F32R)
        slot = [at(f"slot{s}", 16 * s, [P, 4096]) for s in range(6)]
        e_hi = [at(f"e_hi{j}", 96 + 4 * j, [P, 1024], F32R) for j in range(NHI)]
        e_lo = [at(f"e_lo{s}", 16 * s, [P, 4096], F32R) for s in range(6)]
        hg = [at(f"hg{q}", 136 + 4 * q, [P, D]) for q in range(2)]
        hgT_hi = at("hgT_hi", 144, [P, KT * P], F32R)
        hgT_lo = at("hgT_lo", 148, [P, KT * P], F32R)
        sg = at("sg", 152, [P, FE])
        ga = at("ga", 154, [P, FE])
        gaT_hi = at("gaT_hi", 156, [P, FE], F32R)
        gaT_lo = at("gaT_lo", 158, [P, FE], F32R)
        eo = [at(f"eo{q}", 160 + 4 * q, [P, D]) for q in range(2)]
        g_moe = at("g_moe", 168, [P, D])
        y_back = at("y_back", 0, [P, 2, TT, D])
        rt = at("rt", 172, [P, 3072])
        rec_sb = at("rec_sb", 184, [P, NB, 4])
        meta_i = at("meta_i", 185, [P, 2, 2], I32)
        meta_g = at("meta_g", 185.125, [P, 2, 1])
        gather_i = at("gather_i", 185.25, [P, 2, 1], I32)
        e_tab = at("e_tab", 185.5, [1, 32], I32)
        wr = at("wr", 187, [P, KT, NG + NE])
        rec_rhs = at("rec_rhs", 189, [P, 2 * TT, 3, MAXB])
        iota = at("iota", 191.5, [P, P])
        place_oh = at("place_oh", 192, [P, 2 * TT, P])
        cols = at("cols", 196, [P, NCOLS])
        rows = at("rows", 197, [P, NROWS])
        rope = at("rope", 199, [P, 2, TT, HD])
        ident = at("ident", 201, [P, P])
        ones = at("ones", 201.5, [P, P])
        blk = at("blk", 202, [P, P])
        tri = at("tri", 202.5, [P, P])
        small = at("small", 203, [P, 400])

        banks = [ctx.enter_context(nc.psum_tensor(f"bank{b}", [P, 512], F32)) for b in range(8)]

        def sem(name):
            return ctx.enter_context(nc.semaphore(name))

        jobs = psum_jobs()
        number, place, uses = {}, {}, [0] * 8
        turn, first_s = 0, jobs.index(("S", 0))
        last_s = max(n for n, j in enumerate(jobs) if j[0] == "PT")
        for n, j in enumerate(jobs):
            if j[0] == "O":
                b = 6 + j[1] % 2
            else:
                number[j] = len(number)
                span = 6 if first_s <= n <= last_s else 8
                b, turn = turn % span, (turn + 1) % span
            place[j] = (b, uses[b])
            uses[b] += 1
        filled = sem("psum_filled")
        freed = [sem(f"bank{b}_freed") for b in range(8)]
        def bank(job):
            return banks[place[job][0]]

        def wait_filled(eng, job):
            eng.wait_ge(filled, number[job] + 1)

        def free(ins, job):
            ins.then_inc(freed[place[job][0]], 1)

        def wait_freed(eng, job):
            eng.wait_ge(freed[place[job][0]], place[job][1] + 1)

        def open_bank(pe, job):
            b, use = place[job]
            if use:
                pe.wait_ge(freed[b], use)

        ld = {k: sem(f"ld_{k}") for k in ("x", "mem", "cols", "rows", "rope", "ident", "mats", "iota", "w12", "w3", "zemb", "decay",
                                          "dft", "idft", "x2", "g_moe", "wr")}
        ld_back = [sem(f"rows_back{i}") for i in range(TT)]
        ring_ld = [sem(f"ring_ld{s}") for s in range(NSLOT)]
        s_wh = sem("weight_hi_ready")
        s_wl = sem("weight_lo_ready")
        ring_used = sem("ring_used")
        s_hi = sem("hi_ready")
        s_xn = sem("xn_ready")
        s_arg = sem("mlp_arg_ready")
        s_sin = sem("mlp_sin_done")
        s_spdm = sem("spdm_ready")
        s_l1 = sem("l1_added")
        s_rn = sem("rnorm_ready")
        s_ke = sem("spec_parts_ready")
        s_kab = sem("spec_ready")
        s_conv = sem("conv_ready")
        s_a = sem("fwd_sum_ready")
        s_b = sem("fwd_diff_ready")
        s_pb = sem("prod_b_ready")
        s_ab = sem("prod_used")
        s_z = sem("z_ready")
        s_sq = sem("square_done")
        s_rms = sem("rms_ready")
        s_ms = sem("head_sums_ready")
        s_hrms = sem("head_rms_ready")
        s_abs = sem("filt_abs_ready")
        s_hroot = sem("hyena_rms_ready")
        s_rope = sem("rope_ready")
        s_kdup = sem("kdup_ready")
        s_qinv = sem("qk_norms_ready")
        s_mkn = sem("mk_normed")
        s_ysq = sem("y_square_ready")
        s_qsq = sem("q_square_ready")
        s_max = sem("score_max_ready")
        s_exp = sem("exp_done")
        s_att = sem("att_normed")
        s_yh = sem("y_hyena_ready")
        s_mqn = sem("mq_normed")
        s_mnorm = sem("mem_probs_ready")
        s_gq = sem("gq_scaled")
        s_asq = sem("att_square_done")
        s_store = sem("xn_stored")
        s_r1 = sem("route_group_logits")
        s_r2 = sem("route_group_exp")
        s_r3 = sem("route_expert_diff")
        s_r4 = sem("route_expert_exp")
        s_oh = sem("onehots_ready")
        s_rec = sem("records_ready")
        s_slot = sem("slot_onehots_ready")
        s_tab = sem("tables_ready")
        dchain, achain, pchain = sem("dve_step"), sem("act_step"), sem("pool_step")
        w_ld = [sem(f"expert_w_ld{s}") for s in range(6)]
        s_ehi = sem("expert_hi_ready")
        s_elo = sem("expert_lo_ready")
        s_used = sem("expert_piece_used")
        s_gath = [sem(f"gathered{q}") for q in range(2)]
        s_gi = sem("gather_index_ready")
        s_t = sem("rows_transposed")
        s_rhi, s_rlo = sem("rowsT_hi_ready"), sem("rowsT_lo_ready")
        s_silu, s_mul = sem("silu_done"), sem("act_mul_done")
        s_at = sem("actT_filled")
        s_ahi, s_alo = sem("actT_hi_ready"), sem("actT_lo_ready")
        s_oa = sem("out_evac")
        s_meta = sem("meta_ready")
        s_sc = [sem(f"rows_scattered{q}") for q in range(2)]
        s_fin = sem("sum_ready")
        s_out = sem("stored")
        waited_pool, waited_sp = sem("waited_pool"), sem("waited_sp")

        def count(b, j):
            return j + 1 if isinstance(b, int) and b == 0 else PIECES * b + j - 3

        def buffer(b, j):
            return (j if isinstance(b, int) and b == 0 else j + 8) % NHI

        def col(name, i=0, n=P):
            c = COLS[name] + i
            return cols[0:n, c:c + 1]

        def row(name):
            lo, hi = ROWS[name]
            return rows[:, lo:hi]

        w_in = a["w_in"][0].rearrange("(t p) n -> p t n", p=P)

        def mat(name):
            return a[name][0].rearrange("(t p) n -> p t n", p=P)

        w_out, w_om = mat("w_out"), mat("w_o_mem")
        chunks = [("mk", mat("w_k_mem"), 2, [("mk", j) for j in range(MT)]), ("mv", mat("w_v_mem"), 2, [("mv", j) for j in range(MT)]),
                  ("v", w_in[:, :, 0:512], 2, [("u", c) for c in range(4)]),
                  ("g1", w_in[:, :, 512:1024], 2, [("u", c) for c in range(4, 8)]),
                  ("g2", w_in[:, :, 1024:1536], 2, [("u", c) for c in range(8, 12)]),
                  ("q", w_in[:, :, 1536:2048], 2, [("q", i) for i in range(TT)]),
                  ("kv", w_in[:, :, 2048:2304], 4, [("kv", i) for i in range(TT)]),
                  ("wo0", w_out[:, :, 0:512], 2, [("wout", 0, i) for i in range(TT)]),
                  ("wo1", w_out[:, :, 512:1024], 2, [("wout", 1, i) for i in range(TT)]),
                  ("wq", mat("w_q_mem"), 2, [("mq", i) for i in range(TT)]),
                  ("wom0", w_om[:, :, 0:512], 2, [("wom", 0, i) for i in range(TT)]),
                  ("wom1", w_om[:, :, 512:1024], 2, [("wom", 1, i) for i in range(TT)])]
        pieces = [(name, k0, nk, src[:, k0:k0 + nk, :], jobs_) for name, src, nk, jobs_ in chunks
                  for k0 in range(0, src.shape[1], nk)]
        first_piece, last_piece = {}, {}
        for n, piece in enumerate(pieces):
            first_piece.setdefault(piece[0], n)
            last_piece[piece[0]] = n

        def wait_used(eng, n):
            name, jobs_ = pieces[n][0], pieces[n][4]
            if last_piece[name] == n:
                wait_filled(eng, jobs_[-1])
            else:
                eng.wait_ge(ring_used, sum(last_piece[p[0]] != m for m, p in enumerate(pieces[:n + 1])))

        def piece_view(buf, n):
            return buf[n % NSLOT][:].rearrange("p (t n) -> p t n", t=pieces[n][2])

        splits = [("memT", j) for j in range(KT // 2)] + [("hT", 0, k) for k in range(KT)]
        splits += [("yT", k) for k in range(CT)] + [("hT", 1, k) for k in range(KT)] + [("mo", h) for h in range(MH)]

        wg_v = a["w_gate"][0].rearrange("e (t p) n -> p e t n", p=P)
        wu_v = a["w_up"][0].rearrange("e (t p) n -> p e t n", p=P)
        wd_v = a["w_down"][0].rearrange("e (t p) n -> p e t n", p=P)

        NSEQ = TT * NQ
        MSEQ = TT * 2
        block = ctx.enter_context(nc.Block())

        @block.sync
        def _(sp_):
            def load_piece(n):
                if n >= NSLOT:
                    wait_used(sp_, n - NSLOT)
                sp_.dma_start(piece_view(w_raw, n), pieces[n][3]).then_inc(ring_ld[n % NSLOT], 16)

            sp_.dma_start(cols[:], a["cols"]).then_inc(ld["cols"], 16)
            sp_.dma_start(zemb[:], a["zemb"]).then_inc(ld["zemb"], 16)
            sp_.dma_start(w1[:], a["filt_w1"][0]).then_inc(ld["w12"], 16)
            sp_.dma_start(w2[:], a["filt_w2"][0]).then_inc(ld["w12"], 16)
            x_src = a["x"][0].rearrange("(i p) d -> p i d", p=P)
            sp_.dma_start(ident[:], a["mats"][:, 0, :]).then_inc(ld["ident"], 16)
            sp_.dma_start(mem_raw[:], a["mem"][0].rearrange("(j p) d -> p j d", p=P)).then_inc(ld["mem"], 16)
            for n in range(NSLOT):
                load_piece(n)
            for i in range(TT):
                sp_.dma_start(x_in[:, i, :], x_src[:, i, :]).then_inc(ld["x"], 16)
            sp_.dma_start(w3[:], a["filt_w3"][0]).then_inc(ld["w3"], 16)
            sp_.dma_start(decay[:], a["decay"]).then_inc(ld["decay"], 16)
            for n, m in ((1, ones), (2, blk), (3, tri)):
                sp_.dma_start(m[:], a["mats"][:, n, :]).then_inc(ld["mats"], 16)
            load_piece(NSLOT)
            sp_.dma_start(dft[:], a["dft"]).then_inc(ld["dft"], 16)
            sp_.dma_start(rows[:], a["rows"]).then_inc(ld["rows"], 16)
            sp_.dma_start(rope[:], a["rope"]).then_inc(ld["rope"], 16)
            sp_.dma_start(idft[:], a["idft"]).then_inc(ld["idft"], 16)
            for n in range(NSLOT + 1, len(pieces)):
                load_piece(n)
                if n == last_piece["kv"] + NSLOT:
                    wait_freed(sp_, ("inv", 1, CT - 1))
                    sp_.wait_ge(s_z, 2 * CT)
                    for i in range(TT):
                        sp_.dma_start(x2[:, i, :], x_src[:, i, :]).then_inc(ld["x2"], 16)
            views = [wg_v, wu_v, wd_v]

            def slot_view(s):
                return slot[s][:].rearrange("p (t n) -> p t n", t=(8, 8, 4)[s % 3])

            wait_freed(sp_, ("mk", MT - 1))
            wait_freed(sp_, ("mv", MT - 1))
            wait_freed(sp_, ("mo", MH - 1))
            wait_used(sp_, len(pieces) - 1)
            sp_.dma_start(wr[:], a["w_router"]).then_inc(ld["wr"], 16)
            sp_.dma_start(iota[:], a["iota"]).then_inc(ld["iota"], 16)
            sp_.dma_start(g_moe[:], a["g_moe"]).then_inc(ld["g_moe"], 16)
            for s in range(3):
                sp_.dma_start(slot_view(s), views[s][:, 0]).then_inc(w_ld[s], 16)
            wait_freed(sp_, ("router",))
            sp_.wait_ge(s_store, 16 * TT)
            for s in range(3, 5):
                sp_.dma_start(slot_view(s), views[s - 3][:, 1]).then_inc(w_ld[s], 16)
            sp_.wait_ge(s_gath[1], 16)
            sp_.dma_start(slot_view(5), views[2][:, 1]).then_inc(w_ld[5], 16)
            sp_.wait_ge(s_tab, 1)
            nb = sp_.value_load(e_tab[0:1, 31:32], min_val=0, max_val=MAXB - NE) + NE

            def expert_load(b, q, c):
                e = sp_.value_load(e_tab[0:1, bass.ds(b, 1)], min_val=0, max_val=NE - 1)
                sp_.wait_ge(s_used, (count(b - 2, 3), count(b - 2, 7), count(b - 1, 11))[c])
                sp_.sem_inc(waited_sp, 1)
                s = 3 * q + c
                sp_.dma_start(slot_view(s), views[c][:, bass.ds(e, 1)].rearrange("p e t n -> p (e t) n"))\
                    .then_inc(w_ld[s], 16)

            for b, q, c in ((2, 0, 0), (2, 0, 1), (3, 1, 0), (3, 1, 1), (2, 0, 2)):
                expert_load(b, q, c)
            with sp_.Fori(4, nb, 2) as b:
                for q in range(2):
                    expert_load(b + q, q, 0)
                    expert_load(b + q, q, 1)
                    expert_load(b + q - 1, 1 - q, 2)
            expert_load(nb - 1, 1, 2)
            sp_.wait_ge(s_used, count(nb, 3))
            sp_.sem_inc(waited_sp, 1)
            for q in range(2):
                sp_.wait_ge(s_sc[q], nb * 8)
            for i in range(TT):
                for r in range(2):
                    sp_.dma_start(y_back[:, r, i, :], y_dram[r * T + i * P:r * T + (i + 1) * P, :])\
                        .then_inc(ld_back[i], 16)
            for i in range(TT):
                sp_.wait_ge(s_fin, 2 * (i + 1))
                sp_.dma_start(out[0, i * P:(i + 1) * P, :], x2[:, i, :]).then_inc(s_out, 16)
            sp_.wait_ge(s_out, 16 * TT)

        @block.gpsimd
        def _(pool):
            steps = [0]

            def link(ins):
                steps[0] += 1
                ins.then_inc(pchain, 1)
                pool.wait_ge(pchain, steps[0])

            def filter_parts(o, t):
                wait_freed(pool, ("filt", o, t, 0))
                wait_freed(pool, ("filt", o, t, 1))
                fwd, bwd = fb[t % 2][:, 0, :], fb[t % 2][:, 1, :]
                pool.tensor_tensor(sum_diff[o][:, 0, t, :], fwd, bwd, ALU.add)
                pool.tensor_tensor(sum_diff[o][:, 1, t, :], fwd, bwd, ALU.subtract).then_inc(s_spdm, 1)

            def spec_parts(o, f):
                pool.wait_ge(s_ke, 2 * o + f + 1)
                for c in range(2):
                    pool.tensor_tensor(spec[:, o, f, c, :], ep[:, c, :], ep[:, 2 + c, :], ALU.add)
                    last = pool.tensor_tensor(spec[:, o, f, 2 + c, :], ep[:, c, :], ep[:, 2 + c, :], ALU.subtract)
                last.then_inc(s_kab, 1)

            for t in range(4):
                filter_parts(0, t)
            for f in range(2):
                spec_parts(0, f)
                filter_parts(1, 2 * f)
                filter_parts(1, 2 * f + 1)
            for f in range(2):
                spec_parts(1, f)
            for o in range(2):
                for f in range(2):
                    n = 2 * o + f
                    for c in range(4):
                        wait_freed(pool, ("fwd", o, f, c))
                    if n:
                        pool.wait_ge(s_ab, n)
                    pool.tensor_tensor(ab[:, 0, :], ep[:, 0, :], ep[:, 2, :], ALU.add)
                    pool.tensor_tensor(ab[:, 1, :], ep[:, 1, :], ep[:, 3, :], ALU.add).then_inc(s_a, 1)
                    pool.wait_ge(s_a, n + 1)
                    pool.wait_ge(s_b, n + 1)
                    kre, kim = spec[:, o, f, 2, :], spec[:, o, f, 3, :]
                    pool.tensor_tensor(ep[:, 1, :], ab[:, 2, :], kre, ALU.mult)
                    pool.tensor_tensor(ep[:, 3, :], ab[:, 3, :], kim, ALU.mult)
                    pool.tensor_tensor(tmp[:, 0, :], ab[:, 2, :], kim, ALU.mult)
                    pool.tensor_tensor(tmp[:, 1, :], ab[:, 3, :], kre, ALU.mult).then_inc(s_pb, 1)
            for i in range(TT):
                pool.wait_ge(s_xn, TT + 3 + i + 1)
                pool.dma_start(xn_dram[i * P:(i + 1) * P, :], xn[:, i, :]).then_inc(s_store, 16)
            pool.wait_ge(s_rec, 1)
            pool.wait_ge(s_store, 16 * TT)
            pool.wait_ge(s_tab, 1)

            def meta(b, q):
                if not isinstance(b, int) or b >= 2:
                    pool.wait_ge(s_oa, b - 1)
                    pool.wait_ge(s_sc[q], (b - q) * 8)
                pool.tensor_copy(meta_i[:, q, 0:1], rec_sb[:, bass.ds(b, 1), 1:2].rearrange("p b c -> p (b c)"))
                pool.tensor_copy(meta_g[:, q, :], rec_sb[:, bass.ds(b, 1), 2:3].rearrange("p b c -> p (b c)"))\
                    .then_inc(s_meta, 1)

            def gather(b, q):
                if not isinstance(b, int) or b >= 2:
                    pool.wait_ge(s_t, 2 * b - 2)
                pool.tensor_copy(gather_i[:, q, :], rec_sb[:, bass.ds(b, 1), 0:1].rearrange("p b c -> p (b c)"))\
                    .then_inc(s_gi, 1)
                pool.wait_ge(s_gi, b + 1)
                pool.sem_inc(waited_pool, 1)
                pool.indirect_dma_start(hg[q][:], None, xn_dram,
                                        bass.IndirectOffsetOnAxis(ap=gather_i[:, q, :], axis=0)).then_inc(s_gath[q], 16)

            def scatter(b, q):
                pool.wait_ge(s_oa, b + 1)
                pool.wait_ge(s_meta, b + 1)
                if not isinstance(b, int) or b >= 1:
                    pool.wait_ge(s_sc[1 - q], (b + q) * 8)
                pool.sem_inc(waited_pool, 1)
                pool.indirect_dma_start(y_dram, bass.IndirectOffsetOnAxis(ap=meta_i[:, q, 0:1], axis=0),
                                        eo[q][:], None).then_inc(s_sc[q], 16)

            gather(0, 0)
            gather(1, 1)
            meta(0, 0)
            gather(2, 0)
            meta(1, 1)
            gather(3, 1)
            scatter(0, 0)
            nb = pool.value_load(e_tab[0:1, 31:32], min_val=0, max_val=MAXB - NE) + NE
            with pool.Fori(2, nb, 2) as b:
                meta(b, 0)
                gather(b + 2, 0)
                scatter(b - 1, 1)
                meta(b + 1, 1)
                gather(b + 3, 1)
                scatter(b, 0)
            scatter(nb - 1, 1)
            for q in range(2):
                pool.wait_ge(s_gath[q], (nb + 2) * 8)

        @block.scalar
        def _(act):
            steps = [0]

            def link(ins):
                steps[0] += 1
                ins.then_inc(achain, 1)
                act.wait_ge(achain, steps[0])

            def sine(j, dst):
                act.wait_ge(s_arg, j + 1)
                act.activation(dst[:], mlp_arg[:], ACT.Sin).then_inc(s_sin, 1)

            fb_flat = at("junk", 192, [P, D])[:]

            eps = small[:, 395:396]

            def rms(src, first, n, count):
                for i in range(n):
                    act.activation(fb_flat, src[:, i, :], ACT.Square, accum_out=small[:, first + i:first + i + 1])\
                        .then_inc(s_sq, 1)
                    act.wait_ge(s_sq, count - n + i + 1)
                act.activation(small[:, 16 + first:16 + first + n], small[:, first:first + n], ACT.Sqrt,
                               bias=eps, scale=1.0 / D).then_inc(s_rms, 1)

            act.wait_ge(ld["cols"], 16)
            link(act.activation(eps, col("token"), ACT.Copy, scale=0.0, bias=EPS))
            def abs_pair(o, t):
                wait_freed(act, ("filt", o, t, 0))
                wait_freed(act, ("filt", o, t, 1))
                if 4 * o + t >= 2:
                    act.wait_ge(s_l1, 4 * o + t - 1)
                act.activation(fabs[t % 2][:], fb[t % 2][:], ACT.Abs).then_inc(s_abs, 1)

            def head_rms(first, n, width, count):
                act.wait_ge(s_ms, count)
                act.activation(small[:, first:first + n], small[:, first:first + n], ACT.Sqrt, bias=eps,
                               scale=1.0 / width).then_inc(s_hrms, 1)

            def weight_hi(lo, n):
                for m in range(lo, lo + n):
                    act.wait_ge(ring_ld[m % NSLOT], 16 * (m // NSLOT + 1))
                    if m >= NSLOT:
                        wait_used(act, m - NSLOT)
                    act.activation(w_hi[m % NSLOT][:], w_raw[m % NSLOT][:], ACT.Copy).then_inc(s_wh, 1)

            def split_hi(job, dst, scale=1.0):
                wait_filled(act, job)
                act.activation(dst, bank(job)[:], ACT.Copy, scale=scale).then_inc(s_hi, 1)

            def centre_tap(lo):
                for c in range(lo, lo + 4):
                    job = ("u", c)
                    wait_filled(act, job)
                    act.activation(u[:, c, :].rearrange("p (two m) -> p two m", two=2),
                                   bank(job)[:].rearrange("p (m two) -> p two m", two=2), ACT.Identity,
                                   bias=col("short_b", c), scale=col("short_w", 12 + c)).then_inc(s_conv, 1)

            def evac(key, n, dst, scale=None):
                for j in range(n):
                    wait_filled(act, (key, j))
                    out_ = dst(j)
                    by = 1.0 if scale is None else small[:, scale + j:scale + j + 1]
                    free(act.activation(out_, bank((key, j))[:, 0:out_.shape[1]], ACT.Copy, scale=by), (key, j))

            def evac_z(o):
                for k in range(4):
                    job = ("zT", o, k)
                    wait_filled(act, job)
                    if o == 0 and k == 0:
                        wait_freed(act, ("filt", 1, 3, 1))
                    if o == 1 and k == 0:
                        wait_filled(act, ("fwd", 0, 1, 3))
                    free(act.activation(zt[:, k, :], bank(job)[:], ACT.Copy), job)

            def evac_fwd(o):
                for f in range(2):
                    for c in range(4):
                        job = ("fwd", o, f, c)
                        wait_filled(act, job)
                        if c == 0:
                            if o == 0 and f == 0:
                                act.wait_ge(s_kab, 4)
                            else:
                                act.wait_ge(s_ab, 2 * o + f)
                        free(act.activation(ep[:, c, :], bank(job)[:], ACT.Copy), job)

            for j in range(KT // 2):
                job = ("memT", j)
                wait_filled(act, job)
                for c in range(2):
                    k = 2 * j + c
                    ins = act.activation(memT_hi[:, k, :], bank(job)[:, c * NM:(c + 1) * NM], ACT.Copy, scale=col("norm_mem", k))
                ins.then_inc(s_hi, 1)
            sine(0, a1)
            weight_hi(0, 3)
            act.wait_ge(ld["x"], 16 * TT)
            rms(x_in, 4, TT, TT)
            act.wait_ge(ld["mem"], 16)
            rms(mem_raw, 0, MT, TT + MT)
            sine(1, a2)
            weight_hi(3, 1)
            for k in range(4):
                split_hi(("hT", 0, k), hT_hi[:, k, :], col("norm_mix", k))
            act.wait_ge(s_xn, TT + 1)
            evac("mk", MT, lambda j: mk[:, j, :], 16)
            for k in range(4, KT):
                split_hi(("hT", 0, k), hT_hi[:, k, :], col("norm_mix", k))
            weight_hi(4, 3)
            abs_pair(0, 0)
            abs_pair(0, 1)
            weight_hi(7, 1)
            abs_pair(0, 2)
            abs_pair(0, 3)
            evac("mv", MT, lambda j: mv[:, j, :], 16)
            weight_hi(8, 3)
            abs_pair(1, 0)
            abs_pair(1, 1)
            abs_pair(1, 2)
            weight_hi(11, 1)
            abs_pair(1, 3)
            weight_hi(12, 2)
            centre_tap(0)
            weight_hi(14, 1)
            evac_z(0)
            weight_hi(15, 2)
            act.wait_ge(ld["rows"], 16)
            act.activation(row("gq"), row("gq"), ACT.Copy, scale=HD ** -0.5).then_inc(s_gq, 1)
            weight_hi(17, 1)
            centre_tap(4)
            weight_hi(18, 1)

            evac_fwd(0)
            weight_hi(19, 3)
            centre_tap(8)
            weight_hi(22, 1)
            evac_z(1)
            evac_fwd(1)
            head_rms(40, MT * MH, MHD, 1)
            weight_hi(23, 3)
            for i in range(TT):
                job = ("q", i)
                wait_filled(act, job)
                if i == 0:
                    wait_filled(act, ("fwd", 1, 1, 3))
                act.activation(q_sq[:, i, :], bank(job)[:], ACT.Square).then_inc(s_qsq, 1)
                free(act.activation(qkv[:, i, 0:512], bank(job)[:], ACT.Copy), job)
            weight_hi(26, 1)
            evac("kv", TT, lambda i: qkv[:, i, 512:768])
            weight_hi(27, 1)
            head_rms(230, TT * NKV, HD, 2)
            head_rms(240, TT * NQ, HD, 3)
            weight_hi(28, 1)
            act.wait_ge(s_rope, 4)
            for w in range(2):
                ins = act.activation(kdup[:, :, :, w, :], qkv[:, :, 512:640].rearrange("p i (g d) -> p i g d", d=HD), ACT.Copy)
            ins.then_inc(s_kdup, 1)
            for j in range(2):
                wait_filled(act, ("mkT", j))
                free(act.activation(mkT[:, 2 * j:2 * j + 2, :].rearrange("p h m -> p (h m)"), bank(("mkT", j))[:], ACT.Copy),
                     ("mkT", j))
            for c in range(CT):
                act.wait_ge(s_z, CT + c + 1)
                act.activation(y_sq[:, c, :], u[:, c, :], ACT.Square).then_inc(s_ysq, 1)
            for p in range(NQ // 2):
                wait_filled(act, ("qT", p))
                free(act.activation(qT[:, p, :], bank(("qT", p))[:], ACT.Copy), ("qT", p))
            for g in range(NKV):
                wait_filled(act, ("kT", g))
                free(act.activation(kT[:, g, :], bank(("kT", g))[:], ACT.Copy), ("kT", g))

            for c in range(CT):
                job = ("hn", c)
                wait_filled(act, job)
                free(act.activation(y_rs[:, c, :], bank(job)[:], ACT.Identity, bias=eps, scale=1.0 / HD), job)

            def hyena_roots():
                for c in range(CT):
                    wait_freed(act, ("hn", c))
                act.activation(y_rs[:], y_rs[:], ACT.Sqrt).then_inc(s_hroot, 1)

            def gqa_exp(s):
                act.wait_ge(s_max, s + 1)
                if s >= NPR:
                    wait_filled(act, ("PT", s - NPR))
                c0 = 240 + s
                free(act.activation(pr[:, s % NPR, :], bank(("S", s))[:], ACT.Exp, bias=small[:, 100 + s:101 + s],
                                    scale=small[:, c0:c0 + 1],
                                    accum_out=small[:, 140 + s:141 + s]), ("S", s))

            def gqa_pt(s):
                wait_filled(act, ("PT", s))
                if s >= NPR:
                    act.wait_ge(s_asq, s - NPR + 1)
                free(act.activation(pT[:, s % NPR, :], bank(("PT", s))[:], ACT.Copy), ("PT", s))

            for s in range(AHEAD):
                gqa_exp(s)
            for s in range(NSEQ):
                gqa_pt(s)
                if s + AHEAD < NSEQ:
                    gqa_exp(s + AHEAD)
                if s == HN_STEP + 1:
                    hyena_roots()
            head_rms(340, TT * NQ, HD, 4)
            for k in range(CT):
                split_hi(("yT", k), yT_hi[:, CT + k, :], col("attn_norm", k))
            weight_hi(29, 6)

            def x_norm_squares(first, jobkey, count):
                for i in range(TT):
                    wait_freed(act, (jobkey, 0, i))
                    wait_freed(act, (jobkey, 1, i))
                    act.activation(fb_flat, x2[:, i, :], ACT.Square, accum_out=small[:, first + i:first + i + 1])\
                        .then_inc(s_sq, 1)
                    act.wait_ge(s_sq, count + i + 1)
                    act.activation(small[:, 16 + first + i:17 + first + i], small[:, first + i:first + i + 1], ACT.Sqrt,
                                   bias=eps, scale=1.0 / D).then_inc(s_rms, 1)

            weight_hi(35, 2)
            for k in range(KT):
                split_hi(("hT", 1, k), hT_hi[:, k, :], col("norm_xattn", k))
            x_norm_squares(8, "wout", 6)
            weight_hi(37, 3)
            act.wait_ge(s_xn, TT + 2)
            evac("mq", TT, lambda i: mq[:, i, :], 24)
            weight_hi(40, 1)
            for h in range(MH):
                wait_filled(act, ("mqT", h))
                free(act.activation(mqT[:, h, :], bank(("mqT", h))[:], ACT.Copy, scale=col("gmq")), ("mqT", h))

            head_rms(40, TT * MH, MHD, 5)
            act.wait_ge(s_mqn, 1)

            def mem_exp(s):
                i, hp = s // 2, s % 2
                act.wait_ge(s_max, NSEQ + s + 1)
                if s >= NPR:
                    wait_filled(act, ("MPT", s - NPR))
                for c in range(2):
                    ins = act.activation(pr[:, s % NPR, c * NM:(c + 1) * NM], bank(("MS", s))[:, c * NM:(c + 1) * NM], ACT.Exp,
                                         bias=small[:, 180 + 2 * s + c:181 + 2 * s + c],
                                         scale=small[:, 40 + MH * i + 2 * hp + c:41 + MH * i + 2 * hp + c],
                                         accum_out=small[:, 200 + 2 * s + c:201 + 2 * s + c])
                free(ins, ("MS", s))

            def mem_pt(s):
                i, hp = s // 2, s % 2
                job = ("MPT", s)
                wait_filled(act, job)
                free(act.activation(mpT[:, 2 * hp:2 * hp + 2, :, i * P:(i + 1) * P],
                                    bank(job)[:].rearrange("p (h t n) -> p h t n", h=2, t=MT), ACT.Copy), job)

            for s in range(MAHEAD):
                mem_exp(s)
            for s in range(MSEQ):
                mem_pt(s)
                if s + MAHEAD < MSEQ:
                    mem_exp(s + MAHEAD)
            for h in range(MH):
                split_hi(("mo", h), moT_hi[:, h, :])
            weight_hi(41, 1)
            for k in range(0, KT, 2):
                wait_filled(act, ("hT", 2, k))
                free(act.activation(hT[:, k, :], bank(("hT", 2, k))[:], ACT.Copy, scale=col("norm_moe", k)), ("hT", 2, k))
            x_norm_squares(12, "wom", 10)
            act.wait_ge(s_r1, 1)
            act.activation(rt[:, 100:116], rt[:, 84:100], ACT.Exp).then_inc(s_r2, 1)
            act.wait_ge(s_r3, 1)
            act.activation(rt[:, 204:208], rt[:, 200:204], ACT.Exp).then_inc(s_r4, 1)

            def hi_part(b, slot_, part, j):
                if not isinstance(b, int) or count(b, j) > NHI:
                    act.wait_ge(s_used, count(b, j) - NHI)
                act.activation(e_hi[buffer(b, j)][:], slot[slot_][:, 1024 * part:1024 * (part + 1)], ACT.Copy).then_inc(s_ehi, 1)

            def hi_parts(b, q, lo, hi):
                for j in range(lo, hi):
                    kind, part = j // 4, j % 4
                    slot_ = 3 * q + kind if kind < 2 else 3 * (1 - q) + 2
                    act.wait_ge(w_ld[slot_], (b - q) * 8 + 16 if kind < 2 else (b + q) * 8)
                    hi_part(b, slot_, part, j)

            def rows_hi(b):
                act.wait_ge(s_t, 2 * b + 2)
                for half in range(2):
                    ins = act.activation(hgT_hi[:, 512 * half:512 * (half + 1)], banks[half][:], ACT.Copy)
                ins.then_inc(s_rhi, 1)

            def silu(b):
                act.wait_ge(s_used, count(b, 3))
                if not isinstance(b, int) or b >= 1:
                    act.wait_ge(s_mul, b)
                act.activation(sg[:], banks[2][:], ACT.Silu).then_inc(s_silu, 1)

            def actT_hi(b):
                act.wait_ge(s_at, b + 1)
                act.activation(gaT_hi[:], banks[4][:], ACT.Copy).then_inc(s_ahi, 1)

            def out_evac(b, q, used):
                act.wait_ge(s_used, used)
                act.wait_ge(s_meta, b + 1)
                act.activation(eo[q][:, 0:512], banks[5][:], ACT.Copy, scale=meta_g[:, q, :])
                act.activation(eo[q][:, 512:D], banks[6][:], ACT.Copy, scale=meta_g[:, q, :]).then_inc(s_oa, 1)

            def turn(b, q):
                if not isinstance(b, int) or b == 0:
                    hi_parts(b, q, 0, 4)
                if isinstance(b, int) and b == 0:
                    rows_hi(0)
                if not isinstance(b, int) or b >= 2:
                    out_evac(b - 2, q, count(b - 1, 11))
                if not isinstance(b, int) or b >= 1:
                    actT_hi(b - 1)
                first = isinstance(b, int) and b == 0
                hi_parts(b, q, 4, 8 if first else 9)
                silu(b)
                if first:
                    hi_parts(1, 1, 0, 4)
                else:
                    hi_parts(b, q, 9, PIECES)
                rows_hi(b + 1)

            turn(0, 0)
            turn(1, 1)
            act.wait_ge(s_tab, 1)
            nb = act.value_load(e_tab[0:1, 31:32], min_val=0, max_val=MAXB - NE) + NE
            with act.Fori(2, nb, 2) as b:
                turn(b, 0)
                turn(b + 1, 1)
            out_evac(nb - 2, 0, count(nb - 1, 11))
            actT_hi(nb - 1)
            act.wait_ge(w_ld[5], nb * 8)
            for j in range(4):
                hi_part(nb, 5, j, j)
            out_evac(nb - 1, 1, count(nb, 3))

        @block.vector
        def _(dve):
            steps = [0]

            def link(ins):
                steps[0] += 1
                ins.then_inc(dchain, 1)
                dve.wait_ge(dchain, steps[0])

            def range_reduce(j):
                job = ("mlp", j)
                wait_filled(dve, job)
                if j:
                    dve.wait_ge(s_sin, 1)
                link(dve.tensor_scalar(mlp_arg[:], bank(job)[0:FF, :], col("b1" if j == 0 else "b2", 0, FF),
                                       col("freq", j, FF), ALU.add, ALU.mult))
                link(dve.tensor_scalar(mlp_k[:], mlp_arg[:], 1.0 / (2 * np.pi), 12582912.0, ALU.mult, ALU.add))
                link(dve.tensor_scalar(mlp_k[:], mlp_k[:], 12582912.0, None, ALU.subtract))
                hi = 6.28125
                link(dve.scalar_tensor_tensor(mlp_arg[:], mlp_k[:], -hi, mlp_arg[:], ALU.mult, ALU.add))
                link(dve.scalar_tensor_tensor(mlp_arg[:], mlp_k[:], -(2 * np.pi - hi), mlp_arg[:], ALU.mult, ALU.add))
                dve.tensor_scalar(mlp_arg[:], mlp_arg[:], float(np.float32(-3.1415925)), float(np.float32(3.1415925)),
                                  ALU.max, ALU.min).then_inc(s_arg, 1)

            dve.wait_ge(ld["cols"], 16)
            def weight_lo(lo, n):
                for m in range(lo, lo + n):
                    dve.wait_ge(s_wh, m + 1)
                    slot_ = m % NSLOT
                    dve.tensor_tensor(w_lo[slot_][:], w_raw[slot_][:], w_hi[slot_][:].bitcast(F32), ALU.subtract)\
                        .then_inc(s_wl, 1)

            def split_lo(job, dst, hi, scale):
                dve.wait_ge(s_hi, splits.index(job) + 1)
                free(dve.scalar_tensor_tensor(dst, bank(job)[:], scale, hi.bitcast(F32), ALU.mult, ALU.subtract), job)

            range_reduce(0)
            dve.wait_ge(s_arg, 1)
            free(dve.tensor_copy(small[0:1, 399:400], cols[0:1, 0:1]), ("mlp", 0))
            for j in range(KT // 2):
                job = ("memT", j)
                dve.wait_ge(s_hi, splits.index(job) + 1)
                for c in range(2):
                    k = 2 * j + c
                    ins = dve.scalar_tensor_tensor(memT_lo[:, k, :], bank(job)[:, c * NM:(c + 1) * NM], col("norm_mem", k),
                                                   memT_hi[:, k, :].bitcast(F32), ALU.mult, ALU.subtract)
                free(ins, job)
            weight_lo(0, 3)
            range_reduce(1)
            dve.wait_ge(s_rms, 1)
            link(dve.reciprocal(small[:, 20:24], small[:, 20:24]))
            for i in range(TT):
                dve.tensor_scalar(x_in[:, i, :], x_in[:, i, :], small[:, 20 + i:21 + i], None, ALU.mult).then_inc(s_xn, 1)
            dve.wait_ge(s_rms, 2)
            dve.reciprocal(small[:, 16:18], small[:, 16:18]).then_inc(s_xn, 1)
            dve.wait_ge(s_arg, 2)
            free(dve.tensor_copy(small[0:1, 399:400], cols[0:1, 0:1]), ("mlp", 1))
            weight_lo(3, 1)
            for k in range(KT):
                split_lo(("hT", 0, k), hT_lo[:, k, :], hT_hi[:, k, :], col("norm_mix", k))
            weight_lo(4, 3)
            dve.wait_ge(ld["decay"], 16)

            def filters(o, t):
                fwd, bwd = ("filt", o, t, 0), ("filt", o, t, 1)
                if 4 * o + t >= 2:
                    dve.wait_ge(s_spdm, 4 * o + t - 1)
                    dve.wait_ge(s_abs, 4 * o + t - 1)
                if o == 0 and t == 1:
                    dve.wait_ge(s_hi, KT // 2)
                wait_filled(dve, fwd)
                free(dve.tensor_tensor(fb[t % 2][:, 0, :], bank(fwd)[:], decay[:, t, :], ALU.mult), fwd)
                wait_filled(dve, bwd)
                mask = col("not_first") if t == 0 else 1.0
                free(dve.scalar_tensor_tensor(fb[t % 2][:, 1, :], bank(bwd)[:], mask, decay[:, t, :], ALU.mult, ALU.mult), bwd)

            def l1_add(o, t):
                dve.wait_ge(s_abs, 4 * o + t + 1)
                fwd, bwd = fabs[t % 2][:, 0, :], fabs[t % 2][:, 1, :]
                if t == 0:
                    if o == 1:
                        wait_filled(dve, ("l1", 0))
                    dve.tensor_tensor(l1sum[:], fwd, bwd, ALU.add).then_inc(s_l1, 1)
                else:
                    link(dve.tensor_tensor(l1sum[:], l1sum[:], fwd, ALU.add))
                    dve.tensor_tensor(l1sum[:], l1sum[:], bwd, ALU.add).then_inc(s_l1, 1)
                dve.wait_ge(s_l1, 4 * o + t + 1)

            def l1_norm(o):
                wait_filled(dve, ("l1", o))
                if o == 1:
                    dve.wait_ge(s_ke, 2)
                free(dve.tensor_scalar(rnorm[:], bank(("l1", o))[:], EPS, None, ALU.add), ("l1", o))
                wait_freed(dve, ("l1", o))
                dve.reciprocal(rnorm[:], rnorm[:]).then_inc(s_rn, 1)
                dve.wait_ge(s_rn, o + 1)

            def normed_spec(o, f):
                if 2 * o + f:
                    dve.wait_ge(s_kab, 2 * o + f)
                for c in range(4):
                    job = ("spec", o, f, c)
                    wait_filled(dve, job)
                    free(dve.tensor_tensor(ep[:, c, :], bank(job)[:], rnorm[:], ALU.mult), job)
                wait_freed(dve, ("spec", o, f, 3))
                dve.tensor_copy(small[0:1, 398:399], cols[0:1, 0:1]).then_inc(s_ke, 1)

            def outer_taps(lo):
                for c in range(lo, lo + 4):
                    job = ("u", c)
                    dve.wait_ge(s_conv, c + 1)
                    pe_, po = bank(job)[:, 0::2], bank(job)[:, 1::2]
                    ue, uo = u[:, c, 0:HALF], u[:, c, HALF:T]
                    w_prev, w_next = col("short_w", c), col("short_w", 24 + c)
                    dve.scalar_tensor_tensor(ue, po, w_next, ue, ALU.mult, ALU.add)
                    link(dve.scalar_tensor_tensor(uo, pe_, w_prev, uo, ALU.mult, ALU.add))
                    dve.scalar_tensor_tensor(ue[:, 1:HALF], po[:, 0:HALF - 1], w_prev, ue[:, 1:HALF], ALU.mult, ALU.add)
                    free(dve.scalar_tensor_tensor(uo[:, 0:HALF - 1], pe_[:, 1:HALF], w_next, uo[:, 0:HALF - 1],
                                                  ALU.mult, ALU.add), job)

            filters(0, 0)
            filters(0, 1)
            for t in range(4):
                l1_add(0, t)
                if t < 2:
                    filters(0, t + 2)
                if t == 1:
                    weight_lo(7, 1)
            l1_norm(0)
            weight_lo(8, 3)
            normed_spec(0, 0)
            filters(1, 0)
            filters(1, 1)
            l1_add(1, 0)
            normed_spec(0, 1)
            filters(1, 2)
            l1_add(1, 1)
            weight_lo(11, 1)
            filters(1, 3)
            l1_add(1, 2)
            l1_add(1, 3)
            weight_lo(12, 2)
            l1_norm(1)
            outer_taps(0)
            weight_lo(14, 1)
            normed_spec(1, 0)
            normed_spec(1, 1)
            weight_lo(15, 3)

            def head_sums(x3, sq3, ss):
                link(dve.tensor_tensor(sq3, x3, x3, ALU.mult))
                return dve.tensor_reduce(ss, sq3, AX.X, ALU.add)

            for j in range(MT):
                wait_freed(dve, ("mk", j))
                ins = head_sums(mk[:, j, :].rearrange("p (h d) -> p h d", d=MHD),
                                rope_tmp[:, 0:512].rearrange("p (h d) -> p h d", d=MHD), small[:, 40 + MH * j:44 + MH * j])
                if j < MT - 1:
                    link(ins)
            ins.then_inc(s_ms, 1)
            outer_taps(4)
            weight_lo(18, 1)

            def pointwise(o, f):
                n = 2 * o + f
                for c in range(4):
                    wait_freed(dve, ("fwd", o, f, c))
                if n == 0:
                    dve.wait_ge(s_kab, 4)
                if o == 1 and f == 0:
                    wait_filled(dve, ("inv", 0, CT - 1))
                dve.tensor_tensor(ab[:, 2, :], ep[:, 0, :], ep[:, 2, :], ALU.subtract)
                dve.tensor_tensor(ab[:, 3, :], ep[:, 1, :], ep[:, 3, :], ALU.subtract).then_inc(s_b, 1)
                dve.wait_ge(s_a, n + 1)
                kre, kim = spec[:, o, f, 0, :], spec[:, o, f, 1, :]
                are, aim = ab[:, 0, :], ab[:, 1, :]
                s_ = sd[:, f]
                dve.wait_ge(s_b, n + 1)
                dve.tensor_tensor(s_[:, 0, :], are, kre, ALU.mult)
                dve.tensor_tensor(s_[:, 1, :], aim, kim, ALU.mult)
                dve.tensor_tensor(s_[:, 2, :], are, kim, ALU.mult)
                link(dve.tensor_tensor(s_[:, 3, :], aim, kre, ALU.mult))
                dve.tensor_tensor(ep[:, 0, :], s_[:, 0, :], s_[:, 1, :], ALU.subtract)
                link(dve.tensor_tensor(ep[:, 2, :], s_[:, 2, :], s_[:, 3, :], ALU.add))
                dve.wait_ge(s_pb, n + 1)
                dve.tensor_tensor(ab[:, 0, :], ep[:, 1, :], ep[:, 3, :], ALU.subtract)
                link(dve.tensor_tensor(ab[:, 1, :], tmp[:, 0, :], tmp[:, 1, :], ALU.add))
                dve.tensor_tensor(s_[:, 0, :], ep[:, 0, :], ab[:, 0, :], ALU.add)
                dve.tensor_tensor(s_[:, 2, :], ep[:, 0, :], ab[:, 0, :], ALU.subtract)
                dve.tensor_tensor(s_[:, 1, :], ep[:, 2, :], ab[:, 1, :], ALU.add)
                dve.tensor_tensor(s_[:, 3, :], ep[:, 2, :], ab[:, 1, :], ALU.subtract).then_inc(s_ab, 1)

            def gated(o):
                for c in range(CT):
                    job = ("inv", o, c)
                    wait_filled(dve, job)
                    free(dve.scalar_tensor_tensor(u[:, c, :], u[:, c, :], col("skip", o * CT + c), bank(job)[:],
                                                  ALU.mult, ALU.add), job)
                    wait_freed(dve, job)
                    dve.tensor_tensor(u[:, c, :], u[:, c, :], u[:, CT * (o + 1) + c, :], ALU.mult).then_inc(s_z, 1)

            def qk(i):
                return qkv[:, i, 0:640].rearrange("p (h d) -> p h d", d=HD)

            def roped(i, keys_done):
                x3 = qk(i)[:, 0:NQ, :]
                t3 = rope_tmp[:, 0:NQ * HD].rearrange("p (h d) -> p h d", d=HD)
                link(dve.tensor_tensor(x3, x3, row("gq").unsqueeze(1).to_broadcast([P, NQ, HD]), ALU.mult))
                x5 = qkv[:, i, 0:NQ * HD].rearrange("p (h s w d) -> p h s w d", s=2, w=2, d=HD // 4)
                t5 = rope_tmp[:, 0:NQ * HD].rearrange("p (h s w d) -> p h s w d", s=2, w=2, d=HD // 4)
                sn = rope[:, 1, i, :].rearrange("p (s w d) -> p s w d", s=2, w=2)
                for w in range(2):
                    for s in range(2):
                        ins = dve.tensor_tensor(t5[:, :, s, w, :], x5[:, :, s, 1 - w, :],
                                                sn[:, s, w, :].unsqueeze(1).to_broadcast([P, NQ, HD // 4]), ALU.mult)
                link(ins)
                link(dve.tensor_tensor(x3, x3, rope[:, 0, i, :].unsqueeze(1).to_broadcast([P, NQ, HD]), ALU.mult))
                dve.tensor_tensor(x3, x3, t3, ALU.add).then_inc(s_rope, 1)
                dve.wait_ge(s_rope, i + 1 + keys_done)

            pointwise(0, 0)
            weight_lo(19, 1)
            pointwise(0, 1)
            weight_lo(20, 2)
            outer_taps(8)
            gated(0)
            weight_lo(22, 1)
            pointwise(1, 0)
            weight_lo(23, 1)
            pointwise(1, 1)
            weight_lo(24, 1)
            dve.wait_ge(ld["rows"], 16)
            dve.wait_ge(ld["rope"], 16)
            dve.wait_ge(s_gq, 1)
            dve.wait_ge(s_hrms, 1)
            link(dve.reciprocal(small[:, 40:48], small[:, 40:48]))
            for j in range(MT):
                x3 = mk[:, j, :].rearrange("p (h d) -> p h d", d=MHD)
                link(dve.tensor_tensor(x3, x3, small[:, 40 + MH * j:44 + MH * j].unsqueeze(2).to_broadcast([P, MH, MHD]), ALU.mult))
                dve.tensor_tensor(x3, x3, row("gmk").unsqueeze(1).to_broadcast([P, MH, MHD]), ALU.mult).then_inc(s_mkn, 1)
            weight_lo(25, 1)
            dve.wait_ge(s_ms, 1)

            def keys_roped():
                x4 = qkv[:, :, NQ * HD:(NQ + NKV) * HD].rearrange("p i (h d) -> p i h d", d=HD)
                x6 = qkv[:, :, NQ * HD:(NQ + NKV) * HD].rearrange("p i (h s w d) -> p i h s w d", s=2, w=2, d=HD // 4)
                t4 = rope_tmp[:, 0:512].rearrange("p (i h d) -> p i h d", i=TT, d=HD)
                t6 = rope_tmp[:, 0:512].rearrange("p (i h s w d) -> p i h s w d", i=TT, s=2, w=2, d=HD // 4)
                cs = rope[:, 0, :, :]
                sn = rope[:, 1, :, :].rearrange("p i (s w d) -> p i s w d", s=2, w=2)
                inv = small[:, 230:238].rearrange("p (i h) -> p i h", i=TT)
                link(dve.tensor_tensor(x4, x4, inv.unsqueeze(3).to_broadcast([P, TT, NKV, HD]), ALU.mult))
                link(dve.tensor_tensor(x4, x4, row("gk").unsqueeze(1).unsqueeze(1).to_broadcast([P, TT, NKV, HD]), ALU.mult))
                for w in range(2):
                    for s in range(2):
                        ins = dve.tensor_tensor(t6[:, :, :, s, w, :], x6[:, :, :, s, 1 - w, :],
                                                sn[:, :, s, w, :].unsqueeze(2).to_broadcast([P, TT, NKV, HD // 4]), ALU.mult)
                link(ins)
                link(dve.tensor_tensor(x4, x4, cs.unsqueeze(2).to_broadcast([P, TT, NKV, HD]), ALU.mult))
                dve.tensor_tensor(x4, x4, t4, ALU.add).then_inc(s_rope, 1)
                dve.wait_ge(s_rope, 4)

            dve.wait_ge(s_qsq, TT)
            for i in range(TT):
                wait_freed(dve, ("q", i))
            link(dve.tensor_reduce(small[:, 240:272], q_sq[:].rearrange("p i (h d) -> p (i h) d", d=HD), AX.X, ALU.add))
            weight_lo(26, 1)
            roped(0, 0)
            roped(1, 0)
            for i in range(TT):
                wait_freed(dve, ("kv", i))
            keys = qkv[:, :, NQ * HD:(NQ + NKV) * HD].rearrange("p i (h d) -> p i h d", d=HD)
            sq = rope_tmp[:, 0:512].rearrange("p (i h d) -> p i h d", i=TT, d=HD)
            link(dve.tensor_tensor(sq, keys, keys, ALU.mult))
            dve.tensor_reduce(small[:, 230:238], rope_tmp[:, 0:512].rearrange("p (h d) -> p h d", d=HD), AX.X, ALU.add)\
                .then_inc(s_ms, 1)
            dve.wait_ge(s_ms, 2)
            weight_lo(27, 1)
            roped(2, 0)
            dve.tensor_copy(small[0:1, 396:397], small[0:1, 240:241]).then_inc(s_ms, 1)
            dve.wait_ge(s_hrms, 2)
            link(dve.reciprocal(small[:, 230:238], small[:, 230:238]))
            keys_roped()
            roped(3, 1)
            dve.wait_ge(s_hrms, 3)
            dve.reciprocal(small[:, 240:272], small[:, 240:272]).then_inc(s_qinv, 1)
            gated(1)
            weight_lo(28, 1)
            def hyena_recip(n):
                c, piece = n // 4, y_rs[:, n // 4, (n % 4) * P:(n % 4 + 1) * P]
                if n == 0:
                    dve.wait_ge(s_hroot, 1)
                link(dve.reciprocal(piece, piece))

            def hyena_norm(c):
                src = u[:, c, :].rearrange("p (two m) -> p two m", two=2)
                rs = y_rs[:, c, :].rearrange("p (two m) -> p two m", two=2)
                link(dve.scalar_tensor_tensor(src, src, col("hyena_norm", c), rs, ALU.mult, ALU.mult))
                in_time = u[:, c, :].rearrange("p (two m) -> p m two", two=2)

                def pairs(ap):
                    return ap.rearrange("p (m two) -> p m two", two=2)

                link(dve.tensor_copy(pairs(yT_hi[:, c, :]), in_time))
                dve.tensor_tensor(pairs(yT_lo[:, c, :]), in_time, pairs(yT_hi[:, c, :].bitcast(F32)), ALU.subtract)\
                    .then_inc(s_yh, 1)

            def gqa_max(s):
                wait_filled(dve, ("S", s))
                c0 = 240 + s
                top = small[:, 100 + s:101 + s]
                link(dve.tensor_reduce(top, bank(("S", s))[:], AX.X, ALU.max, negate=True))
                dve.tensor_tensor(top, top, small[:, c0:c0 + 1], ALU.mult).then_inc(s_max, 1)

            def att_out(i):
                job = ("O", i)
                for h in range(NQ):
                    wait_freed(dve, ("S", i * NQ + h))
                link(dve.reciprocal(small[:, 50:58], small[:, 140 + i * NQ:148 + i * NQ]))
                dve.wait_ge(s_asq, (i + 1) * NQ)
                o3 = att[:, i, :].rearrange("p (h d) -> p h d", d=HD)
                free(dve.tensor_tensor(o3, bank(job)[:].rearrange("p (h d) -> p h d", d=HD),
                                       small[:, 50:58].unsqueeze(2).to_broadcast([P, NQ, HD]), ALU.mult), job)
                wait_freed(dve, job)
                ins = head_sums(o3, att_sq[:].rearrange("p (h d) -> p h d", d=HD), small[:, 340 + NQ * i:340 + NQ * (i + 1)])
                if i < TT - 1:
                    link(ins)
                else:
                    ins.then_inc(s_ms, 1)

            dve.wait_ge(s_qinv, 1)
            for s in range(AHEAD + 1):
                gqa_max(s)
            for s in range(NSEQ):
                if s + AHEAD + 1 < NSEQ:
                    gqa_max(s + AHEAD + 1)
                if s % NQ == 3 and s > NQ:
                    att_out(s // NQ - 1)
                n = s - HN_STEP - 3
                if 0 <= n < 4 * CT:
                    hyena_recip(n)
                    if n % 4 == 3:
                        hyena_norm(n // 4)
            att_out(TT - 1)
            dve.wait_ge(s_hrms, 4)
            link(dve.reciprocal(small[:, 340:372], small[:, 340:372]))
            for i in range(TT):
                o3 = att[:, i, :].rearrange("p (h d) -> p h d", d=HD)
                dve.tensor_tensor(o3, o3, small[:, 340 + NQ * i:340 + NQ * (i + 1)].unsqueeze(2).to_broadcast([P, NQ, HD]),
                                  ALU.mult).then_inc(s_att, 1)

            def residual(jobkey, h):
                for i in range(TT):
                    job = (jobkey, h, i)
                    wait_filled(dve, job)
                    xs = x2[:, i, h * 512:(h + 1) * 512]
                    free(dve.tensor_tensor(xs, xs, bank(job)[:], ALU.add), job)

            dve.wait_ge(ld["x2"], 16 * TT)
            for k in range(CT):
                split_lo(("yT", k), yT_lo[:, CT + k, :], yT_hi[:, CT + k, :], col("attn_norm", k))
            weight_lo(29, 3)
            residual("wout", 0)
            weight_lo(32, 4)
            residual("wout", 1)
            weight_lo(36, 1)
            for k in range(KT):
                split_lo(("hT", 1, k), hT_lo[:, k, :], hT_hi[:, k, :], col("norm_xattn", k))
            dve.wait_ge(s_rms, 2 + TT)
            dve.reciprocal(small[:, 24:28], small[:, 24:28]).then_inc(s_xn, 1)
            weight_lo(37, 3)
            for i in range(TT):
                wait_freed(dve, ("mq", i))
                ins = head_sums(mq[:, i, :].rearrange("p (h d) -> p h d", d=MHD),
                                att_sq[:].rearrange("p (h d) -> p h d", d=MHD), small[:, 40 + MH * i:44 + MH * i])
                if i < TT - 1:
                    link(ins)
            ins.then_inc(s_ms, 1)
            weight_lo(40, 1)
            dve.wait_ge(s_hrms, 5)
            link(dve.reciprocal(small[:, 40:56], small[:, 40:56]))
            link(dve.tensor_scalar(small[:, 40:56], small[:, 40:56], MHD ** -0.5, None, ALU.mult))
            dve.tensor_copy(small[0:1, 397:398], small[0:1, 40:41]).then_inc(s_mqn, 1)

            def mem_max(s):
                wait_filled(dve, ("MS", s))
                c0 = 40 + MH * (s // 2) + 2 * (s % 2)
                top = small[:, 180 + 2 * s:182 + 2 * s]
                link(dve.tensor_reduce(top, bank(("MS", s))[:].rearrange("p (h m) -> p h m", h=2), AX.X, ALU.max, negate=True))
                dve.tensor_tensor(top, top, small[:, c0:c0 + 2], ALU.mult).then_inc(s_max, 1)

            def mem_probs(s):
                wait_freed(dve, ("MS", s))
                if s:
                    dve.wait_ge(s_mnorm, s)
                link(dve.reciprocal(small[:, 224:226], small[:, 200 + 2 * s:202 + 2 * s]))
                for c in range(2):
                    ins = dve.tensor_scalar(pr[:, s % NPR, c * NM:(c + 1) * NM], pr[:, s % NPR, c * NM:(c + 1) * NM],
                                            small[:, 224 + c:225 + c], None, ALU.mult)
                ins.then_inc(s_mnorm, 1)

            for s in range(MAHEAD):
                mem_max(s)
            for s in range(MSEQ):
                mem_probs(s)
                if s + MAHEAD < MSEQ:
                    mem_max(s + MAHEAD)
            for h in range(MH):
                split_lo(("mo", h), moT_lo[:, h, :], moT_hi[:, h, :], 1.0)
            weight_lo(41, 1)
            residual("wom", 0)
            residual("wom", 1)
            for k in range(1, KT, 2):
                job = ("hT", 2, k)
                wait_filled(dve, job)
                free(dve.tensor_scalar(hT[:, k, :], bank(job)[:], col("norm_moe", k), None, ALU.mult), job)

            def R(lo, n):
                return rt[:, lo:lo + n]

            def R3(lo, w, n=TT):
                return rt[:, lo:lo + n * w].rearrange("p (t w) -> p t w", w=w)

            def bc(x, w):
                return x.unsqueeze(2).to_broadcast([P, TT, w])

            dve.wait_ge(s_rms, 2 + 2 * TT)
            dve.reciprocal(small[:, 28:32], small[:, 28:32]).then_inc(s_xn, 1)
            dve.wait_ge(s_xn, TT + 3)
            dve.wait_ge(ld["g_moe"], 16)
            for i in range(TT):
                dve.scalar_tensor_tensor(xn[:, i, :], x2[:, i, :], small[:, 28 + i:29 + i], g_moe[:], ALU.mult, ALU.mult)\
                    .then_inc(s_xn, 1)
            lg = R3(0, NG + NE)
            job = ("router",)
            wait_filled(dve, job)
            for i in range(TT):
                ins = dve.scalar_tensor_tensor(lg[:, i, :], bank(job)[:, i * 20:(i + 1) * 20], small[:, 28 + i:29 + i],
                                               row("b_router"), ALU.mult, ALU.add)
            free(ins, job)
            wait_freed(dve, job)
            gl = lg[:, :, 0:NG]
            link(dve.tensor_reduce(R(80, 4), gl, AX.X, ALU.max))
            dve.tensor_tensor(R3(84, 4), gl, bc(R(80, 4), 4), ALU.subtract).then_inc(s_r1, 1)
            first4 = row("first4").unsqueeze(1).to_broadcast([P, TT, 4])

            def first_only(dst, x, top, scratch, scratch1):
                link(dve.tensor_tensor(dst, x, bc(top, 4), ALU.is_equal))
                link(dve.tensor_tensor(scratch, dst, first4, ALU.mult))
                link(dve.tensor_reduce(scratch1, scratch, AX.X, ALU.max))
                link(dve.tensor_tensor(dst, scratch, bc(scratch1, 4), ALU.is_equal))

            ohg = R3(120, 4)
            first_only(ohg, gl, R(80, 4), R3(136, 4), R(152, 4))
            pick = rt[:, 640:640 + 64].rearrange("p (t e g) -> p t e g", t=TT, e=EPG)
            el = lg[:, :, NG:].rearrange("p t (g e) -> p t e g", g=NG)
            for t in range(TT):
                ins = dve.tensor_tensor(pick[:, t], el[:, t], ohg[:, t, :].unsqueeze(1).to_broadcast([P, EPG, NG]), ALU.mult)
            link(ins)
            sel = R3(160, 4)
            link(dve.tensor_reduce(sel, pick, AX.X, ALU.add))
            link(dve.tensor_reduce(R(176, 4), sel, AX.X, ALU.max))
            oh1, oh2 = R3(210, 4), R3(226, 4)
            first_only(oh1, sel, R(176, 4), R3(136, 4), R(152, 4))
            rest = R3(242, 4)
            link(dve.scalar_tensor_tensor(rest, oh1, -3.0e38, sel, ALU.mult, ALU.add))
            link(dve.tensor_reduce(R(180, 4), rest, AX.X, ALU.max))
            dve.tensor_tensor(R(200, 4), R(180, 4), R(176, 4), ALU.subtract).then_inc(s_r3, 1)
            first_only(oh2, rest, R(180, 4), R3(136, 4), R(152, 4))
            dve.wait_ge(s_r2, 1)
            link(dve.tensor_reduce(R(260, 4), R3(100, 4), AX.X, ALU.add))
            link(dve.reciprocal(R(260, 4), R(260, 4)))
            dve.wait_ge(s_r4, 1)
            link(dve.tensor_scalar(R(264, 4), R(204, 4), 1.0, None, ALU.add))
            link(dve.reciprocal(R(264, 4), R(264, 4)))
            link(dve.tensor_tensor(R(268, 4), R(260, 4), R(264, 4), ALU.mult))
            link(dve.tensor_tensor(R(272, 4), R(268, 4), R(204, 4), ALU.mult))
            E1 = rt[:, 300:364].rearrange("p (t g e) -> p t g e", t=TT, g=NG)
            E2 = rt[:, 364:428].rearrange("p (t g e) -> p t g e", t=TT, g=NG)
            for oh, E in ((oh1, E1), (oh2, E2)):
                for t in range(TT):
                    ins = dve.tensor_tensor(E[:, t], ohg[:, t, :].unsqueeze(2).to_broadcast([P, NG, EPG]),
                                            oh[:, t, :].unsqueeze(1).to_broadcast([P, NG, EPG]), ALU.mult)
            link(ins)
            dve.tensor_tensor(R(428, 64), R(300, 64), R(364, 64), ALU.add).then_inc(s_oh, 1)
            vals = rt[:, 1850:1874].rearrange("p (g c) -> p g c", c=3)
            tok = cols[:, COLS["token"]:COLS["token"] + TT]
            dve.memset(rec_sb[:], 0.0)
            for r in range(2):
                at_ = slice(r * TT, (r + 1) * TT)
                dve.tensor_copy(vals[:, at_, 0], tok)
                dve.tensor_scalar(vals[:, at_, 1], tok, float(r * T - SPARE), None, ALU.add)
                ins = dve.tensor_copy(vals[:, at_, 2], R(268 + 4 * r, 4))
            link(ins)
            job = ("count",)
            wait_filled(dve, job)
            free(dve.tensor_copy(rt[:, 1500:1628], bank(job)[:, 0:128]), job)
            wait_freed(dve, job)
            within, whole = rt[:, 1500:1564], rt[:, 1564:1628]
            ends = R(516, 64)
            link(dve.tensor_copy(ends[:, 0:NE], whole[:, 0:NE]))
            for i in range(1, TT):
                link(dve.tensor_tensor(ends[:, NE * i:NE * (i + 1)], ends[:, NE * (i - 1):NE * i],
                                       whole[:, NE * i:NE * (i + 1)], ALU.add))
            pos, cnt = R(1640, 64), R(564, 16)
            dve.tensor_copy(pos[:, 0:NE], within[:, 0:NE])
            link(dve.tensor_tensor(pos[:, NE:], within[:, NE:], ends[:, 0:3 * NE], ALU.add))

            def above(dst, x, bounds, op, scratch):
                link(dve.tensor_scalar(dst, x, float(bounds[0]), None, op))
                for v in bounds[1:]:
                    link(dve.scalar_tensor_tensor(dst, x, float(v), dst, op, ALU.add))

            ov, inc, nxt = R(720, 16), R(736, 16), R(752, 16)
            above(ov, cnt, (128, 256, 384), ALU.is_gt, None)
            link(dve.tensor_copy(inc, ov))
            for s in (1, 2, 4, 8):
                dve.tensor_copy(nxt[:, 0:s], inc[:, 0:s])
                link(dve.tensor_tensor(nxt[:, s:], inc[:, s:], inc[:, 0:NE - s], ALU.add))
                inc, nxt = nxt, inc
            hi = R(780, 64)
            above(hi, pos, (128, 256, 384), ALU.is_ge, None)
            far, lo, blkn = R(850, 64), R(920, 64), R(990, 64)
            link(dve.scalar_tensor_tensor(lo, hi, -128.0, pos, ALU.mult, ALU.add))
            link(dve.tensor_scalar(far, hi, 0.0, None, ALU.is_gt))
            exp4 = row("expert").unsqueeze(1).to_broadcast([P, TT, NE])
            link(dve.tensor_tensor(R(1060, 16), inc, ov, ALU.subtract))
            link(dve.tensor_tensor(R(1060, 16), R(1060, 16), row("expert"), ALU.subtract))
            b3 = R3(990, NE)
            link(dve.scalar_tensor_tensor(b3, R3(780, NE), float(NE - 1), R(1060, 16).unsqueeze(1).to_broadcast([P, TT, NE]),
                                          ALU.add, ALU.add))
            link(dve.tensor_tensor(blkn, blkn, far, ALU.mult))
            link(dve.tensor_tensor(b3, b3, exp4, ALU.add))
            both = R(300, 128).rearrange("p (r n) -> p r n", r=2)
            places, blocks = R(1240, 8), rt[:, 1840:1848]
            link(dve.tensor_tensor(R(1100, 128).rearrange("p (r n) -> p r n", r=2), both,
                                   lo.unsqueeze(1).to_broadcast([P, 2, 64]), ALU.mult))
            link(dve.tensor_tensor(rt[:, 1710:1838].rearrange("p (r n) -> p r n", r=2), both,
                                   blkn.unsqueeze(1).to_broadcast([P, 2, 64]), ALU.mult))
            link(dve.tensor_reduce(places, R(1100, 128).rearrange("p (g e) -> p g e", e=NE), AX.X, ALU.add))
            link(dve.tensor_reduce(blocks, rt[:, 1710:1838].rearrange("p (g e) -> p g e", e=NE), AX.X, ALU.add))
            link(dve.tensor_tensor(vals[:, :, 1], vals[:, :, 1], places, ALU.subtract))
            dve.wait_ge(ld["iota"], 16)
            block_oh = rt[:, 1880:2072].rearrange("p (g b) -> p g b", b=MAXB)
            dve.tensor_tensor(place_oh[:], iota[:].unsqueeze(1).to_broadcast([P, 2 * TT, P]),
                              places.unsqueeze(2).to_broadcast([P, 2 * TT, P]), ALU.is_equal)
            link(dve.tensor_tensor(block_oh, iota[:, 0:MAXB].unsqueeze(1).to_broadcast([P, 2 * TT, MAXB]),
                                   blocks.unsqueeze(2).to_broadcast([P, 2 * TT, MAXB]), ALU.is_equal))
            dve.tensor_tensor(rec_rhs[:], block_oh.unsqueeze(2).to_broadcast([P, 2 * TT, 3, MAXB]),
                              vals.unsqueeze(3).to_broadcast([P, 2 * TT, 3, MAXB]), ALU.mult).then_inc(s_slot, 1)
            tab = rt[0:1, 1300:1332]
            tot = inc[0:1, 15:16]
            cmp = rt[0:1, 1340:1468].rearrange("p (i e) -> p i e", e=NE)
            link(dve.tensor_tensor(cmp, inc[0:1, :].unsqueeze(1).to_broadcast([1, 8, NE]),
                                   rows[0:1, ROWS["extra"][0]:ROWS["extra"][1]].unsqueeze(2).to_broadcast([1, 8, NE]), ALU.is_le))
            link(dve.memset(tab, 0.0))
            dve.tensor_copy(tab[:, 0:NE], rows[0:1, ROWS["expert"][0]:ROWS["expert"][1]])
            link(dve.tensor_reduce(tab[:, NE:NE + 8], cmp, AX.X, ALU.add))
            link(dve.tensor_scalar(tab[:, NE:NE + 8], tab[:, NE:NE + 8], float(NE - 1), None, ALU.min))
            half = rt[0:1, 1480:1481]
            above(half, tot, (1, 3, 5, 7), ALU.is_ge, None)
            link(dve.tensor_scalar(tab[:, 31:32], half, 2.0, None, ALU.mult))
            dve.tensor_copy(e_tab[:], tab).then_inc(s_tab, 1)
            job = ("records",)
            wait_filled(dve, job)
            free(dve.tensor_copy(rec_sb[:, 0:MAXB, 0:3], bank(job)[:, 0:3 * MAXB].rearrange("p (c b) -> p b c", c=3)), job)
            wait_freed(dve, job)
            dve.tensor_scalar(rec_sb[:, :, 1], rec_sb[:, :, 1], col("spare"), None, ALU.add).then_inc(s_rec, 1)

            def lo_part(b, slot_, part, j):
                dve.wait_ge(s_ehi, count(b, j))
                at_ = slice(1024 * part, 1024 * (part + 1))
                dve.tensor_tensor(e_lo[slot_][:, at_], slot[slot_][:, at_], e_hi[buffer(b, j)][:].bitcast(F32), ALU.subtract)\
                    .then_inc(s_elo, 1)

            def lo_parts(b, q, lo, hi):
                for j in range(lo, hi):
                    kind = j // 4
                    lo_part(b, 3 * q + kind if kind < 2 else 3 * (1 - q) + 2, j % 4, j)

            def rows_lo(b):
                dve.wait_ge(s_rhi, b + 1)
                for half in range(2):
                    at_ = slice(512 * half, 512 * (half + 1))
                    ins = dve.tensor_tensor(hgT_lo[:, at_], banks[half][:], hgT_hi[:, at_].bitcast(F32), ALU.subtract)
                ins.then_inc(s_rlo, 1)

            def act_mul(b):
                dve.wait_ge(s_silu, b + 1)
                dve.wait_ge(s_used, count(b, 7))
                if not isinstance(b, int) or b >= 1:
                    dve.wait_ge(s_at, b)
                dve.tensor_tensor(ga[:], sg[:], banks[3][:], ALU.mult).then_inc(s_mul, 1)

            def actT_lo(b):
                dve.wait_ge(s_ahi, b + 1)
                dve.tensor_tensor(gaT_lo[:], banks[4][:], gaT_hi[:].bitcast(F32), ALU.subtract).then_inc(s_alo, 1)

            def turn(b, q):
                if not isinstance(b, int) or b == 0:
                    lo_parts(b, q, 0, 4)
                if isinstance(b, int) and b == 0:
                    rows_lo(0)
                if not isinstance(b, int) or b >= 1:
                    actT_lo(b - 1)
                if isinstance(b, int) and b == 0:
                    lo_parts(b, q, 4, 8)
                    lo_parts(1, 1, 0, 4)
                else:
                    lo_parts(b, q, 4, PIECES)
                act_mul(b)
                rows_lo(b + 1)

            dve.wait_ge(s_tab, 1)
            turn(0, 0)
            turn(1, 1)
            nb = dve.value_load(e_tab[0:1, 31:32], min_val=0, max_val=MAXB - NE) + NE
            with dve.Fori(2, nb, 2) as b:
                turn(b, 0)
                turn(b + 1, 1)
            actT_lo(nb - 1)
            for j in range(4):
                lo_part(nb, 5, j, j)
            for i in range(TT):
                dve.wait_ge(ld_back[i], 32)
                dve.tensor_tensor(x2[:, i, :], x2[:, i, :], y_back[:, 0, i, :], ALU.add).then_inc(s_fin, 1)
                dve.wait_ge(s_fin, 2 * i + 1)
                dve.tensor_tensor(x2[:, i, :], x2[:, i, :], y_back[:, 1, i, :], ALU.add).then_inc(s_fin, 1)

        @block.tensor
        def _(pe):
            def done(ins):
                ins.then_inc(filled, 1)

            def accumulate(job, dst, pairs):
                for n, (l, r) in enumerate(pairs):
                    ins = pe.matmul(dst, l, r, start=(n == 0), stop=(n == len(pairs) - 1))
                return ins

            def transposes(job, srcs, width=P):
                open_bank(pe, job)
                for n, s in enumerate(srcs):
                    ins = pe.transpose(bank(job)[:, n * width:(n + 1) * width], s, ident[:])
                done(ins)

            def mlp(j):
                job = ("mlp", j)
                open_bank(pe, job)
                if j == 0:
                    pe.wait_ge(ld["w12"], 32)
                    pe.wait_ge(ld["zemb"], 16)
                    done(pe.matmul(bank(job)[0:FF, :], w1[:], zemb[:], start=True, stop=True))
                else:
                    pe.wait_ge(s_sin, 1)
                    done(pe.matmul(bank(job)[0:FF, :], w2[:], a1[:], start=True, stop=True))

            def hT_jobs(n, src, ready):
                for k in range(KT):
                    ready(k)
                    transposes(("hT", n, k), [src[:, i, k * P:(k + 1) * P] for i in range(TT)])

            def residual_done(key):
                def ready(k):
                    if k % (KT // 2) == 0:
                        for i in range(TT):
                            wait_freed(pe, (key, 2 * k // KT, i))
                return ready

            def chunk_jobs(name, act_hi, act_lo, weights_first=False, width=512, part=slice(None), split=None):
                for n in range(first_piece[name], last_piece[name] + 1)[part]:
                    _, k0, nk, _, jobs_ = pieces[n]
                    pe.wait_ge(s_wl, n + 1)
                    wh, wl = piece_view(w_hi, n), piece_view(w_lo, n)
                    for j, job in enumerate(jobs_):
                        if k0 == 0:
                            open_bank(pe, job)
                        tile_ = slice(j * P, (j + 1) * P)
                        for kk in range(nk):
                            k = k0 + kk
                            if split and j == 0:
                                wait_freed(pe, split(k))
                            final = n == last_piece[name] and kk == nk - 1
                            for m, (act_, w_) in enumerate(((act_hi, wh), (act_hi, wl), (act_lo, wh))):
                                if weights_first:
                                    left, right = w_[:, kk, tile_], act_[:, k, :]
                                else:
                                    left, right = act_[:, k, tile_], w_[:, kk, :]
                                ins = pe.matmul(bank(job)[:, 0:width], left, right, start=(k == 0 and m == 0),
                                                stop=(final and m == 2))
                            if final:
                                done(ins)
                    if not final:
                        ins.then_inc(ring_used, 1)

            def filter_jobs(o, tiles):
                for t in tiles:
                    for way in range(2):
                        job = ("filt", o, t, way)
                        open_bank(pe, job)
                        c0 = (2 * o + way) * CH
                        done(pe.matmul(bank(job)[:], a2[:, t * P:(t + 1) * P], w3[:, c0:c0 + CH], start=True, stop=True))

            def l1_job(o):
                job = ("l1", o)
                open_bank(pe, job)
                if o == 0:
                    pe.wait_ge(ld["mats"], 48)
                pe.wait_ge(s_l1, 4 * o + 4)
                done(pe.matmul(bank(job)[:], ones[:], l1sum[:], start=True, stop=True))

            def spec_jobs(o, f):
                for c in range(4):
                    job = ("spec", o, f, c)
                    open_bank(pe, job)
                    if c == 0:
                        pe.wait_ge(s_spdm, 4 * o + 4)
                    par = c // 2
                    done(accumulate(job, bank(job)[:], [(dft[:, k, c, f * P:(f + 1) * P], sum_diff[o][:, c % 2, 2 * par + k, :])
                                                        for k in range(2)]))

            def z_jobs(o):
                for k in range(4):
                    if k == 0:
                        if o == 0:
                            for c in range(CT):
                                wait_freed(pe, ("u", c))
                        else:
                            pe.wait_ge(s_z, CT)
                    transposes(("zT", o, k), [u[:, c, k * P:(k + 1) * P] for c in range(CT)])

            mlp(0)
            pe.wait_ge(ld["ident"], 16)
            pe.wait_ge(ld["mem"], 16)
            for j in range(KT // 2):
                transposes(("memT", j), [mem_raw[:, m, k * P:(k + 1) * P] for k in (2 * j, 2 * j + 1) for m in range(MT)])
            mlp(1)
            chunk_jobs("mk", memT_hi, memT_lo, split=lambda k: ("memT", k // 2))
            hT_jobs(0, x_in, lambda k: pe.wait_ge(s_xn, TT))
            pe.wait_ge(s_sin, 2)
            pe.wait_ge(ld["w3"], 16)
            filter_jobs(0, range(4))
            chunk_jobs("mv", memT_hi, memT_lo)
            l1_job(0)
            pe.wait_ge(ld["dft"], 16)
            spec_jobs(0, 0)
            filter_jobs(1, (0, 1))
            spec_jobs(0, 1)
            filter_jobs(1, (2, 3))
            for k in range(KT):
                wait_freed(pe, ("hT", 0, k))
            chunk_jobs("v", hT_hi, hT_lo, weights_first=True)
            l1_job(1)
            spec_jobs(1, 0)
            spec_jobs(1, 1)
            z_jobs(0)
            chunk_jobs("g1", hT_hi, hT_lo, weights_first=True)

            def fwd_jobs(o):
                for f in range(2):
                    for c in range(4):
                        job = ("fwd", o, f, c)
                        open_bank(pe, job)
                        if f == 0 and c == 0:
                            for k in range(4):
                                wait_freed(pe, ("zT", o, k))
                        par = c // 2
                        done(accumulate(job, bank(job)[:], [(dft[:, k, c, f * P:(f + 1) * P], zt[:, 2 * par + k, :])
                                                            for k in range(2)]))

            def inv_jobs(o):
                pe.wait_ge(s_ab, 2 * o + 2)
                if o == 0:
                    pe.wait_ge(ld["idft"], 16)
                for c in range(CT):
                    job = ("inv", o, c)
                    open_bank(pe, job)
                    for par in range(2):
                        ins = accumulate(job, bank(job)[:, par * HALF:(par + 1) * HALF],
                                         [(sd[:, f, 2 * par + ri, c * P:(c + 1) * P], idft[:, f, 2 * par + ri, :])
                                          for f in range(2) for ri in range(2)])
                    done(ins)

            fwd_jobs(0)
            chunk_jobs("g2", hT_hi, hT_lo, weights_first=True)
            inv_jobs(0)
            z_jobs(1)
            fwd_jobs(1)
            chunk_jobs("q", hT_hi, hT_lo)
            chunk_jobs("kv", hT_hi, hT_lo, width=256)
            inv_jobs(1)
            pe.wait_ge(s_mkn, MT)
            for j in range(2):
                transposes(("mkT", j), [mk[:, m, h * MHD:(h + 1) * MHD] for h in (2 * j, 2 * j + 1) for m in range(MT)])
            pe.wait_ge(s_rope, TT + 1)
            for p in range(NQ // 2):
                transposes(("qT", p), [qkv[:, i, p * P:(p + 1) * P] for i in range(TT)])
            pe.wait_ge(s_kdup, 1)
            for g in range(NKV):
                transposes(("kT", g), [kdup[:, i, g].rearrange("p w d -> p (w d)") for i in range(TT)])
            for c in range(CT):
                job = ("hn", c)
                open_bank(pe, job)
                pe.wait_ge(s_ysq, c + 1)
                done(pe.matmul(bank(job)[:], blk[:], y_sq[:, c, :], start=True, stop=True))

            def score(s):
                i, h = s // NQ, s % NQ
                job = ("S", s)
                open_bank(pe, job)
                if s == 0:
                    for p in range(NQ // 2):
                        wait_freed(pe, ("qT", p))
                    for g in range(NKV):
                        wait_freed(pe, ("kT", g))
                lo = HD * (h % 2)
                done(pe.matmul(bank(job)[:], qT[lo:lo + HD, h // 2, i * P:(i + 1) * P], kT[lo:lo + HD, h // 4, :],
                               start=True, stop=True))

            def pt(s):
                wait_freed(pe, ("S", s))
                transposes(("PT", s), [pr[:, s % NPR, k * P:(k + 1) * P] for k in range(4)])

            def pv(s):
                i, h = s // NQ, s % NQ
                job = ("O", i)
                if h == 0:
                    open_bank(pe, job)
                wait_freed(pe, ("PT", s))
                v0 = 640 + HD * (h // 4)
                ins = accumulate(job, bank(job)[:, h * HD:(h + 1) * HD],
                                 [(pT[:, s % NPR, k * P:(k + 1) * P], qkv[:, k, v0:v0 + HD]) for k in range(4)])
                ins.then_inc(s_asq, 1)

            for s in range(AHEAD):
                score(s)
            for s in range(-1, NSEQ):
                if s + 1 + AHEAD < NSEQ:
                    score(s + 1 + AHEAD)
                if s + 1 < NSEQ:
                    pt(s + 1)
                if s >= 0:
                    pv(s)
            pe.wait_ge(s_yh, CT)
            chunk_jobs("wo0", yT_hi, yT_lo, part=slice(0, 2))
            pe.wait_ge(s_att, TT)
            for k in range(CT):
                transposes(("yT", k), [att[:, i, k * P:(k + 1) * P] for i in range(TT)])
            chunk_jobs("wo0", yT_hi, yT_lo, part=slice(2, None), split=lambda k: ("yT", k - CT))
            chunk_jobs("wo1", yT_hi, yT_lo)
            hT_jobs(1, x2, residual_done("wout"))
            chunk_jobs("wq", hT_hi, hT_lo, split=lambda k: ("hT", 1, k))
            for i in range(TT):
                wait_freed(pe, ("mq", i))
            for h in range(MH):
                transposes(("mqT", h), [mq[:, i, h * MHD:(h + 1) * MHD] for i in range(TT)])

            def mem_score(s):
                i, hp = s // 2, s % 2
                job = ("MS", s)
                open_bank(pe, job)
                if s == 0:
                    for h in range(MH):
                        wait_freed(pe, ("mqT", h))
                    for j in range(2):
                        wait_freed(pe, ("mkT", j))
                for c in range(2):
                    h = 2 * hp + c
                    ins = pe.matmul(bank(job)[:, c * NM:(c + 1) * NM], mqT[:, h, i * P:(i + 1) * P], mkT[:, h, :],
                                    start=True, stop=True)
                done(ins)

            for s in range(MAHEAD):
                mem_score(s)
            for s in range(MSEQ):
                if s + MAHEAD < MSEQ:
                    mem_score(s + MAHEAD)
                pe.wait_ge(s_mnorm, s + 1)
                transposes(("MPT", s), [pr[:, s % NPR, k * P:(k + 1) * P] for k in range(4)])
            for s in range(MSEQ):
                wait_freed(pe, ("MPT", s))
            for j in range(MT):
                wait_freed(pe, ("mv", j))
            for h in range(MH):
                job = ("mo", h)
                open_bank(pe, job)
                done(accumulate(job, bank(job)[:], [(mv[:, k, h * MHD:(h + 1) * MHD], mpT[:, h, k, :]) for k in range(MT)]))
            for h in range(2):
                chunk_jobs(f"wom{h}", moT_hi, moT_lo, split=lambda k: ("mo", k))
            hT_jobs(2, x2, residual_done("wom"))
            for k in range(KT):
                wait_freed(pe, ("hT", 2, k))
            job = ("router",)
            open_bank(pe, job)
            pe.wait_ge(ld["wr"], 16)
            for i in range(TT):
                ins = accumulate(job, bank(job)[:, i * 20:(i + 1) * 20],
                                 [(hT[:, k, i * P:(i + 1) * P], wr[:, k, :]) for k in range(KT)])
            done(ins)
            job = ("count",)
            open_bank(pe, job)
            pe.wait_ge(s_oh, 1)
            pe.matmul(bank(job)[:, 0:64], tri[:], rt[:, 428:492], start=True, stop=True)
            done(pe.matmul(bank(job)[:, 64:128], ones[:], rt[:, 428:492], start=True, stop=True))

            job = ("records",)
            open_bank(pe, job)
            pe.wait_ge(s_slot, 1)
            done(accumulate(job, bank(job)[:, 0:3 * MAXB],
                            [(place_oh[:, g, :], rec_rhs[:, g].rearrange("p c b -> p (c b)")) for g in range(2 * TT)]))

            for b in range(7):
                pe.wait_ge(freed[b], uses[b])
            pe.wait_ge(s_tab, 1)

            def rows_T(b, q):
                pe.wait_ge(s_gath[q], (b - q) * 8 + 16)
                if not isinstance(b, int) or b >= 1:
                    pe.wait_ge(s_rlo, b)
                for half in range(2):
                    for k in range(4):
                        c = 4 * half + k
                        ins = pe.transpose(banks[half][:, k * P:(k + 1) * P], hg[q][:, c * P:(c + 1) * P], ident[:])
                    ins.then_inc(s_t, 1)

            def three(dst, act_hi, act_lo, w_hi_, w_lo_, first, last):
                pe.matmul(dst, act_hi, w_hi_, start=first, stop=False)
                pe.matmul(dst, act_hi, w_lo_, start=False, stop=False)
                return pe.matmul(dst, act_lo, w_hi_, start=False, stop=last)

            def gate_up(b, q):
                pe.wait_ge(s_rlo, b + 1)
                if not isinstance(b, int) or b >= 1:
                    pe.wait_ge(s_mul, b)
                for j in range(8):
                    kind, part = j // 4, j % 4
                    pe.wait_ge(s_elo, count(b, j))
                    for kk in range(2):
                        k = 2 * part + kk
                        tile_, cols_ = slice(k * P, (k + 1) * P), slice(kk * 512, (kk + 1) * 512)
                        lo_ = slice(k * 512, (k + 1) * 512)
                        ins = three(banks[2 + kind][:], hgT_hi[:, tile_], hgT_lo[:, tile_], e_hi[buffer(b, j)][:, cols_],
                                    e_lo[3 * q + kind][:, lo_], k == 0, k == KT - 1)
                    ins.then_inc(s_used, 1)

            def acts_T(b):
                pe.wait_ge(s_mul, b + 1)
                if not isinstance(b, int) or b >= 1:
                    pe.wait_ge(s_alo, b)
                for k in range(4):
                    ins = pe.transpose(banks[4][:, k * P:(k + 1) * P], ga[:, k * P:(k + 1) * P], ident[:])
                ins.then_inc(s_at, 1)

            def down(b, q, turn_, j0):
                pe.wait_ge(s_alo, b + 1)
                if not isinstance(b, int) or b >= 1:
                    pe.wait_ge(s_oa, b)
                for k in range(4):
                    pe.wait_ge(s_elo, count(turn_, j0 + k))
                    tile_ = slice(k * P, (k + 1) * P)
                    for half in range(2):
                        cols_ = slice(half * 512, (half + 1) * 512)
                        lo_ = slice(k * D + half * 512, k * D + (half + 1) * 512)
                        ins = three(banks[5 + half][:], gaT_hi[:, tile_], gaT_lo[:, tile_], e_hi[buffer(turn_, j0 + k)][:, cols_],
                                    e_lo[3 * q + 2][:, lo_], k == 0, k == 3)
                    ins.then_inc(s_used, 1)

            def turn(b, q):
                gate_up(b, q)
                rows_T(b + 1, 1 - q)
                if not isinstance(b, int) or b >= 1:
                    down(b - 1, 1 - q, b, 8)
                acts_T(b)

            rows_T(0, 0)
            turn(0, 0)
            turn(1, 1)
            nb = pe.value_load(e_tab[0:1, 31:32], min_val=0, max_val=MAXB - NE) + NE
            with pe.Fori(2, nb, 2) as b:
                turn(b, 0)
                turn(b + 1, 1)
            down(nb - 1, 1, nb, 0)


def _constants():
    t = np.arange(T)
    half = np.arange(HALF)
    freq = (half + 0.5) * 2.0 * np.pi / (2 * T)
    parity = np.concatenate([t[0::2], t[1::2]])
    ang = parity[:, None] * freq[None, :]
    cs, sn = np.cos(ang), -np.sin(ang)
    dft = np.zeros((P, 2, 4, HALF))
    for par in range(2):
        for k in range(2):
            r = par * HALF + k * P
            dft[:, k, 2 * par] = cs[r:r + P]
            dft[:, k, 2 * par + 1] = sn[r:r + P]
    idft = np.zeros((P, 2, 4, HALF))
    for f in range(2):
        for par in range(2):
            r = slice(par * HALF, (par + 1) * HALF)
            idft[:, f, 2 * par] = cs[r, f * P:(f + 1) * P].T / T
            idft[:, f, 2 * par + 1] = sn[r, f * P:(f + 1) * P].T / T
    f32 = np.float32
    tl = np.linspace(0.0, 1.0, T, dtype=f32)
    bands = np.linspace(1e-4, 15, 16, dtype=f32)
    w = (f32(2.0 * np.pi / T) * t.astype(f32))[:, None] * bands[None, :]
    w = w.astype(f32)
    zemb = np.concatenate([tl[:, None], np.cos(w.astype(np.float64)), np.sin(w.astype(np.float64))], 1)[parity].T
    deltas = np.abs(np.linspace(np.log(1e-2) / 1.5, np.log(1e-2) / 0.3, CH, dtype=f32))
    decay = np.exp((-tl[:, None] * deltas[None, :]).astype(f32).astype(np.float64))[parity].reshape(4, P, CH).transpose(1, 0, 2)
    inv = 10000.0 ** (-np.arange(16) / 16.0)
    rope = np.zeros((P, 2, TT, HD))
    for i in range(TT):
        tok = i * P + np.arange(P)
        for s, pos in enumerate((tok // 64, tok % 64)):
            a = pos[:, None] * inv[None, :]
            for wv in range(2):
                c0 = 32 * s + 16 * wv
                rope[:, 0, i, c0:c0 + 16] = np.cos(a)
                rope[:, 1, i, c0:c0 + 16] = np.sin(a) * (1 if wv else -1)
    mats = np.zeros((P, 4, P))
    mats[:, 0] = np.eye(P)
    mats[:, 1] = 1.0
    mats[:, 2] = np.kron(np.eye(2), np.ones((HD, HD)))
    mats[:, 3] = np.triu(np.ones((P, P)), 1)
    return {k: np.ascontiguousarray(v, dtype=f32) for k, v in
            dict(dft=dft, idft=idft, zemb=zemb, decay=decay, rope=rope, mats=mats,
                 iota=np.broadcast_to(np.arange(P), (P, P))).items()}


_DIRECT = ["x", "mem", "w_in", "filt_w1", "filt_w2", "filt_w3", "w_out", "w_q_mem", "w_k_mem", "w_v_mem", "w_o_mem",
           "w_gate", "w_up", "w_down"]


def kernel(**inputs):
    import concourse.bacc as _bacc
    from concourse.bass_utils import run_bass_kernel_spmd as _run

    v = {k: np.ascontiguousarray(x) for k, x in inputs.items()}
    arrays = {k: v[k] for k in _DIRECT}
    arrays.update(_constants())

    def column(x):
        x = np.asarray(x).reshape(-1)
        if x.size < P:
            x = np.concatenate([x, np.zeros(P - x.size, x.dtype)])
        return x.reshape(-1, P).T

    not_first = np.ones((P, 1), np.float32)
    not_first[0] = 0.0
    token = (np.arange(P)[:, None] + P * np.arange(TT)[None, :]).astype(np.float32)
    arrays["cols"] = np.ascontiguousarray(np.concatenate(
        [column(v[k]) for k in ("norm_mix", "norm_xattn", "norm_mem", "norm_moe", "hyena_short_w", "hyena_short_b",
                                "hyena_skip", "out_norm_hyena", "out_norm_attn", "filt_b1", "filt_b2")]
        + [column(v["filt_sin_freq"][0, j]) for j in range(2)]
        + [column(v["mem_q_norm"]), not_first, SPARE + token[:, 0:1], token], axis=1))
    one_row = np.concatenate([v["attn_q_norm"][0], v["attn_k_norm"][0], v["mem_q_norm"][0], v["mem_k_norm"][0],
                              v["b_router_grp"][0], v["b_router_exp"][0],
                              np.array([4, 3, 2, 1], np.float32), np.arange(NE, dtype=np.float32),
                              np.arange(8, dtype=np.float32)])
    arrays["g_moe"] = np.ascontiguousarray(np.broadcast_to(v["norm_moe"][0], (P, D)))
    arrays["rows"] = np.ascontiguousarray(np.broadcast_to(one_row, (P, one_row.size)))
    arrays["w_router"] = np.ascontiguousarray(
        np.concatenate([v["w_router_grp"][0], v["w_router_exp"][0]], axis=1).reshape(KT, P, NG + NE).transpose(1, 0, 2))

    nc = _bacc.Bacc("TRN2", target_bir_lowering=False, num_devices=1)
    aps = {k: nc.dram_tensor(f"in_{k}", x.shape, mybir.dt.from_np(x.dtype), kind="ExternalInput").ap()
           for k, x in arrays.items()}
    out = nc.dram_tensor("out_0_dram", (1, T, D), F32, kind="ExternalOutput").ap()
    xn_dram = nc.dram_tensor("xn_dram", (T, D), F32, kind="Internal").ap()
    y_dram = nc.dram_tensor("y_dram", (2 * T + P, D), F32, kind="Internal").ap()
    build(nc, aps, out, xn_dram, y_dram)
    r = _run(nc, [{f"in_{k}": x for k, x in arrays.items()}], core_ids=[0])
    return r.results[0]["out_0_dram"]
```
